# Optimizing a Trainium2 kernel written in Bass

```python
import jax, jax.numpy as jnp
from jax import lax
import numpy as np

D_MODEL = 1024
BATCH = 1
SEQ = 1024
DEPTH = 1
DEC_BATCH = 1
DEC_SEQ = 32
PAST_LEN = 256

CHUNK = 64
N_META = 16
HEAD_DIM = 64
A_HEADS = 8
A_KV_HEADS = 2
A_GROUP = A_HEADS // A_KV_HEADS
A_WINDOW = 128
A_WIN_CHUNKS = A_WINDOW // CHUNK
B_HEADS = 8
SB_BLOCK = 128
ROPE_THETA = 10000.0
N_GROUPS = 4
EXPERTS_PER_GROUP = 8
N_EXPERTS = N_GROUPS * EXPERTS_PER_GROUP
TOP_K = 2
D_EXPERT = 512
MOE_BLOCK = 128
LN_EPS = 1e-5
NEG_INF = -1e30
ALPHA = (2 * DEPTH) ** 0.25
BETA_INIT = (8 * DEPTH) ** -0.25

A_Q = A_HEADS * HEAD_DIM
A_KV = A_KV_HEADS * HEAD_DIM
B_W = B_HEADS * HEAD_DIM
OFF_QA = 0
OFF_KA = OFF_QA + A_Q
OFF_VA = OFF_KA + A_KV
OFF_QB = OFF_VA + A_KV
OFF_KB = OFF_QB + B_W
OFF_VB = OFF_KB + B_W
OFF_GA = OFF_VB + B_W
OFF_GB = OFF_GA + D_MODEL
IN_W = OFF_GB + D_MODEL

kernel_name = 'hybrid_swa_sink_stickbreak_hmoe_stream'

def layer_norm(x, g, b):
    xf = x.astype(jnp.float32)
    mu = jnp.mean(xf, axis=-1, keepdims=True)
    var = jnp.mean(jnp.square(xf - mu), axis=-1, keepdims=True)
    return ((xf - mu) * lax.rsqrt(var + LN_EPS) * g.astype(jnp.float32) + b.astype(jnp.float32)).astype(x.dtype)

def rope(x, pos):
    half = HEAD_DIM // 2
    inv = ROPE_THETA ** (-jnp.arange(half, dtype=jnp.float32) * 2.0 / HEAD_DIM)
    ang = pos.astype(jnp.float32)[:, None] * inv[None, :]
    cos = jnp.cos(ang)[:, None, :]
    sin = jnp.sin(ang)[:, None, :]
    x1 = x[..., :half].astype(jnp.float32)
    x2 = x[..., half:].astype(jnp.float32)
    return jnp.concatenate([x1 * cos - x2 * sin, x2 * cos + x1 * sin], axis=-1).astype(x.dtype)

def in_projection(x, w_in, pos):
    b, l = x.shape[:2]
    u = x @ w_in
    qa = rope(u[..., OFF_QA:OFF_KA].reshape(b, l, A_HEADS, HEAD_DIM), pos)
    ka = rope(u[..., OFF_KA:OFF_VA].reshape(b, l, A_KV_HEADS, HEAD_DIM), pos)
    va = u[..., OFF_VA:OFF_QB].reshape(b, l, A_KV_HEADS, HEAD_DIM)
    qb = u[..., OFF_QB:OFF_KB].reshape(b, l, B_HEADS, HEAD_DIM)
    kb = u[..., OFF_KB:OFF_VB].reshape(b, l, B_HEADS, HEAD_DIM)
    vb = u[..., OFF_VB:OFF_GA].reshape(b, l, B_HEADS, HEAD_DIM)
    return qa, ka, va, qb, kb, vb, u[..., OFF_GA:OFF_GB], u[..., OFF_GB:]

def meta_kv(meta, w_in):
    pos = jnp.arange(N_META)
    ua = meta @ w_in[:, OFF_KA:OFF_QB]
    ub = meta @ w_in[:, OFF_KB:OFF_GA]
    ka = rope(ua[:, :A_KV].reshape(N_META, A_KV_HEADS, HEAD_DIM), pos)
    va = ua[:, A_KV:].reshape(N_META, A_KV_HEADS, HEAD_DIM)
    kb = ub[:, :B_W].reshape(N_META, B_HEADS, HEAD_DIM)
    vb = ub[:, B_W:].reshape(N_META, B_HEADS, HEAD_DIM)
    return ka, va, kb, vb

def sink_attention(q, k, v, valid, sinks):
    s = jnp.einsum('...qhgd,...shd->...hgqs', q, k).astype(jnp.float32) * HEAD_DIM ** -0.5
    if valid is not None:
        s = jnp.where(valid, s, NEG_INF)
    sink = jnp.broadcast_to(sinks.astype(jnp.float32).reshape(A_KV_HEADS, A_GROUP, 1, 1), s.shape[:-1] + (1,))
    p = jax.nn.softmax(jnp.concatenate([s, sink], axis=-1), axis=-1)[..., :-1]
    return jnp.einsum('...hgqs,...shd->...qhgd', p.astype(v.dtype), v)

def window_attention_prompt(qa, ka, va, sinks):
    b, l = qa.shape[:2]
    n_real = l - N_META
    qg = qa.reshape(b, l, A_KV_HEADS, A_GROUP, HEAD_DIM)
    km, vm = ka[:, :N_META], va[:, :N_META]
    outs = [sink_attention(qg[:, :N_META], km, vm, None, sinks).reshape(b, N_META, A_Q)]
    if n_real > 0:
        nc = n_real // CHUNK
        qc = qg[:, N_META:].reshape(b, nc, CHUNK, A_KV_HEADS, A_GROUP, HEAD_DIM)
        kc = ka[:, N_META:].reshape(b, nc, CHUNK, A_KV_HEADS, HEAD_DIM)
        vc = va[:, N_META:].reshape(b, nc, CHUNK, A_KV_HEADS, HEAD_DIM)
        offs = list(range(A_WIN_CHUNKS, -1, -1))
        shift = lambda t, o: jnp.pad(t, ((0, 0), (o, 0), (0, 0), (0, 0), (0, 0)))[:, :nc]
        bmeta = lambda t: jnp.broadcast_to(t[:, None], (b, nc) + t.shape[1:])
        kband = jnp.concatenate([bmeta(km)] + [shift(kc, o) for o in offs], axis=2)
        vband = jnp.concatenate([bmeta(vm)] + [shift(vc, o) for o in offs], axis=2)
        cid = jnp.arange(nc)
        valid = jnp.concatenate([jnp.ones((nc, N_META), bool)]
                                + [jnp.broadcast_to((cid >= o)[:, None], (nc, CHUNK)) for o in offs], axis=1)
        out = sink_attention(qc, kband, vband, valid[None, :, None, None, None, :], sinks)
        outs.append(out.reshape(b, n_real, A_Q))
    return jnp.concatenate(outs, axis=1)

def stick_breaking_block(q, t_idx, k, v):
    z = jnp.einsum('bqhd,bshd->bhqs', q, k).astype(jnp.float32) * HEAD_DIM ** -0.5
    before = jnp.arange(k.shape[1])[None, :] < t_idx[:, None]
    log_keep = jnp.where(before, jax.nn.log_sigmoid(-z), 0.0)
    log_later = lax.cumsum(log_keep, axis=3, reverse=True) - log_keep
    w = jnp.where(before, jnp.exp(jax.nn.log_sigmoid(z) + log_later), 0.0)
    return jnp.einsum('bhqs,bshd->bqhd', w.astype(v.dtype), v)

def stick_breaking_prompt(q, k, v):
    b, l = q.shape[:2]
    nb = -(-l // SB_BLOCK)
    qp = jnp.pad(q, ((0, 0), (0, nb * SB_BLOCK - l), (0, 0), (0, 0)))
    qp = qp.reshape(b, nb, SB_BLOCK, B_HEADS, HEAD_DIM).swapaxes(0, 1)
    t_idx = jnp.arange(nb * SB_BLOCK).reshape(nb, SB_BLOCK)
    out = lax.map(lambda a: stick_breaking_block(a[0], a[1], k, v), (qp, t_idx))
    return out.swapaxes(0, 1).reshape(b, nb * SB_BLOCK, B_W)[:, :l]

def hier_moe(h, lp):
    n_tok = h.shape[0]
    rows_t = jnp.arange(n_tok)
    g_logits = (h @ lp['w_rg']).astype(jnp.float32) + lp['b_rg'].astype(jnp.float32)
    g_sel = jnp.argmax(g_logits, axis=-1)
    g_prob = jax.nn.softmax(g_logits, axis=-1)[rows_t, g_sel][:, None]
    e_logits = ((h @ lp['w_re']).astype(jnp.float32) + lp['b_re'].astype(jnp.float32)).reshape(n_tok, N_GROUPS, EXPERTS_PER_GROUP)
    top_v, top_i = lax.top_k(e_logits[rows_t, g_sel], TOP_K)
    gate = (jax.nn.softmax(top_v, axis=-1) * g_prob).reshape(-1)
    expert = (g_sel[:, None] * EXPERTS_PER_GROUP + top_i).reshape(-1)
    tok = jnp.repeat(rows_t, TOP_K)
    n_assign = n_tok * TOP_K
    n_blocks = (n_assign + N_EXPERTS * (MOE_BLOCK - 1) + MOE_BLOCK - 1) // MOE_BLOCK
    order = jnp.argsort(expert)
    e_s, tok_s, w_s = expert[order], tok[order], gate[order]
    counts = jnp.zeros((N_EXPERTS,), jnp.int32).at[expert].add(1)
    padded = (counts + MOE_BLOCK - 1) // MOE_BLOCK * MOE_BLOCK
    pad_end = jnp.cumsum(padded)
    pad_start = pad_end - padded
    cnt_start = jnp.cumsum(counts) - counts
    dest = pad_start[e_s] + jnp.arange(n_assign) - cnt_start[e_s]
    xb = jnp.zeros((n_blocks * MOE_BLOCK, h.shape[1]), h.dtype).at[dest].set(h[tok_s])
    block_e = jnp.minimum(jnp.searchsorted(pad_end, jnp.arange(n_blocks) * MOE_BLOCK, side='right'), N_EXPERTS - 1)

    def expert_block(a):
        xblk, e = a
        return (jax.nn.silu(xblk @ lp['w_gate'][e]) * (xblk @ lp['w_up'][e])) @ lp['w_down'][e]

    yb = lax.map(expert_block, (xb.reshape(n_blocks, MOE_BLOCK, -1), block_e)).reshape(n_blocks * MOE_BLOCK, -1)
    return jax.ops.segment_sum(yb[dest] * w_s[:, None].astype(yb.dtype), tok_s, num_segments=n_tok)

def finish_layer(x, oa, ob, ga, gb, lp):
    mix = (jax.nn.sigmoid(ga) * (oa @ lp['w_oa']) + jax.nn.sigmoid(gb) * (ob @ lp['w_ob'])) @ lp['w_out']
    h = layer_norm(ALPHA * x + mix, lp['ln1_g'], lp['ln1_b'])
    f = hier_moe(h.reshape(-1, h.shape[-1]), lp).reshape(h.shape)
    return layer_norm(ALPHA * h + f, lp['ln2_g'], lp['ln2_b'])

def prompt_layer(x, lp):
    qa, ka, va, qb, kb, vb, ga, gb = in_projection(x, lp['w_in'], jnp.arange(x.shape[1]))
    oa = window_attention_prompt(qa, ka, va, lp['sinks'])
    ob = stick_breaking_prompt(qb, kb, vb)
    return finish_layer(x, oa, ob, ga, gb, lp), ka, va, kb, vb

def sample_layer(x, meta, ck_a, cv_a, ck_b, cv_b, lp):
    db, t = x.shape[:2]
    past = ck_b.shape[1]
    qa, ka, va, qb, kb, vb, ga, gb = in_projection(x, lp['w_in'], N_META + past + jnp.arange(t))
    mka, mva, mkb, mvb = meta_kv(meta, lp['w_in'])
    bc = lambda m: jnp.broadcast_to(m[None].astype(x.dtype), (db,) + m.shape)
    k_a = jnp.concatenate([bc(mka), ck_a, ka], axis=1)
    v_a = jnp.concatenate([bc(mva), cv_a, va], axis=1)
    oa = sink_attention(qa.reshape(db, t, A_KV_HEADS, A_GROUP, HEAD_DIM), k_a, v_a, None, lp['sinks']).reshape(db, t, A_Q)
    k_b = jnp.concatenate([bc(mkb), ck_b, kb], axis=1)
    v_b = jnp.concatenate([bc(mvb), cv_b, vb], axis=1)
    ob = stick_breaking_block(qb, N_META + past + jnp.arange(t), k_b, v_b).reshape(db, t, B_W)
    return finish_layer(x, oa, ob, ga, gb, lp), ka, va, kb, vb

def setup_inputs(seed: int = 0) -> dict:
    key = jax.random.key(seed)
    ks = jax.random.split(key, 24)
    f32 = jnp.float32
    nrm = lambda k, shape, scale: jax.random.normal(k, shape, f32) * scale
    a_cache = min(A_WINDOW, PAST_LEN)
    col_scale = jnp.concatenate([jnp.ones((OFF_VA,), f32), jnp.full((A_KV,), BETA_INIT, f32),
                                 jnp.ones((OFF_VB - OFF_QB,), f32), jnp.full((B_W,), BETA_INIT, f32),
                                 jnp.ones((IN_W - OFF_GA,), f32)])
    return {
        'x_prompt': nrm(ks[0], (BATCH, SEQ, D_MODEL), 1.0),
        'x_sample': nrm(ks[1], (DEC_BATCH, DEC_SEQ, D_MODEL), 1.0),
        'cache_a_k': nrm(ks[2], (DEPTH, DEC_BATCH, a_cache, A_KV_HEADS, HEAD_DIM), 1.0),
        'cache_a_v': nrm(ks[3], (DEPTH, DEC_BATCH, a_cache, A_KV_HEADS, HEAD_DIM), BETA_INIT),
        'cache_b_k': nrm(ks[4], (DEPTH, DEC_BATCH, PAST_LEN, B_HEADS, HEAD_DIM), 1.0),
        'cache_b_v': nrm(ks[5], (DEPTH, DEC_BATCH, PAST_LEN, B_HEADS, HEAD_DIM), BETA_INIT),
        'meta_tokens': nrm(ks[6], (N_META, D_MODEL), 1.0),
        'w_in': nrm(ks[7], (DEPTH, D_MODEL, IN_W), D_MODEL ** -0.5) * col_scale,
        'attn_sinks': nrm(ks[8], (DEPTH, A_HEADS), 0.5),
        'w_oa': nrm(ks[9], (DEPTH, A_Q, D_MODEL), A_Q ** -0.5 * BETA_INIT),
        'w_ob': nrm(ks[10], (DEPTH, B_W, D_MODEL), B_W ** -0.5 * BETA_INIT),
        'w_out': nrm(ks[11], (DEPTH, D_MODEL, D_MODEL), D_MODEL ** -0.5 * BETA_INIT),
        'ln1_g': 1.0 + nrm(ks[12], (DEPTH, D_MODEL), 0.02),
        'ln1_b': nrm(ks[13], (DEPTH, D_MODEL), 0.02),
        'w_router_group': nrm(ks[14], (DEPTH, D_MODEL, N_GROUPS), D_MODEL ** -0.5),
        'b_router_group': nrm(ks[15], (DEPTH, N_GROUPS), 0.01),
        'w_router_expert': nrm(ks[16], (DEPTH, D_MODEL, N_EXPERTS), D_MODEL ** -0.5),
        'b_router_expert': nrm(ks[17], (DEPTH, N_EXPERTS), 0.01),
        'w_gate': nrm(ks[18], (DEPTH, N_EXPERTS, D_MODEL, D_EXPERT), D_MODEL ** -0.5),
        'w_up': nrm(ks[19], (DEPTH, N_EXPERTS, D_MODEL, D_EXPERT), D_MODEL ** -0.5 * BETA_INIT),
        'w_down': nrm(ks[20], (DEPTH, N_EXPERTS, D_EXPERT, D_MODEL), D_EXPERT ** -0.5 * BETA_INIT),
        'ln2_g': 1.0 + nrm(ks[21], (DEPTH, D_MODEL), 0.02),
        'ln2_b': nrm(ks[22], (DEPTH, D_MODEL), 0.02),
    }

def reference(x_prompt, x_sample, cache_a_k, cache_a_v, cache_b_k, cache_b_v, meta_tokens, w_in, attn_sinks,
              w_oa, w_ob, w_out, ln1_g, ln1_b, w_router_group, b_router_group, w_router_expert, b_router_expert,
              w_gate, w_up, w_down, ln2_g, ln2_b):
    bp, seq = x_prompt.shape[:2]
    a_keep = min(A_WINDOW, seq)
    xp = jnp.concatenate([jnp.broadcast_to(meta_tokens[None].astype(x_prompt.dtype), (bp, N_META, D_MODEL)), x_prompt], axis=1)
    xs = x_sample
    meta = meta_tokens
    akp, avp, bkp, bvp, aks, avs, bks, bvs = [], [], [], [], [], [], [], []
    for l in range(DEPTH):
        lp = {'w_in': w_in[l], 'sinks': attn_sinks[l], 'w_oa': w_oa[l], 'w_ob': w_ob[l], 'w_out': w_out[l],
              'ln1_g': ln1_g[l], 'ln1_b': ln1_b[l], 'w_rg': w_router_group[l], 'b_rg': b_router_group[l],
              'w_re': w_router_expert[l], 'b_re': b_router_expert[l], 'w_gate': w_gate[l], 'w_up': w_up[l],
              'w_down': w_down[l], 'ln2_g': ln2_g[l], 'ln2_b': ln2_b[l]}
        xp, ka, va, kb, vb = prompt_layer(xp, lp)
        akp.append(ka[:, N_META:][:, seq - a_keep:])
        avp.append(va[:, N_META:][:, seq - a_keep:])
        bkp.append(kb[:, N_META:])
        bvp.append(vb[:, N_META:])
        xs, ka_s, va_s, kb_s, vb_s = sample_layer(xs, meta, cache_a_k[l], cache_a_v[l], cache_b_k[l], cache_b_v[l], lp)
        aks.append(ka_s)
        avs.append(va_s)
        bks.append(kb_s)
        bvs.append(vb_s)
        if l + 1 < DEPTH:
            meta = prompt_layer(meta[None], lp)[0][0]
    y_prompt = xp[:, N_META:]
    return (y_prompt, xs, jnp.stack(akp), jnp.stack(avp), jnp.stack(bkp), jnp.stack(bvp),
            jnp.stack(aks), jnp.stack(avs), jnp.stack(bks), jnp.stack(bvs))


_drawn_inputs = setup_inputs


def setup_inputs(seed=0):
    import zlib

    import numpy as np

    out = dict(_drawn_inputs(seed))
    spreads = {}
    factors = {'cache_a_k': 5.169,
     'cache_a_v': 4.134,
     'cache_b_k': 8.0,
     'cache_b_v': 4.922,
     'meta_tokens': 8.0,
     'attn_sinks': 64.0,
     'w_oa': 4.17,
     'b_router_group': 200.0,
     'b_router_expert': 31.527,
     'ln2_g': 20.574,
     'ln2_b': 21.275}
    for name, (base, spread) in spreads.items():
        noise = np.random.default_rng([zlib.crc32(name.encode()), seed]).standard_normal(out[name].shape)
        drawn = base * np.exp(spread * noise) if base else spread * noise
        out[name] = __import__('jax').numpy.asarray(drawn.astype(out[name].dtype))
    for name, factor in factors.items():
        out[name] = (out[name] * factor).astype(out[name].dtype)
    return out
```

```python
from contextlib import ExitStack

import concourse.bass as bass
from concourse import mybir

ALU = mybir.AluOpType
ACT = mybir.ActivationFunctionType
AX = mybir.AxisListType
F32 = mybir.dt.float32
F32R = mybir.dt.float32r
I32 = mybir.dt.int32
U32 = mybir.dt.uint32

P = 128
D = 1024
SEQ, DEC, META, PAST = 1024, 32, 16, 256
TOK = SEQ + DEC + META
LIVE = SEQ + DEC
SAM, MET = SEQ, SEQ + DEC
KD = D // P
HD = 64
NH = 8
PAIRS = NH // 2
NT = SEQ // P
AWIN = 128
NE, NG, EPG = 32, 4, 8
DE = 512
MAXBLK = NE + 2 * LIVE // P
ALPHA = 2.0 ** 0.25
EPS = 1e-5
NEG = -1e30
SCALE = HD ** -0.5
ZCAP = 40.0

C_QA, C_KA, C_VA, C_QB, C_KB, C_VB = 0, 4, 5, 6, 10, 14
NCH = 18
NROPE = C_VA
TCUT = (0, 358, 716, 1072)
TW = LIVE // 3
BAND = META + 2 * P
AKEYS = DEC + AWIN + META
QCH = 512

STEPS = [(a, c, t) for a in range(2) for c in range(2) for t in [*range(4 * c + 3, -1, -1), -1]]
NSTEP = len(STEPS)
LATER_BEFORE = [sum(x[2] >= 0 for x in STEPS[:n]) for n in range(NSTEP + 1)]
NLATER = LATER_BEFORE[NSTEP]


def step_shape(c, t):
    return (META if t < 0 else P), max(P * t - QCH * c, 0), t == 4 * c + 3


def s_bank(n):
    return 2 * (n % 2)


SAMPLE_TILES = [(DEC, slice(SAM, MET), None), (P, slice(P, PAST), 1), (P, slice(0, P), 0),
                (META, slice(MET, TOK), None)]

NTL = NT + 1
NR = NG + NE
VROWS = NTL * P
GC = KD * DE
SILU_SET = "silu_and_others"
TABR = NE * NTL // 3
PIECE = GC // 4
HH = DE // 2

K_IDENT, K_NTRI, K_NONES, K_SUP, K_ONES, K_MASK, K_ROT = (P * n for n in range(7))
K_BAND = 7 * P
K_SMASK = K_BAND + BAND
K_IOTA = K_SMASK + NH * DEC
K_TOK = K_IOTA + MAXBLK + 1
K_HALF = K_TOK + NTL
K_N = K_HALF + 1


def rows_of(t):
    return P if t < NT else DEC


def build(nc, io):
    with ExitStack() as ctx:
        def sem(name):
            return ctx.enter_context(nc.semaphore(name))

        limit = nc.sbuf_usable_end
        tok_table = nc.dram_tensor("tok_table", [NE * VROWS, 1], I32, kind="Internal").ap()
        h_rows = nc.dram_tensor("h_rows", [LIVE, D], F32, kind="Internal").ap()
        y_rows = nc.dram_tensor("y_rows", [MAXBLK * P, D], F32, kind="Internal").ap()

        class Region:
            def __init__(self, base):
                self.at = base

            def take(self, name, shape, dt=F32):
                n = 4
                for k in shape[1:]:
                    n *= k
                t = nc.alloc_sbuf_tensor_at(name, shape, dt, offset=self.at)
                self.at += (n + 31) // 32 * 32
                assert self.at <= limit, (name, self.at, limit)
                return t

            def split(self, name, shape):
                hi = self.take(name + "_hi", shape, F32R)
                raw = nc.alloc_sbuf_tensor_at(name + "_raw", shape, F32, offset=self.at)
                return raw, hi, self.take(name + "_lo", shape, F32R)

        ps = ctx.enter_context(nc.psum_tensor("ps", [P, 8, 512], F32))

        keep = Region((nc.sbuf_base + 31) // 32 * 32)
        const = keep.take("const", [P, K_N])
        ident, ntri, nones, sup, ones, blkmask, rot = (const[:, k:k + P] for k in range(0, 7 * P, P))
        amask = const[:, K_BAND:K_BAND + BAND]
        zero = const[:, K_BAND:K_BAND + 1]
        smask = const[0:DEC, K_SMASK:K_SMASK + NH * DEC]
        iota = const[:, K_IOTA:K_IOTA + MAXBLK + 1]
        sinks = keep.take("sinks", [P, NH])
        sinks_s = keep.take("sinks_s", [P, 2])
        base = keep.at

        r = Region(base)
        xraw, xh, xl = r.split("xT", [P, KD, TOK])
        U = r.take("U", [P, NCH, TOK])
        work = r.at
        r = Region(work)
        wraw, whi, wlo = zip(*[r.split(f"win{n}", [P, KD, P]) for n in range(2)])
        cos = r.take("cos", [P, TOK])
        sin = r.take("sin", [P, TOK])
        ropet = [r.take(f"ropet{n}", [P, 512]) for n in range(2)]
        r = Region(work)
        van = r.take("van", [P, NT, P])
        van_m = r.take("van_m", [META, P])
        van_s = r.take("van_s", [DEC, P])
        qas = r.take("qas", [P, 4, P])
        kas = r.take("kas", [P, 2 * P])
        qas_s = r.take("qas_s", [P, 4, DEC])
        vas = r.take("vas", [P, 2, P])
        msk = [r.take(f"msk{n}", [P, 2, BAND]) for n in range(2)]
        prob = [r.take(f"prob{n}", [P, 2, BAND]) for n in range(2)]
        pts = r.take("pts", [P, 512])
        ptms = r.take("ptms", [META, 2 * P])
        stat = [r.take(f"stat{n}", [P, 8, 2]) for n in range(2)]
        ck_a = r.take("ck_a", [P, AWIN])
        cv_a = r.take("cv_a", [P, P])
        r = Region(work)
        kh = r.take("kh", [P, TOK], F32R)
        kl = r.take("kl", [P, TOK], F32R)
        qh = r.take("qh", [P, SEQ], F32R)
        ql = r.take("ql", [P, SEQ], F32R)
        vts = r.take("vts", [P, TOK])
        vn = r.take("vn", [P, NT, P])
        vn_m = r.take("vn_m", [META, P])
        capped = [r.take(f"capped{n}", [P, QCH]) for n in range(2)]
        soft = [r.take(f"soft{n}", [P, QCH]) for n in range(2)]
        wgt = [r.take(f"wgt{n}", [P, QCH]) for n in range(2)]
        later = r.take("later", [P, QCH])
        vall_m = r.take("vall_m", [META, PAIRS, P])
        vall_s = r.take("vall_s", [DEC, PAIRS, P])
        SQ = NH * DEC
        ck_b = r.take("ck_b", [P, PAIRS, PAST])
        cv_b = r.take("cv_b", [P, 2, PAIRS * P])
        qs = r.take("qs", [P, PAIRS, DEC])
        capped_s = r.take("capped_s", [P, SQ])
        soft_s = r.take("soft_s", [P, SQ])
        wgt_s = r.take("wgt_s", [P, SQ])
        later_s = r.take("later_s", [P, SQ])

        def u_at(c):
            return nc_u + c * TOK * 4
        nc_u = work - NCH * TOK * 4
        oa_lo = nc.alloc_sbuf_tensor_at("oa_lo", [P, 4, TOK], F32R, offset=u_at(C_QA))
        ob_lo = nc.alloc_sbuf_tensor_at("ob_lo", [P, 4, TOK], F32R, offset=u_at(C_QB))
        oa_hi = nc.alloc_sbuf_tensor_at("oa_hi", [P, 4, TOK], F32R, offset=u_at(C_KB))
        ob_hi = nc.alloc_sbuf_tensor_at("ob_hi", [P, 4, TOK], F32R, offset=u_at(C_VB))
        r = Region(u_at(C_KA))
        sig = [[r.take(f"sig{n}{w}", [P, TW]) for w in "ab"] for n in range(2)]
        mixa = r.take("mixa", [P, TW])
        mixb = r.take("mixb", [P, TW])
        assert r.at <= u_at(C_QB)
        r = Region(work)
        mT = r.take("mT", [P, KD, LIVE])
        after_m = r.at
        graw, ghi, glo = zip(*[r.split(f"wmix{n}", [P, KD, P]) for n in range(3)])
        r = Region(base)
        oraw, ohi, olo = r.split("wout", [P, KD, D])
        assert r.at <= nc_u
        r = Region(nc_u)
        hkeep = r.take("hkeep", [P, NTL, D])
        moe_small = r.at
        ms_hi = [r.take(f"ms_hi{n}", [P, KD, P], F32R) for n in range(2)]
        ms_lo = [r.take(f"ms_lo{n}", [P, KD, P], F32R) for n in range(2)]
        xn = [r.take(f"xn{n}", [P, D]) for n in range(2)]
        hT = r.take("hT", [P, KD, P])
        g1 = r.take("g1", [P, D])
        assert r.at <= work
        tab_i = r.take("tab_i", [TABR, 3, P], I32)
        tab_f = r.take("tab_f", [TABR, 3, P])
        tokens = r.take("tokens", [P, NE * NTL], I32)
        assert r.at <= work
        r = Region(after_m)
        b1 = r.take("b1", [P, D])
        g2 = r.take("g2", [P, D])
        b2 = r.take("b2", [P, D])
        wr = r.take("wr", [P, KD, NR])
        rbias = r.take("rbias", [P, NR])
        bn = r.take("bn", [P, 2, 6])
        mv = r.take("mv", [P, 4])
        rt = r.take("rt", [P, 16 * 8])
        el = r.take("el", [P, NG, EPG])
        elm = r.take("elm", [P, NG, EPG])
        gi = r.take("gi", [P, 8], U32)
        ei = r.take("ei", [P, 8], U32)
        onehot = r.take("onehot", [P, NTL, 2, NE])
        chosen = r.take("chosen", [P, NE])
        seen = r.take("seen", [P, NE])
        posx = r.take("posx", [P, 2, NE])
        exk = r.take("exk", [P, NTL, 2])
        loc = r.take("loc", [P, NTL, 2])
        prow = r.take("prow", [P, NTL, 2])
        vdest = r.take("vdest", [P, NTL, 2], I32)
        tokid = r.take("tokid", [P, NTL], I32)
        zeros_i = r.take("zeros_i", [P, NE * VROWS // P], I32)
        cnt_i = r.take("cnt_i", [P, NE], I32)
        nblk = r.take("nblk", [P, NE])
        cum = [r.take(f"cum{n}", [P, NE]) for n in range(2)]
        first_row = r.take("first_row", [P, NE])
        blk = r.take("blk", [1, 4, MAXBLK + 1])
        blk_i = r.take("blk_i", [1, 2, MAXBLK + 1], I32)
        last_blk = r.take("last_blk", [1, NE], I32)
        yfirst = r.take("yfirst", [P, 2 * NTL])
        ydest_done = r.take("ydest_done", [P, 1])
        ydest = r.take("ydest", [P, NTL, 2], I32)
        scratch_end = r.at
        r = Region(base)
        e_raw, e_hi, e_lo = map(list, zip(*[r.split(f"we{n}", [P, GC]) for n in range(2)]))
        assert r.at <= nc_u
        r = Region(work)
        for lst, ten in zip((e_raw, e_hi, e_lo), r.split("we2", [P, GC])):
            lst.append(ten)
        assert r.at <= after_m
        r = Region(moe_small)
        xg = r.take("xg", [P, D])
        xb_hi = r.take("xb_hi", [P, KD, P], F32R)
        xb_lo = r.take("xb_lo", [P, KD, P], F32R)
        sg = r.take("sg", [P, DE])
        hid = r.take("hid", [P, DE])
        hb_hi = r.take("hb_hi", [P, 4, P], F32R)
        hb_lo = r.take("hb_lo", [P, 4, P], F32R)
        yb = r.take("yb", [P, D])
        assert r.at <= work - 2 * 4096 - 64
        idx = nc.alloc_sbuf_tensor_at("idx", [P, 1], I32, offset=scratch_end)
        tick = nc.alloc_sbuf_tensor_at("tick", [1, 1], F32, offset=scratch_end + 32)
        assert scratch_end + 64 <= limit
        cmp = nc.alloc_sbuf_tensor_at("cmp", [P, NTL * 2 * NE * 3], F32, offset=moe_small + 4096 * 4)
        r = Region(base)
        yg = [[r.take(f"yg{n}{k}", [P, D]) for k in range(2)] for n in range(2)]
        on = [r.take(f"on{n}", [P, D]) for n in range(2)]

        sems = {}

        def s(name):
            if name not in sems:
                sems[name] = sem(name)
            return sems[name]

        E_IN = [("g_in0", "w_in0"), ("g_in1", "w_in1"), ("g_in2", "g_in3")]
        E_IN_BEFORE = [(16 * KD, 16 * (NCH // 2)), (16 * KD, 16 * (NCH // 2)), (16 * KD, 0)]

        block = ctx.enter_context(nc.Block())

        def col(M, n, a, b):
            return rt[0:M, 8 * n + a:8 * n + b]

        def halves(t):
            return t.rearrange("p (a c) -> p a c", a=2)

        def as_f32(t):
            return t.bitcast(F32)

        @block.sync
        def _(sp):
            for k in range(KD):
                sp.dma_start(xraw[:, k, :], io["xT"][:, k, :]).then_inc(s(f"k_in{k}"), 16)
                if k < 2:
                    sp.dma_start(wraw[k][:], io["w_u"][k]).then_inc(s(f"w_in{k}"), 16)
            sp.dma_start(const[:], io["const"]).then_inc(s("const_in"), 16)
            sp.dma_start(cos[:], io["cos"]).then_inc(s("const_in"), 16)
            sp.dma_start(sin[:], io["sin"]).then_inc(s("const_in"), 16)
            sp.dma_start(sinks[:], io["sinks"].partition_broadcast(P)).then_inc(s("const_in"), 16)
            for g in range(2):
                for h in range(4):
                    sp.dma_start(sinks_s[DEC * h:DEC * h + DEC, g:g + 1],
                                 io["sinks"][4 * g + h:4 * g + h + 1].partition_broadcast(DEC)
                                 ).then_inc(s("const_in"), 16)
            with sp.Fori(1, NCH // 2) as i:
                for n in range(2):
                    sp.wait_ge(s("u_mm"), 2 * (i - 1) + (n + 1))
                    sp.dma_start(wraw[n][:], io["w_u"][bass.ds(2 * i + n, 1)].rearrange("a p k c -> (a p) k c")
                                 ).then_inc(s(f"w_in{n}"), 16)
            sp.wait_ge(s("u_out"), NCH)
            sp.dma_start(io["vat"], U[:, C_VA, SEQ - AWIN:MET]).then_inc(s("stored"), 16)
            sp.dma_start(io["kvb"], U[:, C_KB:NCH, 0:MET]).then_inc(s("stored"), 16)
            sp.wait_ge(s("rope_done"), 3 * NROPE)
            sp.dma_start(io["kat"], U[:, C_KA, SEQ - AWIN:MET]).then_inc(s("stored"), 16)
            sp.dma_start(y_rows[NE * P:MAXBLK * P, :].rearrange("(b p) d -> p b d", p=P),
                         U[:, C_KB:C_KB + 1, 0:D].to_broadcast([P, MAXBLK - NE, D])).then_inc(s("stored"), 16)
            sp.wait_ge(s("a_staged"), 1)
            sp.dma_start(ck_a[:], io["ck_a"]).then_inc(s("cache_in"), 16)
            sp.dma_start(cv_a[:], io["cv_a"]).then_inc(s("cache_in"), 16)
            sp.dma_start(ck_b[:], io["ck_b"]).then_inc(s("cache_in"), 16)
            sp.dma_start(cv_b[:], io["cv_b"]).then_inc(s("cache_in"), 16)
            sp.wait_ge(s("s_out"), 2)
            for n in range(3):
                sp.dma_start(graw[n][:], io["w_mix"][0, n]).then_inc(s(f"g_in{n}"), 16)
            with sp.Fori(1, KD) as i:
                for n in range(3):
                    sp.wait_ge(s(f"w_used{n}"), i)
                    sp.dma_start(graw[n][:], io["w_mix"][bass.ds(i, 1), n].rearrange("a p k c -> (a p) k c")
                                 ).then_inc(s(f"g_in{n}"), 16)
            for n in range(3):
                sp.wait_ge(s(f"w_used{n}"), KD)
            sp.wait_ge(s("m_out"), 3 * KD + 1)
            for k in range(KD):
                sp.dma_start(oraw[:, k, :], io["w_out"][k]).then_inc(s(f"k_in{k}"), 16)
                if k == 0:
                    for n in range(2):
                        sp.dma_start(xn[n][:], io["x_nat"][P * n:P * n + P, :]).then_inc(s(f"xn_in{n}"), 16)
                    for dst, src in ((g1, "ln1_g"), (b1, "ln1_b"), (g2, "ln2_g"), (b2, "ln2_b"), (rbias, "b_r")):
                        sp.dma_start(dst[:], io[src].partition_broadcast(P)).then_inc(s("ln_in"), 16)
                    sp.dma_start(wr[:], io["w_r"]).then_inc(s("ln_in"), 16)
            sp.wait_ge(s("zeros"), 1)
            sp.dma_start(tok_table.rearrange("(p c) o -> p (c o)", p=P), zeros_i[:]).then_inc(s("stored"), 16)
            for t in range(NTL):
                M = rows_of(t)
                sp.wait_ge(s("h_done"), t + 1)
                sp.dma_start(h_rows[P * t:P * t + M, :], hkeep[0:M, t, :]).then_inc(s("rows_out"), 16)
                if t + 2 < NTL:
                    M2 = rows_of(t + 2)
                    sp.dma_start(xn[t % 2][0:M2, :], io["x_nat"][P * (t + 2):P * (t + 2) + M2, :]
                                 ).then_inc(s(f"xn_in{t % 2}"), 16)

            def load_piece(e, n, q):
                c = slice(2 * PIECE * q, 2 * PIECE * q + 2 * PIECE)
                src = io["w_moe"][bass.ds(e, 1), n, :, c].rearrange("a p c -> (a p) c")
                sp.dma_start(e_raw[n][:, c], src).then_inc(s(E_IN[n][q]), 16)

            sp.wait_ge(s("ms_hi"), NTL)
            sp.wait_ge(s("ms_split"), NTL)
            for q in range(2):
                load_piece(0, 2, q)
            sp.wait_ge(s("o_mm"), NTL)
            for n in range(2):
                for q in range(2):
                    load_piece(0, n, q)
            sp.wait_ge(s("plan"), 3)
            with sp.Fori(1, NE) as e:
                b = sp.value_load(last_blk[0:1, bass.ds(e - 1, 1)], min_val=0, max_val=MAXBLK - 2) + 1
                for n in range(3):
                    for q in range(2):
                        sp.wait_ge(s(f"w_used{n}"), KD - 1 + q + 2 * b)
                        load_piece(e, n, q)
            for t in range(NTL):
                M = rows_of(t)
                sp.wait_ge(s("out_done"), t + 1)
                sp.dma_start(io["y"][P * t:P * t + M, :], on[t % 2][0:M, :]).then_inc(s(f"y_out{t % 2}"), 16)
            sp.wait_ge(s("stored"), 16 * 5)
            sp.wait_ge(s("y_out0"), 16 * ((NTL + 1) // 2))
            sp.wait_ge(s("y_out1"), 16 * (NTL // 2))

        @block.tensor
        def _(pe):
            def project(i, first):
                for n in range(2):
                    pe.wait_ge(s("w_split"), 2 * i + (n + 1))
                    if not first:
                        pe.wait_ge(s("u_out"), 2 * (i - 1) + (n + 1))
                    for k in range(KD):
                        if first and n == 0:
                            pe.wait_ge(s("x_split"), k + 1)
                        for c in range(3):
                            a, b = TCUT[c], TCUT[c + 1]
                            o = ps[:, 3 * n + c, 0:b - a]
                            pe.matmul(o, whi[n][:, k, :], xh[:, k, a:b], start=k == 0, stop=False)
                            pe.matmul(o, whi[n][:, k, :], xl[:, k, a:b], start=False, stop=False)
                            last = pe.matmul(o, wlo[n][:, k, :], xh[:, k, a:b], start=False, stop=k == KD - 1)
                    last.then_inc(s("u_mm"), 1)

            project(0, True)
            with pe.Fori(1, NCH // 2) as i:
                project(i, False)
            pe.wait_ge(s("u_out"), NCH)
            for c in range(NROPE):
                for j in range(3):
                    u = 3 * c + j
                    a, b = TCUT[j], TCUT[j + 1]
                    if u >= 2:
                        pe.wait_ge(s("rope_sin"), u - 1)
                    pe.matmul(ps[:, u % 2, 0:b - a], rot, U[:, c, a:b], start=True, stop=True
                              ).then_inc(s("rope_swap"), 1)
            for t in range(NT):
                last = pe.transpose(ps[:, 2 + t // 4, P * (t % 4):P * (t % 4) + P], U[:, C_VA, P * t:P * t + P], ident)
                if t < 2:
                    last.then_inc(s("b_vtr2" if t else "b_pv"), 1)
            pe.transpose(ps[0:DEC, 4, 0:P], U[:, C_VA, SAM:MET], ident)
            pe.transpose(ps[0:META, 5, 0:P], U[:, C_VA, MET:TOK], ident).then_inc(s("va_tr"), 1)

            def a_scores(m, u, peeled):
                if not (peeled and m < 2):
                    pe.wait_ge(s("a_masked"), u - 1)
                for g in range(2):
                    rows = slice(HD * g, HD * g + HD)
                    bank = ps[:, 2 * (m % 2) + g, :]
                    q = qas[rows, m, :]
                    pe.matmul(bank[:, 0:META], q, U[rows, C_KA, MET:TOK], start=True, stop=True)
                    if peeled:
                        last = pe.matmul(bank[:, META + P:BAND], q, kas[rows, P:2 * P], start=True, stop=True)
                    else:
                        last = pe.matmul(bank[:, META:BAND], q, kas[rows, :], start=True, stop=True)
                last.then_inc(s("a_scored"), 1)

            def a_values(m, u, peeled):
                pe.wait_ge(s("a_prob"), 2 * u + 2)
                for g in range(2):
                    e = prob[m % 2][:, g, :]
                    pe.transpose(ps[:, 4, 2 * P * g:2 * P * g + P], e[:, META:META + P], ident)
                    pe.transpose(ps[:, 4, 2 * P * g + P:2 * P * g + 2 * P], e[:, META + P:BAND], ident)
                    last = pe.transpose(ps[0:META, 5, P * g:P * g + P], e[:, 0:META], ident)
                last.then_inc(s("a_turned"), 1)
                pe.wait_ge(s("a_pt"), u + 1)
                pe.wait_ge(s("a_ptm"), u + 1)
                if not (peeled and m == 0):
                    pe.wait_ge(s("a_out"), u)
                for g in range(2):
                    rows = slice(HD * g, HD * g + HD)
                    o = ps[rows, 6, 0:P]
                    if not peeled:
                        pe.matmul(o, vas[:, 0, rows], pts[:, 2 * P * g:2 * P * g + P], start=True, stop=False)
                    pe.matmul(o, vas[:, 1, rows], pts[:, 2 * P * g + P:2 * P * g + 2 * P], start=peeled, stop=False)
                    last = pe.matmul(o, van_m[:, rows], ptms[:, P * g:P * g + P], start=False, stop=True)
                last.then_inc(s("a_mixed"), 1)

            def a_tile(u0, peeled):
                a_scores(0, u0, peeled)
                for m in range(PAIRS):
                    if m + 1 < PAIRS:
                        a_scores(m + 1, u0 + (m + 1), peeled)
                    a_values(m, u0 + m, peeled)

            pe.wait_ge(s("rope_done"), 3 * NROPE)
            pe.wait_ge(s("a_staged"), 1)
            pe.wait_ge(s("va_out"), 4)
            a_tile(0, True)
            with pe.Fori(1, NT) as i:
                pe.wait_ge(s("a_staged"), i + 1)
                a_tile(PAIRS * i, False)
            NU = NT * PAIRS
            pe.wait_ge(s("cache_in"), 16 * 4)
            pe.wait_ge(s("as_staged"), 1)
            pe.wait_ge(s("a_masked"), NU)
            for g in range(2):
                rows = slice(HD * g, HD * g + HD)
                q = qas_s[rows].rearrange("p h q -> p (h q)")
                o = ps[:, g, :]
                pe.matmul(o[:, 0:DEC], q, U[rows, C_KA, SAM:MET], start=True, stop=True)
                pe.matmul(o[:, DEC:DEC + AWIN], q, ck_a[rows, :], start=True, stop=True)
                pe.matmul(o[:, DEC + AWIN:AKEYS], q, U[rows, C_KA, MET:TOK], start=True, stop=True
                          ).then_inc(s("as_scored"), 1)
            pe.wait_ge(s("a_out"), NU)
            for g in range(2):
                rows = slice(HD * g, HD * g + HD)
                pe.wait_ge(s("as_prob"), g + 1)
                if g:
                    pe.wait_ge(s("as_pt"), 3)
                e = prob[0][:, g, :]
                pe.transpose(ps[0:DEC, 4, 0:P], e[:, 0:DEC], ident)
                pe.transpose(ps[:, 4, P:2 * P], e[:, DEC:DEC + AWIN], ident)
                pe.transpose(ps[0:META, 4, 2 * P:3 * P], e[:, DEC + AWIN:AKEYS], ident).then_inc(s("as_turned"), 1)
                pe.wait_ge(s("as_pt"), 3 * g + 3)
                o = ps[rows, 6, 0:P]
                pe.matmul(o, van_s[:, rows], pts[0:DEC, 0:P], start=True, stop=False)
                pe.matmul(o, cv_a[:, rows], pts[:, P:2 * P], start=False, stop=False)
                pe.matmul(o, van_m[:, rows], pts[0:META, 2 * P:3 * P], start=False, stop=True
                          ).then_inc(s("as_mixed"), 1)

            pe.wait_ge(s("as_out"), 2)
            with pe.Fori(0, PAIRS) as p:
                pe.wait_ge(s("b_vstaged"), p + 1)
                pe.wait_ge(s("b_omain"), 4 * p + 1)
                for t in range(NT):
                    pe.transpose(ps[:, 6 + t // 4, P * (t % 4):P * (t % 4) + P], vts[:, P * t:P * t + P], ident
                                 ).then_inc(s("b_vtr"), 1)
                pe.wait_ge(s("b_vn"), 5 * p + 2)
                pe.transpose(ps[0:META, 6, 0:P], vts[:, MET:TOK], ident)
                pe.transpose(ps[0:DEC, 7, 0:P], vts[:, SAM:MET], ident).then_inc(s("b_vtr2"), 1)
                pe.wait_ge(s("b_kl"), p + 1)
                pe.wait_ge(s("b_ql"), p + 1)
                pe.wait_ge(s("b_vn"), 5 * p + 5)

                def z_of(n):
                    a, c, t = STEPS[n]
                    rows = slice(HD * a, HD * a + HD)
                    M, q0, _ = step_shape(c, t)
                    o = ps[0:M, n % 4, q0:QCH]
                    keys = slice(P * t, P * t + P) if t >= 0 else slice(MET, TOK)
                    cols = slice(QCH * c + q0, QCH * c + QCH)
                    pe.matmul(o, kh[rows, keys], qh[rows, cols], start=True, stop=False, skip_group_check=True)
                    pe.matmul(o, kh[rows, keys], ql[rows, cols], start=False, stop=False, skip_group_check=True)
                    last = pe.matmul(o, kl[rows, keys], qh[rows, cols], start=False, stop=False,
                                     skip_group_check=True)
                    if t >= 4 * c:
                        last = pe.matmul(ps[:, n % 4, q0:q0 + P], ident, blkmask, start=False, stop=False,
                                         skip_group_check=True)
                    last.then_inc(s("b_z"), 1)

                def values_of(n):
                    a, c, t = STEPS[n]
                    rows = slice(HD * a, HD * a + HD)
                    M, q0, first = step_shape(c, t)
                    group = 2 * a + c
                    if first and group >= 2:
                        pe.wait_ge(s("b_omain"), 4 * p + group)
                    pe.wait_ge(s("b_w"), NSTEP * p + n + 1)
                    v = vn[:, t, rows] if t >= 0 else vn_m[:, rows]
                    last = pe.matmul(ps[rows, 4 + group % 2, q0:QCH], v, wgt[n % 2][0:M, q0:QCH],
                                     start=first, stop=t < 0, skip_group_check=True)
                    last.then_inc(s("b_pv"), 1)

                z_of(0)
                z_of(1)
                for n in range(NSTEP):
                    a, c, t = STEPS[n]
                    M, q0, first = step_shape(c, t)
                    if n + 2 < NSTEP:
                        z_of(n + 2)
                    o = ps[0:M, n % 4, q0:QCH]
                    pe.wait_ge(s("b_soft"), NSTEP * p + n + 1)
                    if not first:
                        pe.wait_ge(s("b_later"), NLATER * p + LATER_BEFORE[n])
                        pe.wait_ge(s("b_zeroed"), 4 * p + (2 * a + c + 1))
                        pe.matmul(o, nones[:, 0:M], later[:, q0:QCH], start=False, stop=False,
                                  skip_group_check=True)
                    last = pe.matmul(o, ntri[0:M, 0:M], soft[n % 2][0:M, q0:QCH], start=False, stop=True,
                                     skip_group_check=True)
                    last.then_inc(s("b_arg"), 1)
                    if n:
                        values_of(n - 1)
                values_of(NSTEP - 1)

            pe.wait_ge(s("cache_in"), 16 * 4)
            pe.wait_ge(s("s_q"), 1)
            pe.wait_ge(s("b_omain"), 4 * PAIRS + 1)
            def s_z(n):
                M, kt, _ = SAMPLE_TILES[n]
                for h in range(NH):
                    m, a = divmod(h, 2)
                    rows = slice(HD * a, HD * a + HD)
                    k = U[rows, C_KB + m, kt] if n in (0, 3) else ck_b[rows, m, kt]
                    last = pe.matmul(ps[0:M, s_bank(n) + a, DEC * m:DEC * m + DEC], k, qs[rows, m, :],
                                     start=m == 0, stop=False, skip_group_check=True)
                if n == 0:
                    for a in range(2):
                        last = pe.matmul(ps[0:M, a, 0:P], ident[0:M, 0:M], smask[:, P * a:P * a + P], start=False,
                                         stop=False, skip_group_check=True)
                last.then_inc(s("s_z"), 1)

            s_z(0)
            s_z(1)
            for n, (M, kt, vt) in enumerate(SAMPLE_TILES):
                if n:
                    pe.wait_ge(s("s_later"), n)
                pe.wait_ge(s("s_soft"), n + 1)
                for a in range(2):
                    o = ps[0:M, s_bank(n) + a, 0:P]
                    if n:
                        pe.matmul(o, nones[:, 0:M], later_s[:, P * a:P * a + P], start=False, stop=False,
                                  skip_group_check=True)
                    last = pe.matmul(o, ntri[0:M, 0:M], soft_s[0:M, P * a:P * a + P], start=False, stop=True,
                                     skip_group_check=True)
                last.then_inc(s("s_arg"), 1)
                pe.wait_ge(s("s_w"), n + 1)
                for h in range(NH):
                    m, a = divmod(h, 2)
                    rows = slice(HD * a, HD * a + HD)
                    v = (vall_s[:, m, rows] if n == 0 else vall_m[:, m, rows] if n == 3
                         else cv_b[:, vt, HD * h:HD * h + HD])
                    last = pe.matmul(ps[rows, 4 + a, DEC * m:DEC * m + DEC], v,
                                     wgt_s[0:M, P * a + DEC * m:P * a + DEC * m + DEC], start=n == 0 and m == 0,
                                     stop=n == 3, skip_group_check=True)
                last.then_inc(s("s_pv"), 1)
                if n < 2:
                    s_z(n + 2)

            def mix_thirds(i, odd):
                for j in range(3):
                    bank = 4 * ((odd + j) % 2)
                    cols = slice(TW * j, TW * j + TW)
                    for n in range(3):
                        if j == 0:
                            pe.wait_ge(s("g_split"), 3 * i + (n + 1))
                        if n == 0:
                            pe.wait_ge(s("m_read"), 3 * i + (j + 1))
                        for k in range(KD):
                            if n < 2:
                                o, hi, lo, first, end = ps[:, bank + n, 0:TW], xh[:, k, cols], xl[:, k, cols], \
                                    k == 0, k == KD - 1
                            else:
                                src = (oa_hi, oa_lo) if k < 4 else (ob_hi, ob_lo)
                                o, hi, lo = ps[:, bank + 2 + k // 4, 0:TW], src[0][:, k % 4, cols], \
                                    src[1][:, k % 4, cols]
                                first, end = k % 4 == 0, k % 4 == 3
                            pe.matmul(o, ghi[n][:, k, :], hi, start=first, stop=False)
                            pe.matmul(o, ghi[n][:, k, :], lo, start=False, stop=False)
                            last = pe.matmul(o, glo[n][:, k, :], hi, start=False, stop=end)
                        if j == 2:
                            last.then_inc(s(f"w_used{n}"), 1)
                        elif n == 2:
                            last.then_inc(s("m_mm"), 1)

            pe.wait_ge(s("oa_split"), 2)
            pe.wait_ge(s("s_out"), 2)
            with pe.Fori(0, KD // 2) as i:
                mix_thirds(2 * i, 0)
                mix_thirds(2 * i + 1, 1)

            def route_logits(t):
                M = rows_of(t)
                pe.wait_ge(s("h_done"), t + 1)
                if t:
                    pe.wait_ge(s("hT_out"), 2 * t)
                for k in range(KD):
                    last = pe.transpose(ps[:, 4 + k // 4, P * (k % 4):P * (k % 4) + M],
                                        hkeep[0:M, t, P * k:P * k + P], ident[0:M, 0:M])
                last.then_inc(s("hT_tr"), 1)
                pe.wait_ge(s("hT_out"), 2 * t + 2)
                if t:
                    pe.wait_ge(s("r_read"), t)
                for k in range(KD):
                    last = pe.matmul(ps[0:M, 6, 0:NR], hT[:, k, 0:M], wr[:, k, :], start=k == 0, stop=k == KD - 1)
                last.then_inc(s("r_mm"), 1)

            def route_places(t):
                M = rows_of(t)
                pe.wait_ge(s("r_chosen"), t + 1)
                if t:
                    pe.wait_ge(s("r_seen"), t)
                pe.matmul(ps[0:M, 7, 0:NE], sup[0:M, 0:M], chosen[0:M, :], start=True, stop=False)
                pe.matmul(ps[0:M, 7, 0:NE], ones[:, 0:M], seen[:], start=False, stop=True).then_inc(s("r_pos"), 1)

            pe.wait_ge(s("ln_in"), 16 * 6)
            pe.wait_ge(s("m_read"), 3 * KD + 2)
            for t in range(NTL):
                M, n = rows_of(t), t % 2
                pe.wait_ge(s("ms_split"), t + 1)
                if t >= 2:
                    pe.wait_ge(s("r_added"), t - 1)
                for k in range(KD):
                    if t == 0:
                        pe.wait_ge(s("o_split"), k + 1)
                    for c in range(2):
                        o, cols = ps[0:M, 2 * n + c, :], slice(512 * c, 512 * c + 512)
                        pe.matmul(o, ms_hi[n][:, k, 0:M], ohi[:, k, cols], start=k == 0, stop=False)
                        pe.matmul(o, ms_hi[n][:, k, 0:M], olo[:, k, cols], start=False, stop=False)
                        last = pe.matmul(o, ms_lo[n][:, k, 0:M], ohi[:, k, cols], start=False, stop=k == KD - 1)
                last.then_inc(s("o_mm"), 1)
                if t:
                    route_logits(t - 1)
                if t >= 2:
                    route_places(t - 2)
            route_logits(NTL - 1)
            route_places(NTL - 2)
            route_places(NTL - 1)
            pe.wait_ge(s("r_seen"), NTL)
            pe.matmul(ps[:, 0, 0:NE], ones, seen[:], start=True, stop=True).then_inc(s("r_count"), 1)
            pe.wait_ge(s("tokens"), 1)
            for g in range(3):
                last = pe.transpose(ps[:, 1, TABR * g:TABR * g + TABR], tab_f[:, g, :], ident[0:TABR, 0:TABR])
            last.then_inc(s("tab_tr"), 1)

            def turn_x(b):
                pe.wait_ge(s("x_got"), 16 * b + 16)
                for k in range(KD):
                    last = pe.transpose(ps[:, 2 + k // 4, P * (k % 4):P * (k % 4) + P], xg[:, P * k:P * k + P], ident)
                last.then_inc(s("xb_tr"), 1)

            def turn_h(b, half):
                pe.wait_ge(s("hid"), 2 * b + (half + 1))
                for k in (2 * half, 2 * half + 1):
                    last = pe.transpose(ps[:, 4, P * k:P * k + P], hid[:, P * k:P * k + P], ident)
                last.then_inc(s("hb_tr"), 1)

            def block_mm(b, e, first):
                for half in range(2):
                    if not first:
                        pe.wait_ge(s("hid"), 2 * (b - 1) + (half + 1))
                    for k in range(KD):
                        if half == 0 and k == 0:
                            pe.wait_ge(s("xb_split"), 2 * b + 2)
                        if k % 2 == 0:
                            q = k // 2
                            if q < 3:
                                pe.wait_ge(s("e_split"), 9 * e + (3 * half + q + 1))
                            else:
                                pe.wait_ge(s("e_split3"), 3 * e + (half + 1))
                        o, c = ps[:, half, :], slice(2 * HH * k, 2 * HH * k + 2 * HH)
                        pe.matmul(o, xb_hi[:, k, :], e_hi[half][:, c], start=k == 0, stop=False)
                        pe.matmul(o, xb_hi[:, k, :], e_lo[half][:, c], start=False, stop=False)
                        last = pe.matmul(o, xb_lo[:, k, :], e_hi[half][:, c], start=False, stop=k == KD - 1)
                        if k in (3, 7):
                            last.then_inc(s(f"w_used{half}"), 1)
                turn_h(b, 0)
                turn_x(b + 1)
                if not first:
                    pe.wait_ge(s("y_read"), 2 * b)
                for k in range(4):
                    if k == 1:
                        turn_h(b, 1)
                    if k % 2 == 0:
                        pe.wait_ge(s("hb_split"), 2 * b + (k // 2 + 1))
                    if k < 3:
                        pe.wait_ge(s("e_split"), 9 * e + (6 + k + 1))
                    else:
                        pe.wait_ge(s("e_split3"), 3 * e + 3)
                    for c in range(2):
                        o, cols = ps[:, 5 + c, :], slice(D * k + 512 * c, D * k + 512 * c + 512)
                        pe.matmul(o, hb_hi[:, k, :], e_hi[2][:, cols], start=k == 0, stop=False)
                        pe.matmul(o, hb_hi[:, k, :], e_lo[2][:, cols], start=False, stop=False)
                        last = pe.matmul(o, hb_lo[:, k, :], e_hi[2][:, cols], start=False, stop=k == 3)
                    if k in (1, 3):
                        last.then_inc(s("w_used2"), 1)

            pe.wait_ge(s("plan"), 3)
            nb = pe.value_load(last_blk[0:1, NE - 1:NE], min_val=NE - 1, max_val=MAXBLK - 1) + 1
            turn_x(0)
            block_mm(0, 0, True)
            with pe.Fori(1, nb) as b:
                e = pe.value_load(blk_i[0:1, 0, bass.ds(b, 1)], min_val=0, max_val=NE - 1)
                block_mm(b, e, False)

        @block.scalar
        def _(act):
            act.preload_act_table_set("natural_log_exp_and_others")
            with act.Fori(0, NCH // 2) as i:
                for n in range(2):
                    act.wait_ge(s("u_mm"), 2 * i + (n + 1))
                    for c in range(3):
                        a, b = TCUT[c], TCUT[c + 1]
                        last = act.activation(U[:, bass.ds(2 * i + n, 1), a:b], ps[:, 3 * n + c, 0:b - a], ACT.Copy)
                    last.then_inc(s("u_out"), 1)
            act.wait_ge(s("va_tr"), 1)
            for j in range(2):
                act.activation(van[:, 4 * j:4 * j + 4, :], ps[:, 2 + j, :].rearrange("p (t c) -> p t c", t=4),
                               ACT.Copy).then_inc(s("va_out"), 1)
            act.activation(van_s[:], ps[0:DEC, 4, 0:P], ACT.Copy).then_inc(s("va_out"), 1)
            act.activation(van_m[:], ps[0:META, 5, 0:P], ACT.Copy).then_inc(s("va_out"), 1)

            def a_exp(m, u):
                st = stat[m % 2]
                act.wait_ge(s("a_nmax"), u + 1)
                for g in range(2):
                    act.activation(prob[m % 2][:, g, :], msk[m % 2][:, g, :], ACT.Exp, bias=st[:, 1, g:g + 1],
                                   scale=SCALE, accum_out=st[:, 3, g:g + 1]).then_inc(s("a_exp"), 1)
                act.wait_ge(s("a_dsink"), u + 1)
                act.activation(st[:, 4, :], st[:, 2, :], ACT.Exp).then_inc(s("a_exp"), 1)

            def a_drain(m, u, cols):
                act.wait_ge(s("a_turned"), u + 1)
                act.activation(pts[:], ps[:, 4, :], ACT.Copy).then_inc(s("a_pt"), 1)
                act.wait_ge(s("a_mixed"), u + 1)
                act.activation(U[:, m, cols], ps[:, 6, 0:P], ACT.Copy).then_inc(s("a_out"), 1)

            def a_tile(u0, cols):
                a_exp(0, u0)
                for m in range(PAIRS):
                    if m + 1 < PAIRS:
                        a_exp(m + 1, u0 + (m + 1))
                    a_drain(m, u0 + m, cols)

            a_tile(0, slice(0, P))
            with act.Fori(1, NT) as i:
                a_tile(PAIRS * i, bass.ds(P * i, P))
            for g in range(2):
                st = stat[0]
                act.wait_ge(s("as_nmax"), g + 1)
                act.activation(prob[0][:, g, 0:AKEYS], msk[0][:, g, 0:AKEYS], ACT.Exp, bias=st[:, 1, g:g + 1],
                               scale=SCALE, accum_out=st[:, 3, g:g + 1]).then_inc(s("as_exp"), 1)
                act.wait_ge(s("as_dsink"), g + 1)
                act.activation(st[:, 4, g:g + 1], st[:, 2, g:g + 1], ACT.Exp).then_inc(s("as_exp"), 1)
            for g in range(2):
                rows = slice(HD * g, HD * g + HD)
                act.wait_ge(s("as_turned"), g + 1)
                if g:
                    act.wait_ge(s("as_mixed"), 1)
                act.activation(pts[0:DEC, 0:P], ps[0:DEC, 4, 0:P], ACT.Copy).then_inc(s("as_pt"), 1)
                act.activation(pts[:, P:2 * P], ps[:, 4, P:2 * P], ACT.Copy).then_inc(s("as_pt"), 1)
                act.activation(pts[0:META, 2 * P:3 * P], ps[0:META, 4, 2 * P:3 * P], ACT.Copy
                               ).then_inc(s("as_pt"), 1)
                act.wait_ge(s("as_mixed"), g + 1)
                act.activation(U[rows, 0:4, SAM:MET], ps[rows, 6, 0:P].rearrange("p (h q) -> p h q", h=4),
                               ACT.Copy).then_inc(s("as_out"), 1)

            act.wait_ge(s("as_out"), 2)
            with act.Fori(0, PAIRS) as p:
                act.wait_ge(s("b_pv"), NSTEP * p + 1)
                act.activation(kh[:], U[:, bass.ds(C_KB + p, 1), :], ACT.Copy).then_inc(s("b_kh"), 1)
                act.activation(qh[:], U[:, bass.ds(C_QB + p, 1), 0:SEQ], ACT.Copy, scale=SCALE
                               ).then_inc(s("b_qh"), 1)
                act.wait_ge(s("b_vtr"), NT * p + NT)
                for j in range(2):
                    act.activation(vn[:, 4 * j:4 * j + 4, :], ps[:, 6 + j, :].rearrange("p (t c) -> p t c", t=4),
                                   ACT.Copy).then_inc(s("b_vn"), 1)
                act.wait_ge(s("b_vtr2"), p + 2)
                act.activation(vn_m[:], ps[0:META, 6, 0:P], ACT.Copy).then_inc(s("b_vn"), 1)
                act.activation(vall_m[:, bass.ds(p, 1), :], ps[0:META, 6, 0:P], ACT.Copy).then_inc(s("b_vn"), 1)
                act.activation(vall_s[:, bass.ds(p, 1), :], ps[0:DEC, 7, 0:P], ACT.Copy).then_inc(s("b_vn"), 1)

                def soft_of(n):
                    a, c, t = STEPS[n]
                    M, q0, _ = step_shape(c, t)
                    e = capped[n % 2][0:M, q0:QCH]
                    act.wait_ge(s("b_cap"), NSTEP * p + n + 1)
                    act.activation(e, e, ACT.Exp).then_inc(s("b_exp"), 1)
                    act.wait_ge(s("b_exp"), NSTEP * p + n + 1)
                    act.activation(e, e, ACT.Ln, bias=1.0).then_inc(s("b_ln"), 1)

                soft_of(0)
                for n in range(NSTEP):
                    a, c, t = STEPS[n]
                    M, q0, _ = step_shape(c, t)
                    if n + 1 < NSTEP:
                        soft_of(n + 1)
                    act.wait_ge(s("b_arg"), NSTEP * p + n + 1)
                    if n >= 2:
                        act.wait_ge(s("b_pv"), NSTEP * p + n)
                    act.activation(wgt[n % 2][0:M, q0:QCH], ps[0:M, n % 4, q0:QCH], ACT.Exp
                                   ).then_inc(s("b_w"), 1)
            for n, (M, kt, vt) in enumerate(SAMPLE_TILES):
                e = capped_s[0:M, :]
                act.wait_ge(s("s_cap"), n + 1)
                act.activation(e, e, ACT.Exp).then_inc(s("s_exp"), 1)
                act.wait_ge(s("s_exp"), n + 1)
                act.activation(e, e, ACT.Ln, bias=1.0).then_inc(s("s_ln"), 1)
                act.wait_ge(s("s_arg"), n + 1)
                if n:
                    act.wait_ge(s("s_pv"), n)
                act.activation(halves(wgt_s[0:M, :]), ps[0:M, s_bank(n):s_bank(n) + 2, 0:P], ACT.Exp).then_inc(s("s_w"), 1)
            act.wait_ge(s("s_pv"), 4)
            for a in range(2):
                rows = slice(HD * a, HD * a + HD)
                act.activation(U[rows, C_QB:C_QB + PAIRS, SAM:MET],
                               ps[rows, 4 + a, 0:PAIRS * DEC].rearrange("p (m q) -> p m q", m=PAIRS), ACT.Copy
                               ).then_inc(s("s_out"), 1)

            act.wait_ge(s("s_out"), 2)
            act.wait_ge(s("b_omain"), 4 * PAIRS + 1)
            act.wait_ge(s("stored"), 16 * 4)
            act.activation(oa_hi[:, :, 0:LIVE], U[:, C_QA:C_QA + 4, 0:LIVE], ACT.Copy).then_inc(s("oa_hi"), 1)
            act.activation(ob_hi[:, :, 0:LIVE], U[:, C_QB:C_QB + 4, 0:LIVE], ACT.Copy).then_inc(s("oa_hi"), 1)
            act.preload_act_table_set("sigmoid_and_others")
            def round_mix(i, n):
                act.wait_ge(s(f"g_in{n}"), 16 * i + 16)
                act.activation(ghi[n][:], graw[n][:], ACT.Copy).then_inc(s("g_hi"), 1)

            def gate_thirds(i, odd, last):
                for j in range(3):
                    if j < 2:
                        act.wait_ge(s("m_mm"), 2 * i + (j + 1))
                    else:
                        if not last:
                            round_mix(i + 1, 0)
                        act.wait_ge(s("w_used2"), i + 1)
                    act.wait_ge(s("m_read"), 3 * i + (j + 1))
                    for w in range(2):
                        act.activation(sig[(odd + j) % 2][w][:], ps[:, 4 * ((odd + j) % 2) + w, 0:TW], ACT.Sigmoid
                                       ).then_inc(s("sig"), 1)
                if not last:
                    round_mix(i + 1, 1)
                    round_mix(i + 1, 2)

            for n in range(3):
                round_mix(0, n)
            with act.Fori(0, KD // 2 - 1) as i:
                gate_thirds(2 * i, 0, False)
                gate_thirds(2 * i + 1, 1, False)
            gate_thirds(KD - 2, 0, False)
            gate_thirds(KD - 1, 1, True)
            def ms_round(t):
                M, n = rows_of(t), t % 2
                if t >= 2:
                    act.wait_ge(s("o_mm"), t - 1)
                act.activation(ms_hi[n][:, :, 0:M], mT[:, :, P * t:P * t + M], ACT.Copy).then_inc(s("ms_hi"), 1)

            def hT_drain(t):
                M = rows_of(t)
                act.wait_ge(s("hT_tr"), t + 1)
                if t:
                    act.wait_ge(s("r_mm"), t)
                for c in range(2):
                    act.activation(hT[:, 4 * c:4 * c + 4, 0:M],
                                   ps[:, 4 + c, :].rearrange("p (k m) -> p k m", k=4)[:, :, 0:M], ACT.Copy
                                   ).then_inc(s("hT_out"), 1)

            def route_exp(t):
                M = rows_of(t)
                act.wait_ge(s("r_nmax"), t + 1)
                act.activation(col(M, 4, 0, 4), col(M, 0, 0, 4), ACT.Exp, bias=col(M, 3, 0, 1),
                               accum_out=col(M, 5, 0, 1)).then_inc(s("r_exp"), 1)
                act.wait_ge(s("r_gap"), t + 1)
                act.activation(col(M, 7, 0, 1), col(M, 6, 0, 1), ACT.Exp).then_inc(s("r_exp"), 1)

            act.wait_ge(s("m_out"), 3 * KD + 1)
            act.preload_act_table_set("exp_and_others")
            ms_round(0)
            for k in range(KD):
                act.wait_ge(s(f"k_in{k}"), 32)
                act.activation(ohi[:, k, :], oraw[:, k, :], ACT.Copy).then_inc(s("o_hi"), 1)
            for t in range(NTL):
                if t + 1 < NTL:
                    ms_round(t + 1)
                if t:
                    hT_drain(t - 1)
                    route_exp(t - 1)
            hT_drain(NTL - 1)
            route_exp(NTL - 1)

            def drain_y(done):
                act.wait_ge(s("w_used2"), KD + 2 * done)
                act.wait_ge(s("rows_out"), 16 * (NTL - 1) + 16 * done)
                for c in range(2):
                    act.activation(yb[:, 512 * c:512 * c + 512], ps[:, 5 + c, :], ACT.Copy).then_inc(s("y_read"), 1)
                act.wait_ge(s("y_read"), 2 * done)
                act.dma_start(y_rows[bass.ds(P * (done - 1), P), :], yb[:]).then_inc(s("rows_out"), 16)

            def round_third(n, e):
                for q in range(4):
                    if q % 2 == 0:
                        act.wait_ge(s(E_IN[n][q // 2]), E_IN_BEFORE[n][q // 2] + 16 * e + 16)
                    c = slice(PIECE * q, PIECE * q + PIECE)
                    act.activation(e_hi[n][:, c], e_raw[n][:, c], ACT.Copy).then_inc(s("e_hi"), 1)

            def silu(half, b):
                act.wait_ge(s(f"w_used{half}"), KD + 2 + 2 * b)
                act.activation(sg[:, HH * half:HH * half + HH], ps[:, half, 0:HH], ACT.Silu
                               ).then_inc(s("silu"), 1)

            def round_x(b):
                act.wait_ge(s("xb_tr"), b + 1)
                for c in range(2):
                    act.activation(xb_hi[:, 4 * c:4 * c + 4, :], ps[:, 2 + c, :].rearrange("p (k m) -> p k m", k=4),
                                   ACT.Copy).then_inc(s("xb_hi"), 1)

            def round_h(half, b):
                act.wait_ge(s("hb_tr"), 2 * b + (half + 1))
                act.activation(hb_hi[:, 2 * half:2 * half + 2, :],
                               ps[:, 4, HH * half:HH * half + HH].rearrange("p (k m) -> p k m", k=2), ACT.Copy
                               ).then_inc(s("hb_hi"), 1)

            def new_expert(b, e, first):
                if not first:
                    round_third(0, e)
                    drain_y(b)
                    round_third(1, e)
                silu(0, b)
                if not first:
                    round_third(2, e)
                silu(1, b)
                round_h(0, b)
                round_x(b + 1)
                round_h(1, b)

            def more_blocks(e, b):
                last = act.value_load(last_blk[0:1, bass.ds(e, 1)], min_val=0, max_val=MAXBLK - 1)
                with act.If(last > b):
                    with act.Fori(b + 1, last + 1) as more:
                        drain_y(more)
                        silu(0, more)
                        silu(1, more)
                        round_h(0, more)
                        round_x(more + 1)
                        round_h(1, more)

            for n in range(3):
                round_third(n, 0)
            act.wait_ge(s("plan"), 3)
            act.preload_act_table_set(SILU_SET)
            round_x(0)
            new_expert(0, 0, True)
            more_blocks(0, 0)
            with act.Fori(1, NE) as e:
                b = act.value_load(last_blk[0:1, bass.ds(e - 1, 1)], min_val=0, max_val=MAXBLK - 2) + 1
                new_expert(b, e, False)
                more_blocks(e, b)
            nb = act.value_load(last_blk[0:1, NE - 1:NE], min_val=NE - 1, max_val=MAXBLK - 1) + 1
            drain_y(nb)
            for t in range(NTL):
                M, n = rows_of(t), t % 2
                act.wait_ge(s(f"y_got{n}"), 32 * (t // 2) + 32)
                act.activation(yg[n][0][0:M, :], yg[n][0][0:M, :], ACT.Copy, scale=prow[0:M, t, 0:1]
                               ).then_inc(s("c_scaled"), 1)

        @block.vector
        def _(dve):
            steps = [0]

            def link(ins):
                steps[0] += 1
                ins.then_inc(s("dve_step"), 1)
                dve.wait_ge(s("dve_step"), steps[0])

            for k in range(KD):
                dve.wait_ge(s(f"k_in{k}"), 16)
                dve.tensor_copy(xh[:, k, :], xraw[:, k, :]).then_inc(s("x_hi"), 1)
                dve.wait_ge(s("x_hi"), k + 1)
                dve.tensor_tensor(xl[:, k, :], xraw[:, k, :], as_f32(xh[:, k, :]), ALU.subtract
                                  ).then_inc(s("x_split"), 1)
                if k < 2:
                    dve.wait_ge(s(f"w_in{k}"), 16)
                    dve.tensor_copy(whi[k][:], wraw[k][:]).then_inc(s("w_hi"), 1)
                    dve.wait_ge(s("w_hi"), k + 1)
                    dve.tensor_tensor(wlo[k][:], wraw[k][:], as_f32(whi[k][:]), ALU.subtract
                                      ).then_inc(s("w_split"), 1)
            with dve.Fori(1, NCH // 2) as i:
                for n in range(2):
                    dve.wait_ge(s(f"w_in{n}"), 16 * i + 16)
                    dve.tensor_copy(whi[n][:], wraw[n][:]).then_inc(s("w_hi"), 1)
                    dve.wait_ge(s("w_hi"), 2 * i + (n + 1))
                    dve.tensor_tensor(wlo[n][:], wraw[n][:], as_f32(whi[n][:]), ALU.subtract
                                      ).then_inc(s("w_split"), 1)
            dve.wait_ge(s("const_in"), 16 * 12)
            for c in range(NROPE):
                for j in range(3):
                    u = 3 * c + j
                    a, b = TCUT[j], TCUT[j + 1]
                    t = ropet[u % 2][:, 0:b - a]
                    dve.wait_ge(s("rope_swap"), u + 1)
                    dve.tensor_tensor(t, ps[:, u % 2, 0:b - a], sin[:, a:b], ALU.mult).then_inc(s("rope_sin"), 1)
                    dve.tensor_tensor(U[:, c, a:b], U[:, c, a:b], cos[:, a:b], ALU.mult).then_inc(s("rope_cos"), 1)
                    dve.wait_ge(s("rope_sin"), u + 1)
                    dve.wait_ge(s("rope_cos"), u + 1)
                    dve.tensor_tensor(U[:, c, a:b], U[:, c, a:b], t, ALU.add).then_inc(s("rope_done"), 1)
            dve.wait_ge(s("rope_done"), 3 * NROPE)
            for n in range(2):
                dve.memset(msk[n][:, :, META:META + P], NEG).then_inc(s("b_omain" if n else "m_read"), 1)
            for n in range(2):
                dve.memset(stat[n][:, 6, :], 0.0).then_inc(s("m_out" if n else "m_read"), 1)

            def a_softmax_in(m, u, peeled):
                st, sm = stat[m % 2], msk[m % 2]
                banks = ps[:, 2 * (m % 2):2 * (m % 2) + 2, :]
                both = amask.rearrange("p (o k) -> p o k", o=1)
                dve.wait_ge(s("a_scored"), u + 1)
                if peeled:
                    dve.tensor_copy(sm[:, :, 0:META], banks[:, :, 0:META])
                    last = dve.tensor_tensor(sm[:, :, META + P:BAND], banks[:, :, META + P:BAND],
                                             both[:, :, META + P:BAND].to_broadcast([P, 2, P]), ALU.add)
                else:
                    last = dve.tensor_tensor(sm[:], banks[:, :, 0:BAND], both.to_broadcast([P, 2, BAND]), ALU.add)
                last.then_inc(s("a_masked"), 1)
                dve.wait_ge(s("a_masked"), u + 1)
                dve.tensor_reduce(st[:, 0, :], sm[:], AX.X, ALU.max).then_inc(s("a_max"), 1)
                dve.wait_ge(s("a_max"), u + 1)
                sink = sinks[:, m:m + 5:4]
                dve.scalar_tensor_tensor(out=st[:, 5, :], in0=st[:, 0, :], scalar=SCALE, in1=sink, op0=ALU.mult,
                                         op1=ALU.max).then_inc(s("a_top"), 1)
                dve.wait_ge(s("a_top"), u + 1)
                dve.tensor_scalar(st[:, 1, :], st[:, 5, :], -1.0, None, ALU.mult).then_inc(s("a_nmax"), 1)
                dve.tensor_tensor(st[:, 2, :], sink, st[:, 5, :], ALU.subtract).then_inc(s("a_dsink"), 1)

            def a_softmax_out(m, u):
                st = stat[m % 2]
                dve.wait_ge(s("a_exp"), 3 * u + 3)
                dve.tensor_tensor(st[:, 6, :], st[:, 3, :], st[:, 4, :], ALU.add).then_inc(s("a_den"), 1)
                dve.wait_ge(s("a_den"), u + 1)
                dve.reciprocal(st[:, 7, :], st[:, 6, :]).then_inc(s("a_rden"), 1)
                dve.wait_ge(s("a_rden"), u + 1)
                for g in range(2):
                    e = prob[m % 2][:, g, :]
                    dve.tensor_scalar(e, e, st[:, 7, g:g + 1], None, ALU.mult).then_inc(s("a_prob"), 1)
                dve.wait_ge(s("a_turned"), u + 1)
                dve.tensor_copy(ptms[:], ps[0:META, 5, 0:2 * P]).then_inc(s("a_ptm"), 1)

            def a_tile(u0, peeled):
                a_softmax_in(0, u0, peeled)
                for m in range(PAIRS):
                    if m + 1 < PAIRS:
                        a_softmax_in(m + 1, u0 + (m + 1), peeled)
                    a_softmax_out(m, u0 + m)

            a_tile(0, True)
            with dve.Fori(1, NT) as i:
                a_tile(PAIRS * i, False)
            st = stat[0]
            for g in range(2):
                sm = msk[0][:, g, 0:AKEYS]
                dve.wait_ge(s("as_scored"), g + 1)
                link(dve.tensor_copy(sm, ps[:, g, 0:AKEYS]))
                link(dve.tensor_reduce(st[:, 0, g:g + 1], sm, AX.X, ALU.max))
                sink = sinks_s[:, g:g + 1]
                link(dve.scalar_tensor_tensor(out=st[:, 5, g:g + 1], in0=st[:, 0, g:g + 1], scalar=SCALE, in1=sink,
                                              op0=ALU.mult, op1=ALU.max))
                dve.tensor_scalar(st[:, 1, g:g + 1], st[:, 5, g:g + 1], -1.0, None, ALU.mult
                                  ).then_inc(s("as_nmax"), 1)
                dve.tensor_tensor(st[:, 2, g:g + 1], sink, st[:, 5, g:g + 1], ALU.subtract
                                  ).then_inc(s("as_dsink"), 1)
            for g in range(2):
                e = prob[0][:, g, 0:AKEYS]
                dve.wait_ge(s("as_exp"), 2 * g + 2)
                link(dve.tensor_tensor(st[:, 6, g:g + 1], st[:, 3, g:g + 1], st[:, 4, g:g + 1], ALU.add))
                link(dve.reciprocal(st[:, 7, g:g + 1], st[:, 6, g:g + 1]))
                dve.tensor_scalar(e, e, st[:, 7, g:g + 1], None, ALU.mult).then_inc(s("as_prob"), 1)

            dve.wait_ge(s("as_out"), 2)
            with dve.Fori(0, PAIRS) as p:
                dve.wait_ge(s("b_kh"), p + 1)
                dve.tensor_tensor(kl[:], U[:, bass.ds(C_KB + p, 1), :], as_f32(kh[:]), ALU.subtract
                                  ).then_inc(s("b_kl"), 1)
                dve.wait_ge(s("b_qh"), p + 1)
                dve.scalar_tensor_tensor(out=ql[:], in0=U[:, bass.ds(C_QB + p, 1), 0:SEQ], scalar=SCALE,
                                         in1=as_f32(qh[:]), op0=ALU.mult, op1=ALU.subtract
                                         ).then_inc(s("b_ql"), 1)

                def cap_of(n):
                    a, c, t = STEPS[n]
                    M, q0, _ = step_shape(c, t)
                    if n >= 2:
                        dve.wait_ge(s("b_soft"), NSTEP * p + n - 1)
                    dve.wait_ge(s("b_z"), NSTEP * p + n + 1)
                    dve.tensor_scalar(capped[n % 2][0:M, q0:QCH], ps[0:M, n % 4, q0:QCH], ZCAP, None, ALU.min
                                      ).then_inc(s("b_cap"), 1)

                def drain_of(n):
                    a, c, _ = STEPS[n]
                    rows = slice(HD * a, HD * a + HD)
                    dve.wait_ge(s("b_pv"), NSTEP * p + n + 2)
                    dve.tensor_scalar(U[rows, bass.ds(C_QB + p, 1), QCH * c:QCH * c + QCH], ps[rows, 4 + c, :],
                                      1.0, None, ALU.mult).then_inc(s("b_omain"), 1)

                cap_of(0)
                for n in range(NSTEP):
                    a, c, t = STEPS[n]
                    M, q0, _ = step_shape(c, t)
                    if n + 1 < NSTEP:
                        cap_of(n + 1)
                    dve.wait_ge(s("b_ln"), NSTEP * p + n + 1)
                    if n >= 2:
                        dve.wait_ge(s("b_arg"), NSTEP * p + n - 1)
                        dve.wait_ge(s("b_later"), NLATER * p + LATER_BEFORE[n - 1])
                    dve.tensor_tensor(soft[n % 2][0:M, q0:QCH], capped[n % 2][0:M, q0:QCH],
                                      ps[0:M, n % 4, q0:QCH], ALU.max).then_inc(s("b_soft"), 1)
                    if n >= 2 and STEPS[n - 2][2] < 0:
                        drain_of(n - 2)
                drain_of(NSTEP - 1)
            dve.tensor_scalar(qs[:], U[:, C_QB:C_QB + PAIRS, SAM:MET], SCALE, None, ALU.mult
                              ).then_inc(s("s_q"), 1)
            dve.memset(later_s[:], 0.0).then_inc(s("s_zeroed"), 1)
            dve.wait_ge(s("s_zeroed"), 1)
            for n, (M, kt, vt) in enumerate(SAMPLE_TILES):
                dve.wait_ge(s("s_z"), n + 1)
                dve.tensor_scalar(halves(capped_s[0:M, :]), ps[0:M, s_bank(n):s_bank(n) + 2, 0:P], ZCAP, None,
                                  ALU.min).then_inc(s("s_cap"), 1)
                dve.wait_ge(s("s_ln"), n + 1)
                dve.tensor_tensor(halves(soft_s[0:M, :]), halves(capped_s[0:M, :]),
                                  ps[0:M, s_bank(n):s_bank(n) + 2, 0:P], ALU.max).then_inc(s("s_soft"), 1)
                if n < 3:
                    dve.wait_ge(s("s_arg"), n + 1)
                    dve.wait_ge(s("s_soft"), n + 1)
                    dve.tensor_tensor(later_s[0:M, :], later_s[0:M, :], soft_s[0:M, :], ALU.add
                                      ).then_inc(s("s_later"), 1)
                    dve.wait_ge(s("s_later"), n + 1)


            for hi, lo, c in ((oa_hi, oa_lo, C_QA), (ob_hi, ob_lo, C_QB)):
                dve.wait_ge(s("oa_hi"), 1 if c == C_QA else 2)
                dve.tensor_tensor(lo[:, :, 0:LIVE], U[:, c:c + 4, 0:LIVE], as_f32(hi[:, :, 0:LIVE]), ALU.subtract
                                  ).then_inc(s("oa_split"), 1)
            def rest_mix(i, n):
                dve.wait_ge(s("g_hi"), 3 * i + (n + 1))
                dve.tensor_tensor(glo[n][:], graw[n][:], as_f32(ghi[n][:]), ALU.subtract).then_inc(s("g_split"), 1)

            def mix_of(i, odd, last):
                for j in range(3):
                    bank = (odd + j) % 2
                    if j == 2 and not last:
                        rest_mix(i + 1, 0)
                    dve.wait_ge(s("m_out"), 3 * i + (j + 1))
                    dve.wait_ge(s("sig"), 6 * i + (2 * j + 2))
                    dve.tensor_tensor(mixa[:], sig[bank][0][:], ps[:, 4 * bank + 2, 0:TW], ALU.mult
                                      ).then_inc(s("m_a"), 1)
                    dve.tensor_tensor(mixb[:], sig[bank][1][:], ps[:, 4 * bank + 3, 0:TW], ALU.mult
                                      ).then_inc(s("m_read"), 1)
                    dve.wait_ge(s("m_a"), 3 * i + (j + 1))
                    dve.wait_ge(s("m_read"), 3 * i + (j + 3))
                    dve.tensor_tensor(mT[:, bass.ds(i, 1), TW * j:TW * j + TW], mixa[:], mixb[:], ALU.add
                                      ).then_inc(s("m_out"), 1)
                if not last:
                    rest_mix(i + 1, 1)
                    rest_mix(i + 1, 2)

            for n in range(3):
                rest_mix(0, n)
            with dve.Fori(0, KD // 2 - 1) as i:
                mix_of(2 * i, 0, False)
                mix_of(2 * i + 1, 1, False)
            mix_of(KD - 2, 0, False)
            mix_of(KD - 1, 1, True)

            dve.wait_ge(s("m_out"), 3 * KD + 1)
            link(dve.memset(rt[:], -3e38))
            link(dve.memset(seen[:], 0.0))
            link(dve.memset(onehot[:], 0.0))

            def ms_rest(t):
                M, n = rows_of(t), t % 2
                dve.wait_ge(s("ms_hi"), t + 1)
                dve.tensor_tensor(ms_lo[n][:, :, 0:M], mT[:, :, P * t:P * t + M], as_f32(ms_hi[n][:, :, 0:M]),
                                  ALU.subtract).then_inc(s("ms_split"), 1)

            normed = [0]

            def norm(M, x, out, gain, shift):
                for c in range(2):
                    link(dve.bn_stats(bn[0:M, c, :], x[:, 512 * c:512 * c + 512]))
                link(dve.bn_aggr(mv[0:M, 0:2], bn[0:M].rearrange("p c k -> p (c k)")))
                dve.tensor_scalar(mv[0:M, 2:3], mv[0:M, 1:2], EPS, None, ALU.add).then_inc(s("var_out"), 1)
                normed[0] += 1
                dve.wait_ge(s("rstd"), normed[0])
                link(dve.tensor_scalar(x, x, mv[0:M, 0:1], mv[0:M, 3:4], ALU.subtract, ALU.mult))
                link(dve.tensor_tensor(x, x, gain[0:M, :], ALU.mult))
                return dve.tensor_tensor(out, x, shift[0:M, :], ALU.add)

            def norm1(t):
                M, n = rows_of(t), t % 2
                h = hkeep[0:M, t, :]
                dve.wait_ge(s("o_mm"), t + 1)
                dve.wait_ge(s(f"xn_in{n}"), 16 * (t // 2) + 16)
                dve.scalar_tensor_tensor(out=halves(h), in0=halves(xn[n][0:M, :]), scalar=ALPHA,
                                         in1=ps[0:M, 2 * n:2 * n + 2, :], op0=ALU.mult, op1=ALU.add
                                         ).then_inc(s("r_added"), 1)
                dve.wait_ge(s("r_added"), t + 1)
                norm(M, h, h, g1, b1).then_inc(s("h_done"), 1)

            def route(t):
                M = rows_of(t)
                dve.wait_ge(s("r_mm"), t + 1)
                link(dve.tensor_tensor(col(M, 0, 0, NG), ps[0:M, 6, 0:NG], rbias[0:M, 0:NG], ALU.add))
                dve.tensor_tensor(el[0:M].rearrange("p g e -> p (g e)"), ps[0:M, 6, NG:NR], rbias[0:M, NG:NR],
                                  ALU.add).then_inc(s("r_read"), 1)
                link(dve.max(col(M, 1, 0, 8), col(M, 0, 0, 8)))
                link(dve.max_index(gi[0:M, :], col(M, 1, 0, 8), col(M, 0, 0, 8)))
                dve.tensor_scalar(col(M, 3, 0, 1), col(M, 1, 0, 1), -1.0, None, ALU.mult).then_inc(s("r_nmax"), 1)
                link(dve.tensor_copy(col(M, 2, 0, 1), gi[0:M, 0:1]))
                link(dve.tensor_scalar(col(M, 8, 0, NG), iota[0:M, 0:NG], col(M, 2, 0, 1), None, ALU.is_equal))
                dve.wait_ge(s("r_read"), t + 1)
                link(dve.tensor_tensor(elm[0:M], el[0:M],
                                       col(M, 8, 0, NG).rearrange("p (g o) -> p g o", o=1).to_broadcast([M, NG, EPG]),
                                       ALU.mult))
                link(dve.tensor_reduce(col(M, 9, 0, EPG), elm[0:M].rearrange("p g e -> p e g"), AX.X, ALU.add))
                link(dve.max(col(M, 10, 0, 8), col(M, 9, 0, 8)))
                link(dve.max_index(ei[0:M, :], col(M, 10, 0, 8), col(M, 9, 0, 8)))
                dve.tensor_tensor(col(M, 6, 0, 1), col(M, 10, 1, 2), col(M, 10, 0, 1), ALU.subtract
                                  ).then_inc(s("r_gap"), 1)
                link(dve.tensor_copy(col(M, 11, 0, 2), ei[0:M, 0:2]))
                link(dve.tensor_scalar(col(M, 12, 0, 1), col(M, 2, 0, 1), float(EPG), None, ALU.mult))
                link(dve.tensor_scalar(exk[0:M, t, :], col(M, 11, 0, 2), col(M, 12, 0, 1), None, ALU.add))
                for k in range(2):
                    link(dve.tensor_scalar(onehot[0:M, t, k, :], iota[0:M, 0:NE], exk[0:M, t, k:k + 1], None,
                                           ALU.is_equal))
                if t:
                    place(t - 1)
                dve.tensor_tensor(chosen[0:M, :], onehot[0:M, t, 0, :], onehot[0:M, t, 1, :], ALU.add
                                  ).then_inc(s("r_chosen"), 1)
                dve.wait_ge(s("r_exp"), 2 * t + 2)
                link(dve.tensor_scalar(col(M, 13, 0, 1), col(M, 7, 0, 1), 1.0, None, ALU.add))
                link(dve.tensor_tensor(col(M, 13, 1, 2), col(M, 13, 0, 1), col(M, 5, 0, 1), ALU.mult))
                link(dve.reciprocal(prow[0:M, t, 0:1], col(M, 13, 1, 2)))
                link(dve.tensor_tensor(prow[0:M, t, 1:2], prow[0:M, t, 0:1], col(M, 7, 0, 1), ALU.mult))

            def place(t):
                M = rows_of(t)
                dve.wait_ge(s("r_chosen"), t + 1)
                dve.wait_ge(s("r_pos"), t + 1)
                link(dve.tensor_tensor(posx[0:M], onehot[0:M, t],
                                       ps[0:M, 7, 0:NE].rearrange("p (o e) -> p o e", o=1).to_broadcast([M, 2, NE]),
                                       ALU.mult))
                link(dve.tensor_reduce(loc[0:M, t, :], posx[0:M], AX.X, ALU.add))
                dve.scalar_tensor_tensor(out=vdest[0:M, t, :], in0=exk[0:M, t, :], scalar=float(VROWS),
                                         in1=loc[0:M, t, :], op0=ALU.mult, op1=ALU.add).then_inc(s("r_dest"), 1)
                dve.tensor_tensor(seen[0:M, :], seen[0:M, :], chosen[0:M, :], ALU.add).then_inc(s("r_seen"), 1)
                dve.wait_ge(s("r_seen"), t + 1)

            ms_rest(0)
            for k in range(KD):
                dve.wait_ge(s("o_hi"), k + 1)
                dve.tensor_tensor(olo[:, k, :], oraw[:, k, :], as_f32(ohi[:, k, :]), ALU.subtract
                                  ).then_inc(s("o_split"), 1)
            for t in range(NTL):
                if t + 1 < NTL:
                    ms_rest(t + 1)
                if t == 0:
                    dve.wait_ge(s("ln_in"), 16 * 6)
                norm1(t)
                if t:
                    route(t - 1)
            route(NTL - 1)
            place(NTL - 1)

            dve.wait_ge(s("r_count"), 1)
            link(dve.tensor_scalar(cnt_i[:], ps[:, 0, 0:NE], float(P - 1), None, ALU.add))
            link(dve.tensor_scalar(cnt_i[:], cnt_i[:], 7, None, ALU.arith_shift_right))
            link(dve.tensor_copy(nblk[:], cnt_i[:]))
            link(dve.tensor_scalar(nblk[:], nblk[:], 1.0, None, ALU.max))
            link(dve.tensor_copy(cum[0][:], nblk[:]))
            a, d = 0, 1
            while d < NE:
                link(dve.tensor_tensor(cum[1 - a][:, d:], cum[a][:, d:], cum[a][:, :NE - d], ALU.add))
                link(dve.tensor_copy(cum[1 - a][:, :d], cum[a][:, :d]))
                a, d = 1 - a, 2 * d
            total = cum[a]
            NB1 = MAXBLK + 1
            cells = cmp[0:1, 0:NB1 * NE].rearrange("p (b e) -> p b e", e=NE)
            link(dve.tensor_tensor(cells, total[0:1, :].rearrange("p (o e) -> p o e", o=1).to_broadcast([1, NB1, NE]),
                                   iota[0:1, :].rearrange("p (b o) -> p b o", o=1).to_broadcast([1, NB1, NE]),
                                   ALU.is_le))
            link(dve.tensor_reduce(blk[:, 0, :], cells, AX.X, ALU.add))
            link(dve.tensor_tensor(cells, cells,
                                   nblk[0:1, :].rearrange("p (o e) -> p o e", o=1).to_broadcast([1, NB1, NE]),
                                   ALU.mult))
            link(dve.tensor_reduce(blk[:, 1, :], cells, AX.X, ALU.add))
            link(dve.tensor_scalar(blk[:, 0, :], blk[:, 0, :], float(NE - 1), None, ALU.min))
            link(dve.tensor_tensor(blk[:, 2, :], iota[0:1, :], blk[:, 1, :], ALU.subtract))
            link(dve.scalar_tensor_tensor(out=blk[:, 3, :], in0=blk[:, 0, :], scalar=float(NTL),
                                          in1=blk[:, 2, :], op0=ALU.mult, op1=ALU.add))
            dve.tensor_copy(blk_i[:, 0, :], blk[:, 0, :]).then_inc(s("plan"), 1)
            dve.tensor_scalar(blk_i[:, 1, :], blk[:, 3, :], float(NE * NTL - 1), None, ALU.min
                              ).then_inc(s("plan"), 1)
            dve.tensor_scalar(last_blk[:], total[0:1, :], -1.0, None, ALU.add).then_inc(s("plan"), 1)
            dve.wait_ge(s("tab_in"), 16)
            dve.tensor_copy(tab_f[:], tab_i[:]).then_inc(s("tokens"), 1)
            dve.wait_ge(s("tab_tr"), 1)
            dve.tensor_copy(tokens[:], ps[:, 1, 0:NE * NTL]).then_inc(s("tokens"), 1)
            link(dve.tensor_tensor(first_row[:], total[:], nblk[:], ALU.subtract))
            link(dve.tensor_scalar(first_row[:], first_row[:], float(P), None, ALU.mult))
            own = cmp[:, 0:NTL * 2 * NE].rearrange("p (a e) -> p a e", e=NE)
            dve.wait_ge(s("plan"), 3)
            link(dve.tensor_tensor(own, onehot[:].rearrange("p t k e -> p (t k) e"),
                                   first_row[:].rearrange("p (o e) -> p o e", o=1).to_broadcast([P, 2 * NTL, NE]),
                                   ALU.mult))
            link(dve.tensor_reduce(yfirst[:], own, AX.X, ALU.add))
            for t in range(NTL):
                M = rows_of(t)
                link(dve.tensor_tensor(ydest[0:M, t, :], yfirst[0:M, 2 * t:2 * t + 2], loc[0:M, t, :], ALU.add))
            dve.tensor_copy(ydest_done[:], total[:, 0:1]).then_inc(s("ydest"), 1)

            def rest_third(n, e):
                for q in range(3):
                    dve.wait_ge(s("e_hi"), 12 * e + (4 * n + q + 1))
                    c = slice(PIECE * q, PIECE * q + PIECE)
                    dve.tensor_tensor(e_lo[n][:, c], e_raw[n][:, c], as_f32(e_hi[n][:, c]), ALU.subtract
                                      ).then_inc(s("e_split"), 1)

            def hidden(half, b, first):
                dve.wait_ge(s("silu"), 2 * b + (half + 1))
                if not first:
                    dve.wait_ge(s("hb_tr"), 2 * (b - 1) + (half + 1))
                c = slice(HH * half, HH * half + HH)
                dve.tensor_tensor(hid[:, c], sg[:, c], ps[:, half, HH:2 * HH], ALU.mult
                                  ).then_inc(s("hid"), 1)

            def rest_x(b):
                for c in range(2):
                    dve.wait_ge(s("xb_hi"), 2 * b + (c + 1))
                    dve.tensor_tensor(xb_lo[:, 4 * c:4 * c + 4, :], ps[:, 2 + c, :].rearrange("p (k m) -> p k m", k=4),
                                      as_f32(xb_hi[:, 4 * c:4 * c + 4, :]), ALU.subtract
                                      ).then_inc(s("xb_split"), 1)

            def rest_h(half, b):
                dve.wait_ge(s("hb_hi"), 2 * b + (half + 1))
                dve.tensor_tensor(hb_lo[:, 2 * half:2 * half + 2, :],
                                  ps[:, 4, HH * half:HH * half + HH].rearrange("p (k m) -> p k m", k=2),
                                  as_f32(hb_hi[:, 2 * half:2 * half + 2, :]), ALU.subtract
                                  ).then_inc(s("hb_split"), 1)

            def new_expert(b, e, first):
                rest_third(0, e)
                rest_third(1, e)
                hidden(0, b, first)
                rest_third(2, e)
                hidden(1, b, first)
                rest_h(0, b)
                rest_x(b + 1)
                rest_h(1, b)

            def more_blocks(e, b):
                last = dve.value_load(last_blk[0:1, bass.ds(e, 1)], min_val=0, max_val=MAXBLK - 1)
                with dve.If(last > b):
                    with dve.Fori(b + 1, last + 1) as more:
                        hidden(0, more, False)
                        hidden(1, more, False)
                        rest_h(0, more)
                        rest_x(more + 1)
                        rest_h(1, more)

            rest_x(0)
            new_expert(0, 0, True)
            more_blocks(0, 0)
            with dve.Fori(1, NE) as e:
                b = dve.value_load(last_blk[0:1, bass.ds(e - 1, 1)], min_val=0, max_val=MAXBLK - 2) + 1
                new_expert(b, e, False)
                more_blocks(e, b)
            for t in range(NTL):
                M, n = rows_of(t), t % 2
                f = yg[n][0][0:M, :]
                dve.wait_ge(s("c_scaled"), t + 1)
                link(dve.scalar_tensor_tensor(out=f, in0=yg[n][1][0:M, :], scalar=prow[0:M, t, 1:2], in1=f,
                                              op0=ALU.mult, op1=ALU.add))
                link(dve.scalar_tensor_tensor(out=f, in0=hkeep[0:M, t, :], scalar=ALPHA, in1=f, op0=ALU.mult,
                                              op1=ALU.add))
                if t >= 2:
                    dve.wait_ge(s(f"y_out{n}"), 16 * (t // 2))
                norm(M, f, on[n][0:M, :], g2, b2).then_inc(s("out_done"), 1)

        @block.gpsimd
        def _(pool):
            pool.wait_ge(s("rope_done"), 3 * NROPE)
            pool.wait_ge(s("va_out"), 4)
            pool.tensor_copy(qas_s[:], U[:, C_QA:C_QA + 4, SAM:MET]).then_inc(s("as_staged"), 1)
            pool.tensor_copy(vas[:, 1, :], van[:, 0, :])
            pool.tensor_copy(kas[:, P:2 * P], U[:, C_KA, 0:P])
            pool.tensor_copy(qas[:], U[:, C_QA:C_QA + 4, 0:P]).then_inc(s("a_staged"), 1)
            with pool.Fori(1, NT) as i:
                pool.wait_ge(s("a_mixed"), PAIRS * i)
                pool.tensor_copy(vas[:], van[:, bass.ds(i - 1, 2), :])
                pool.tensor_copy(kas[:], U[:, C_KA, bass.ds(P * (i - 1), 2 * P)])
                pool.tensor_copy(qas[:], U[:, C_QA:C_QA + 4, bass.ds(P * i, P)]).then_inc(s("a_staged"), 1)
            pool.wait_ge(s("as_out"), 2)
            with pool.Fori(0, PAIRS) as p:
                pool.wait_ge(s("b_vtr2"), p + 1)
                pool.tensor_copy(vts[:], U[:, bass.ds(C_VB + p, 1), :]).then_inc(s("b_vstaged"), 1)
                for n in range(NSTEP):
                    a, c, t = STEPS[n]
                    M, q0, first = step_shape(c, t)
                    if t < 0:
                        continue
                    pool.wait_ge(s("b_arg"), NSTEP * p + n + 1)
                    pool.wait_ge(s("b_soft"), NSTEP * p + n + 1)
                    cols = slice(q0, QCH)
                    if first:
                        pool.tensor_tensor(later[:, cols], soft[n % 2][:, cols],
                                           zero.to_broadcast([P, QCH - q0]), ALU.add).then_inc(s("b_later"), 1)
                        pool.memset(later[:, 0:q0], 0.0).then_inc(s("b_zeroed"), 1)
                    else:
                        pool.wait_ge(s("b_later"), NLATER * p + LATER_BEFORE[n])
                        pool.wait_ge(s("b_zeroed"), 4 * p + (2 * a + c + 1))
                        pool.tensor_tensor(later[:, cols], later[:, cols], soft[n % 2][:, cols], ALU.add
                                           ).then_inc(s("b_later"), 1)

            pool.wait_ge(s("w_used2"), KD)
            pool.memset(zeros_i[:], 0).then_inc(s("zeros"), 1)
            pool.tensor_copy(tokid[:], const[:, K_TOK:K_TOK + NTL]).then_inc(s("pool_step"), 1)
            pool.wait_ge(s("pool_step"), 1)
            pool.wait_ge(s("stored"), 16 * 5)

            def rstd(n, M):
                pool.wait_ge(s("var_out"), n + 1)
                pool.tensor_tensor(mv[0:M, 3:4], mv[0:M, 2:3], const[0:M, K_HALF:K_HALF + 1], ALU.pow
                                   ).then_inc(s("rstd"), 1)

            def enter(t):
                M = rows_of(t)
                pool.wait_ge(s("r_dest"), t + 1)
                for k in range(2):
                    pool.indirect_dma_start(
                        out=tok_table, out_offset=bass.IndirectOffsetOnAxis(ap=vdest[0:M, t, k:k + 1], axis=0),
                        in_=tokid[0:M, t:t + 1], in_offset=None).then_inc(s("table_in"), 16)

            for t in range(NTL):
                rstd(t, rows_of(t))
                if t >= 2:
                    enter(t - 2)
            enter(NTL - 2)
            enter(NTL - 1)
            pool.wait_ge(s("table_in"), 16 * 2 * NTL)
            pool.dma_start(tab_i[:], tok_table.rearrange("(g r p) o -> r g (p o)", g=3, p=P)).then_inc(s("tab_in"), 16)
            pool.wait_ge(s("rows_out"), 16 * NTL)
            pool.wait_ge(s("plan"), 3)
            pool.wait_ge(s("ydest"), 1)

            def step(count):
                pool.wait_ge(s("pool_step"), count)
                pool.tensor_tensor(tick[:], zero[0:1, :], zero[0:1, :], ALU.add).then_inc(s("pool_step"), 1)

            def fetch(b, first):
                column = pool.value_load(blk_i[0:1, 1, bass.ds(b, 1)], min_val=0, max_val=NE * NTL - 1)
                if not first:
                    pool.wait_ge(s("x_got"), 16 * b)
                    pool.wait_ge(s("xb_tr"), b)
                    step(2 * b)
                pool.tensor_copy(idx[:], tokens[:, bass.ds(column, 1)]).then_inc(s("idx_set"), 1)
                pool.wait_ge(s("idx_set"), b + 1)
                step(2 * b + 1)
                pool.indirect_dma_start(out=xg[:], out_offset=None, in_=h_rows,
                                        in_offset=bass.IndirectOffsetOnAxis(ap=idx[:, 0:1], axis=0)
                                        ).then_inc(s("x_got"), 16)

            def rest_last(n, e):
                pool.wait_ge(s("e_hi"), 12 * e + (4 * n + 4))
                c = slice(3 * PIECE, 4 * PIECE)
                pool.tensor_tensor(e_lo[n][:, c], e_raw[n][:, c], as_f32(e_hi[n][:, c]), ALU.subtract
                                   ).then_inc(s("e_split3"), 1)

            def more_blocks(e, b):
                last = pool.value_load(last_blk[0:1, bass.ds(e, 1)], min_val=0, max_val=MAXBLK - 1)
                with pool.If(last > b):
                    with pool.Fori(b + 1, last + 1) as more:
                        fetch(more + 1, False)

            pool.wait_ge(s("tokens"), 2)
            fetch(0, True)
            for n in range(3):
                rest_last(n, 0)
            fetch(1, False)
            more_blocks(0, 0)
            with pool.Fori(1, NE) as e:
                b = pool.value_load(last_blk[0:1, bass.ds(e - 1, 1)], min_val=0, max_val=MAXBLK - 2) + 1
                fetch(b + 1, False)
                rest_last(0, e)
                rest_last(1, e)
                rest_last(2, e)
                more_blocks(e, b)
            nb = pool.value_load(last_blk[0:1, NE - 1:NE], min_val=NE - 1, max_val=MAXBLK - 1) + 1
            pool.wait_ge(s("rows_out"), 16 * NTL + 16 * nb)
            step(2 * nb + 2)

            def collect(t):
                M, n = rows_of(t), t % 2
                if t >= 2:
                    pool.wait_ge(s("out_done"), t - 1)
                for k in range(2):
                    pool.indirect_dma_start(
                        out=yg[n][k][0:M, :], out_offset=None, in_=y_rows,
                        in_offset=bass.IndirectOffsetOnAxis(ap=ydest[0:M, t, k:k + 1], axis=0)
                    ).then_inc(s(f"y_got{n}"), 16)

            collect(0)
            collect(1)
            for t in range(NTL):
                rstd(NTL + t, rows_of(t))
                if t + 2 < NTL:
                    collect(t + 2)


def constants(np):
    i = np.arange(P)
    rot = np.zeros((P, P), np.float32)
    for h in range(0, P, HD):
        for d in range(HD // 2):
            rot[h + d + HD // 2, h + d] = -1.0
            rot[h + d, h + d + HD // 2] = 1.0
    band = np.zeros((P, BAND), np.float32)
    band[P // 2:, META:META + P // 2] = NEG
    band[:P // 2, META + P + P // 2:] = NEG
    smask = np.zeros((P, NH, DEC), np.float32)
    smask[:DEC] = np.where(i[:DEC, None] >= i[None, :DEC], np.float32(NEG), np.float32(0))[:, None, :]
    cols = [np.eye(P), -1.0 * (i[:, None] >= i), -np.ones((P, P)), i[:, None] < i, np.ones((P, P)),
            np.where(i[:, None] >= i, NEG, 0.0), rot, band, smask.reshape(P, -1),
            np.broadcast_to(np.arange(MAXBLK + 1), (P, MAXBLK + 1)), P * np.arange(NTL)[None] + i[:, None],
            np.full((P, 1), -0.5)]
    const = np.concatenate([np.asarray(c, np.float32) for c in cols], axis=1)
    pos = np.concatenate([np.arange(SEQ) + META, np.arange(DEC) + META + PAST, np.arange(META)]).astype(np.float32)
    inv = np.float32(10000.0) ** (-np.arange(HD // 2, dtype=np.float32) * np.float32(2.0) / np.float32(HD))
    ang = (pos[None, :] * inv.astype(np.float32)[:, None]).astype(np.float32)
    ang = np.tile(ang, (P // (HD // 2), 1))
    return const, np.cos(ang), np.sin(ang)


def lay_out(np, x):
    a = {k: np.asarray(v) for k, v in x.items()}
    const, cos, sin = constants(np)
    d = {"const": const, "cos": cos, "sin": sin}
    tok = np.concatenate([a["x_prompt"][0], a["x_sample"][0], a["meta_tokens"]])
    d["xT"] = tok.T.reshape(KD, P, TOK).transpose(1, 0, 2)
    w = a["w_in"][0]
    q = w[:, :NH * HD].reshape(D, 2, 4, HD).transpose(0, 2, 1, 3).reshape(D, NH * HD)
    gates = NH * HD + 2 * P + 3 * NH * HD
    u = np.concatenate([q, w[:, NH * HD:gates]], axis=1)
    d["w_u"] = u.reshape(KD, P, NCH, P).transpose(2, 1, 0, 3)
    d["sinks"] = a["attn_sinks"][0]
    d["ck_a"] = a["cache_a_k"][0, 0].reshape(AWIN, P).T
    d["cv_a"] = a["cache_a_v"][0, 0].reshape(AWIN, P)
    d["ck_b"] = a["cache_b_k"][0, 0].reshape(PAST, PAIRS, P).transpose(2, 1, 0)
    d["cv_b"] = a["cache_b_v"][0, 0].reshape(2, P, PAIRS * P).transpose(1, 0, 2)
    def tiles(m):
        return m.reshape(-1, P, KD, P).transpose(2, 1, 0, 3)

    ga, gb = w[:, gates:gates + D], w[:, gates + D:]
    woa = a["w_oa"][0].reshape(2, 4, HD, D).transpose(1, 0, 2, 3).reshape(NH * HD, D)
    d["w_mix"] = np.stack([tiles(ga), tiles(gb), np.concatenate([tiles(woa), tiles(a["w_ob"][0])], axis=2)], axis=1)
    d["w_out"] = a["w_out"][0].reshape(KD, P, D)
    d["x_nat"] = np.concatenate([a["x_prompt"][0], a["x_sample"][0]])
    for k in ("ln1_g", "ln1_b", "ln2_g", "ln2_b"):
        d[k] = a[k][0]
    d["w_r"] = np.concatenate([a["w_router_group"][0], a["w_router_expert"][0]], axis=1
                              ).reshape(KD, P, NR).transpose(1, 0, 2)
    d["b_r"] = np.concatenate([a["b_router_group"][0], a["b_router_expert"][0]])
    gu = np.stack([a["w_gate"][0], a["w_up"][0]]).reshape(2, NE, KD, P, 2, HH)
    moe = np.empty((NE, 3, P, GC), np.float32)
    moe[:, 0:2] = gu.transpose(1, 4, 3, 2, 0, 5).reshape(NE, 2, P, GC)
    moe[:, 2] = a["w_down"][0].reshape(NE, 4, P, D).transpose(0, 2, 1, 3).reshape(NE, P, GC)
    d["w_moe"] = moe
    return {k: np.ascontiguousarray(v) for k, v in d.items()}


_OUTS = {"kat": (P, AWIN + DEC), "vat": (P, AWIN + DEC), "kvb": (P, 2 * PAIRS, LIVE), "y": (LIVE, D)}


def kernel(**inputs):
    import numpy as np
    import concourse.bacc as bacc
    from concourse.bass_utils import run_bass_kernel_spmd as run

    nc = bacc.Bacc("TRN2", target_bir_lowering=False, num_devices=1)
    arrays = lay_out(np, inputs)
    io = {k: nc.dram_tensor(k, v.shape, mybir.dt.from_np(v.dtype), kind="ExternalInput").ap()
          for k, v in arrays.items()}
    for k, shape in _OUTS.items():
        io[k] = nc.dram_tensor(k, shape, F32, kind="ExternalOutput").ap()
    build(nc, io)
    r = run(nc, [arrays], core_ids=[0]).results[0]
    kv_a = [r[k].T.reshape(1, 1, AWIN + DEC, 2, HD) for k in ("kat", "vat")]
    kv_b = r["kvb"].transpose(2, 1, 0).reshape(1, 1, LIVE, 2, NH, HD)
    kv_b = [kv_b[:, :, :, n] for n in range(2)]
    out = [r["y"][None, :SEQ], r["y"][None, SEQ:]]
    out += [x[:, :, :AWIN] for x in kv_a] + [x[:, :, :SEQ] for x in kv_b]
    out += [x[:, :, AWIN:] for x in kv_a] + [x[:, :, SEQ:] for x in kv_b]
    return tuple(np.ascontiguousarray(x) for x in out)
```

```python
from contextlib import ExitStack

import concourse.bass as bass
from concourse import mybir

ALU = mybir.AluOpType
ACT = mybir.ActivationFunctionType
AX = mybir.AxisListType
F32 = mybir.dt.float32
F32R = mybir.dt.float32r
I32 = mybir.dt.int32
U32 = mybir.dt.uint32

P = 128
D = 1024
SEQ, DEC, META, PAST = 1024, 32, 16, 256
TOK = SEQ + DEC + META
LIVE = SEQ + DEC
SAM, MET = SEQ, SEQ + DEC
KD = D // P
HD = 64
NH = 8
PAIRS = NH // 2
NT = SEQ // P
AWIN = 128
NE, NG, EPG = 32, 4, 8
DE = 512
MAXBLK = NE + 2 * LIVE // P
ALPHA = 2.0 ** 0.25
EPS = 1e-5
NEG = -1e30
SCALE = HD ** -0.5
ZCAP = 40.0

C_QA, C_KA, C_VA, C_QB, C_KB, C_VB = 0, 4, 5, 6, 10, 14
NCH = 18
NROPE = C_VA
TCUT = (0, 358, 716, 1072)
TW = LIVE // 3
BAND = META + 2 * P
AKEYS = DEC + AWIN + META
QCH = 512

STEPS = [(a, c, t) for a in range(2) for c in range(2) for t in [*range(4 * c + 3, -1, -1), -1]]
NSTEP = len(STEPS)
LATER_BEFORE = [sum(x[2] >= 0 for x in STEPS[:n]) for n in range(NSTEP + 1)]
NLATER = LATER_BEFORE[NSTEP]
AHEAD = 3


def step_shape(c, t):
    return (META if t < 0 else P), max(P * t - QCH * c, 0), t == 4 * c + 3


def s_bank(n):
    return 2 * (n % 2)


SAMPLE_TILES = [(DEC, slice(SAM, MET), None), (P, slice(P, PAST), 1), (P, slice(0, P), 0),
                (META, slice(MET, TOK), None)]

NTL = NT + 1
NR = NG + NE
VROWS = NTL * P
GC = KD * DE
SILU_SET = "silu_and_others"
TABR = NE * NTL // 3
PIECE = GC // 4
YB = 5
HH = DE // 2

K_IDENT, K_NTRI, K_NONES, K_SUP, K_ONES, K_MASK, K_ROT = (P * n for n in range(7))
K_BAND = 7 * P
K_SMASK = K_BAND + BAND
K_IOTA = K_SMASK + NH * DEC
K_TOK = K_IOTA + MAXBLK + 1
K_HALF = K_TOK + NTL
K_N = K_HALF + 1


def rows_of(t):
    return P if t < NT else DEC


def build(nc, io):
    with ExitStack() as ctx:
        def sem(name):
            return ctx.enter_context(nc.semaphore(name))

        limit = nc.sbuf_usable_end
        tok_table = nc.dram_tensor("tok_table", [NE * VROWS, 1], I32, kind="Internal").ap()
        h_rows = nc.dram_tensor("h_rows", [LIVE, D], F32, kind="Internal").ap()
        y_rows = nc.dram_tensor("y_rows", [MAXBLK * P, D], F32, kind="Internal").ap()

        class Region:
            def __init__(self, base):
                self.at = base

            def take(self, name, shape, dt=F32):
                n = 4
                for k in shape[1:]:
                    n *= k
                t = nc.alloc_sbuf_tensor_at(name, shape, dt, offset=self.at)
                self.at += (n + 31) // 32 * 32
                assert self.at <= limit, (name, self.at, limit)
                return t

            def split(self, name, shape):
                hi = self.take(name + "_hi", shape, F32R)
                raw = nc.alloc_sbuf_tensor_at(name + "_raw", shape, F32, offset=self.at)
                return raw, hi, self.take(name + "_lo", shape, F32R)

        ps = ctx.enter_context(nc.psum_tensor("ps", [P, 8, 512], F32))

        keep = Region((nc.sbuf_base + 31) // 32 * 32)
        const = keep.take("const", [P, K_N])
        ident, ntri, nones, sup, ones, blkmask, rot = (const[:, k:k + P] for k in range(0, 7 * P, P))
        amask = const[:, K_BAND:K_BAND + BAND]
        zero = const[:, K_BAND:K_BAND + 1]
        smask = const[0:DEC, K_SMASK:K_SMASK + NH * DEC]
        iota = const[:, K_IOTA:K_IOTA + MAXBLK + 1]
        sinks = keep.take("sinks", [P, NH])
        sinks_s = keep.take("sinks_s", [P, 2])
        base = keep.at

        r = Region(base)
        xraw, xh, xl = r.split("xT", [P, KD, TOK])
        U = r.take("U", [P, NCH, TOK])
        work = r.at
        r = Region(work)
        wraw, whi, wlo = zip(*[r.split(f"win{n}", [P, KD, P]) for n in range(2)])
        cos = r.take("cos", [P, TOK])
        sin = r.take("sin", [P, TOK])
        ropet = [r.take(f"ropet{n}", [P, 360]) for n in range(3)]
        r = Region(work)
        van = r.take("van", [P, NT, P])
        van_m = r.take("van_m", [META, P])
        van_s = r.take("van_s", [DEC, P])
        qas = [r.take(f"qas{n}", [P, 4, P]) for n in range(2)]
        kas = [r.take(f"kas{n}", [P, 2 * P]) for n in range(2)]
        qas_s = r.take("qas_s", [P, 4, DEC])
        vas = [r.take(f"vas{n}", [P, 2, P]) for n in range(2)]
        msk = [r.take(f"msk{n}", [P, 2, BAND]) for n in range(2)]
        prob = [r.take(f"prob{n}", [P, 2, BAND]) for n in range(2)]
        pts = r.take("pts", [P, 512])
        ptms = r.take("ptms", [META, 2 * P])
        stat = [r.take(f"stat{n}", [P, 8, 2]) for n in range(2)]
        ck_a = r.take("ck_a", [P, AWIN])
        cv_a = r.take("cv_a", [P, P])
        r = Region(work)
        kh = r.take("kh", [P, TOK], F32R)
        kl = r.take("kl", [P, TOK], F32R)
        qh = r.take("qh", [P, SEQ], F32R)
        ql = r.take("ql", [P, SEQ], F32R)
        vts = r.take("vts", [P, TOK])
        vn = r.take("vn", [P, NT, P])
        vn_m = r.take("vn_m", [META, P])
        scratch = r.at
        capped = [r.take(f"capped{n}", [P, QCH]) for n in range(2)]
        soft = [r.take(f"soft{n}", [P, QCH]) for n in range(3)]
        soft_hi = [r.take(f"soft_hi{n}", [P, QCH], F32R) for n in range(2)]
        soft_lo = [r.take(f"soft_lo{n}", [P, QCH], F32R) for n in range(2)]
        a_keys = Region(work - (NCH - C_KA) * TOK * 4)
        soft_hi.append(a_keys.take("soft_hi2", [P, QCH], F32R))
        soft_lo.append(a_keys.take("soft_lo2", [P, QCH], F32R))
        wgt = [r.take(f"wgt{n}", [P, QCH]) for n in range(2)]
        later = [r.take(f"later{n}", [P, QCH]) for n in range(2)]
        ident_r, mask_r, ntri_r = (r.take(f"{n}_r", [P, P], F32R) for n in ("ident", "mask", "ntri"))
        vall_m = r.take("vall_m", [META, PAIRS, P])
        vall_s = r.take("vall_s", [DEC, PAIRS, P])
        SQ = NH * DEC
        ck_b = nc.alloc_sbuf_tensor_at("ck_b", [P, PAIRS, PAST], F32, offset=work)
        r = Region(scratch)
        capped_s = r.take("capped_s", [P, SQ])
        soft_s = r.take("soft_s", [P, SQ])
        wgt_s = r.take("wgt_s", [P, SQ])
        later_s = r.take("later_s", [P, SQ])
        qs = r.take("qs", [P, PAIRS, DEC])

        def u_at(c):
            return nc_u + c * TOK * 4
        nc_u = work - NCH * TOK * 4
        cv_b = nc.alloc_sbuf_tensor_at("cv_b", [P, 2, PAIRS * P], F32, offset=u_at(C_VA))
        oa_lo = nc.alloc_sbuf_tensor_at("oa_lo", [P, 4, TOK], F32R, offset=u_at(C_QA))
        ob_lo = nc.alloc_sbuf_tensor_at("ob_lo", [P, 4, TOK], F32R, offset=u_at(C_QB))
        oa_hi = nc.alloc_sbuf_tensor_at("oa_hi", [P, 4, TOK], F32R, offset=u_at(C_KB))
        ob_hi = nc.alloc_sbuf_tensor_at("ob_hi", [P, 4, TOK], F32R, offset=u_at(C_VB))
        r = Region(u_at(C_KA))
        sig = [[r.take(f"sig{n}{w}", [P, TW]) for w in "ab"] for n in range(2)]
        mixa = r.take("mixa", [P, TW])
        mixb = r.take("mixb", [P, TW])
        assert r.at <= u_at(C_QB)
        r = Region(work)
        mT = r.take("mT", [P, KD, LIVE])
        after_m = r.at
        graw, ghi, glo = zip(*[r.split(f"wmix{n}", [P, KD, P]) for n in range(3)])
        r = Region(base)
        oraw, ohi, olo = r.split("wout", [P, KD, D])
        assert r.at <= nc_u
        r = Region(nc_u)
        hkeep = r.take("hkeep", [P, NTL, D])
        moe_small = r.at
        ms_hi = [r.take(f"ms_hi{n}", [P, KD, P], F32R) for n in range(2)]
        ms_lo = [r.take(f"ms_lo{n}", [P, KD, P], F32R) for n in range(2)]
        xn = [r.take(f"xn{n}", [P, D]) for n in range(2)]
        hT = r.take("hT", [P, KD, P])
        g1 = r.take("g1", [P, D])
        assert r.at <= work
        tab_i = r.take("tab_i", [TABR, 3, P], I32)
        tab_f = r.take("tab_f", [TABR, 3, P])
        tokens = r.take("tokens", [P, NE * NTL], I32)
        assert r.at <= work
        r = Region(after_m)
        b1 = r.take("b1", [P, D])
        g2 = r.take("g2", [P, D])
        b2 = r.take("b2", [P, D])
        wr = r.take("wr", [P, KD, NR])
        rbias = r.take("rbias", [P, NR])
        bn = r.take("bn", [P, 2, 6])
        mv = [r.take(f"mv{n}", [P, 6]) for n in range(2)]
        rt = r.take("rt", [P, 16 * 8])
        el = r.take("el", [P, NG, EPG])
        elm = r.take("elm", [P, NG, EPG])
        gi = r.take("gi", [P, 8], U32)
        ei = r.take("ei", [P, 8], U32)
        onehot = r.take("onehot", [P, NTL, 2, NE])
        chosen = r.take("chosen", [P, NE])
        seen = r.take("seen", [P, NE])
        posx = r.take("posx", [P, 2, NE])
        exk = r.take("exk", [P, NTL, 2])
        loc = r.take("loc", [P, NTL, 2])
        prow = r.take("prow", [P, NTL, 2])
        vdest = r.take("vdest", [P, NTL, 2], I32)
        tokid = r.take("tokid", [P, NTL], I32)
        zeros_i = r.take("zeros_i", [P, NE * VROWS // P], I32)
        cnt_i = r.take("cnt_i", [P, NE], I32)
        nblk = r.take("nblk", [P, NE])
        cum = [r.take(f"cum{n}", [P, NE]) for n in range(2)]
        first_row = r.take("first_row", [P, NE])
        blk = r.take("blk", [1, 4, MAXBLK + 1])
        blk_i = r.take("blk_i", [1, 2, MAXBLK + 1], I32)
        last_blk = r.take("last_blk", [1, NE], I32)
        yfirst = r.take("yfirst", [P, 2 * NTL])
        ydest_done = r.take("ydest_done", [P, 1])
        ydest = r.take("ydest", [P, NTL, 2], I32)
        scratch_end = r.at
        r = Region(base)
        e_raw, e_hi, e_lo = map(list, zip(*[r.split(f"we{n}", [P, GC]) for n in range(2)]))
        assert r.at <= nc_u
        r = Region(work)
        for lst, ten in zip((e_raw, e_hi, e_lo), r.split("we2", [P, GC])):
            lst.append(ten)
        assert r.at <= after_m
        r = Region(moe_small)
        xg = r.take("xg", [P, D])
        xb_hi = r.take("xb_hi", [P, KD, P], F32R)
        xb_lo = r.take("xb_lo", [P, KD, P], F32R)
        sg = r.take("sg", [P, DE])
        hid = r.take("hid", [P, DE])
        hb_hi = r.take("hb_hi", [P, 4, P], F32R)
        hb_lo = r.take("hb_lo", [P, 4, P], F32R)
        yb = r.take("yb", [P, D])
        assert r.at <= work - 2 * 4096 - 64
        idx = nc.alloc_sbuf_tensor_at("idx", [P, 1], I32, offset=scratch_end)
        tick = nc.alloc_sbuf_tensor_at("tick", [1, 1], F32, offset=scratch_end + 32)
        assert scratch_end + 64 <= limit
        cmp = nc.alloc_sbuf_tensor_at("cmp", [P, NTL * 2 * NE * 3], F32, offset=r.at)
        r = Region(base)
        yg = [[r.take(f"yg{n}{k}", [P, D]) for k in range(2)] for n in range(YB)]
        on = [r.take(f"on{n}", [P, D]) for n in range(2)]

        sems = {}

        def s(name):
            if name not in sems:
                sems[name] = sem(name)
            return sems[name]

        E_IN = [("g_in0", "w_in0"), ("g_in1", "w_in1"), ("g_in2", "g_in3")]
        E_IN_BEFORE = [(16 * KD, 16 * (NCH // 2)), (16 * KD, 16 * (NCH // 2)), (16 * KD, 0)]

        block = ctx.enter_context(nc.Block())

        def col(M, n, a, b):
            return rt[0:M, 8 * n + a:8 * n + b]

        def halves(t):
            return t.rearrange("p (a c) -> p a c", a=2)

        def as_f32(t):
            return t.bitcast(F32)

        @block.sync
        def _(sp):
            for k in range(KD):
                sp.dma_start(xraw[:, k, :], io["xT"][:, k, :]).then_inc(s(f"k_in{k}"), 16)
                if k < 2:
                    sp.dma_start(wraw[k][:], io["w_u"][k]).then_inc(s(f"w_in{k}"), 16)
            sp.dma_start(const[:], io["const"]).then_inc(s("const_in"), 16)
            sp.dma_start(cos[:], io["cos"]).then_inc(s("const_in"), 16)
            sp.dma_start(sin[:], io["sin"]).then_inc(s("const_in"), 16)
            sp.dma_start(sinks[:], io["sinks"].partition_broadcast(P)).then_inc(s("const_in"), 16)
            for g in range(2):
                for h in range(4):
                    sp.dma_start(sinks_s[DEC * h:DEC * h + DEC, g:g + 1],
                                 io["sinks"][4 * g + h:4 * g + h + 1].partition_broadcast(DEC)
                                 ).then_inc(s("const_in"), 16)
            with sp.Fori(1, NCH // 2) as i:
                for n in range(2):
                    sp.wait_ge(s("u_mm"), 2 * (i - 1) + (n + 1))
                    sp.dma_start(wraw[n][:], io["w_u"][bass.ds(2 * i + n, 1)].rearrange("a p k c -> (a p) k c")
                                 ).then_inc(s(f"w_in{n}"), 16)
            sp.wait_ge(s("u_out"), NCH)
            sp.dma_start(io["vat"], U[:, C_VA, SEQ - AWIN:MET]).then_inc(s("stored"), 16)
            sp.dma_start(io["kvb"], U[:, C_KB:NCH, 0:MET]).then_inc(s("stored"), 16)
            sp.wait_ge(s("rope_done"), 3 * NROPE)
            sp.dma_start(io["kat"], U[:, C_KA, SEQ - AWIN:MET]).then_inc(s("stored"), 16)
            sp.dma_start(y_rows[NE * P:MAXBLK * P, :].rearrange("(b p) d -> p b d", p=P),
                         U[:, C_KB:C_KB + 1, 0:D].to_broadcast([P, MAXBLK - NE, D])).then_inc(s("stored"), 16)
            sp.wait_ge(s("a_staged"), 1)
            sp.dma_start(ck_a[:], io["ck_a"]).then_inc(s("cache_in"), 16)
            sp.dma_start(cv_a[:], io["cv_a"]).then_inc(s("cache_in"), 16)
            sp.wait_ge(s("stored"), 16 * 4)
            sp.wait_ge(s("cache_in"), 16 * 2)
            sp.dma_start(cv_b[:], io["cv_b"]).then_inc(s("cache_in"), 16)
            sp.wait_ge(s("b_z"), NSTEP * PAIRS)
            sp.dma_start(ck_b[:], io["ck_b"]).then_inc(s("cache_in"), 16)
            sp.wait_ge(s("s_out"), 2)
            for n in range(3):
                sp.dma_start(graw[n][:], io["w_mix"][0, n]).then_inc(s(f"g_in{n}"), 16)
            with sp.Fori(1, KD) as i:
                for n in range(3):
                    sp.wait_ge(s(f"w_used{n}"), i)
                    sp.dma_start(graw[n][:], io["w_mix"][bass.ds(i, 1), n].rearrange("a p k c -> (a p) k c")
                                 ).then_inc(s(f"g_in{n}"), 16)
            for n in range(3):
                sp.wait_ge(s(f"w_used{n}"), KD)
            sp.wait_ge(s("m_out"), 3 * KD + 1)
            for k in range(KD):
                sp.dma_start(oraw[:, k, :], io["w_out"][k]).then_inc(s(f"k_in{k}"), 16)
                if k == 0:
                    for n in range(2):
                        sp.dma_start(xn[n][:], io["x_nat"][P * n:P * n + P, :]).then_inc(s(f"xn_in{n}"), 16)
                    for dst, src in ((g1, "ln1_g"), (b1, "ln1_b"), (g2, "ln2_g"), (b2, "ln2_b"), (rbias, "b_r")):
                        sp.dma_start(dst[:], io[src].partition_broadcast(P)).then_inc(s("ln_in"), 16)
                    sp.dma_start(wr[:], io["w_r"]).then_inc(s("ln_in"), 16)
            sp.wait_ge(s("zeros"), 1)
            sp.dma_start(tok_table.rearrange("(p c) o -> p (c o)", p=P), zeros_i[:]).then_inc(s("stored"), 16)
            for t in range(NTL):
                M = rows_of(t)
                sp.wait_ge(s("h_done"), t + 1)
                sp.dma_start(h_rows[P * t:P * t + M, :], hkeep[0:M, t, :]).then_inc(s("rows_out"), 16)
                if t + 2 < NTL:
                    M2 = rows_of(t + 2)
                    sp.dma_start(xn[t % 2][0:M2, :], io["x_nat"][P * (t + 2):P * (t + 2) + M2, :]
                                 ).then_inc(s(f"xn_in{t % 2}"), 16)

            def load_piece(e, n, q):
                c = slice(2 * PIECE * q, 2 * PIECE * q + 2 * PIECE)
                src = io["w_moe"][bass.ds(e, 1), n, :, c].rearrange("a p c -> (a p) c")
                sp.dma_start(e_raw[n][:, c], src).then_inc(s(E_IN[n][q]), 16)

            sp.wait_ge(s("ms_hi"), NTL)
            sp.wait_ge(s("ms_split"), NTL)
            for q in range(2):
                load_piece(0, 2, q)
            sp.wait_ge(s("o_mm"), NTL)
            for n in range(2):
                for q in range(2):
                    load_piece(0, n, q)
            sp.wait_ge(s("plan"), 3)
            with sp.Fori(1, NE) as e:
                b = sp.value_load(last_blk[0:1, bass.ds(e - 1, 1)], min_val=0, max_val=MAXBLK - 2) + 1
                for n in range(3):
                    for q in range(2):
                        sp.wait_ge(s(f"w_used{n}"), KD - 1 + q + 2 * b)
                        load_piece(e, n, q)
            for t in range(NTL):
                M = rows_of(t)
                sp.wait_ge(s("out_done"), t + 1)
                sp.dma_start(io["y"][P * t:P * t + M, :], on[t % 2][0:M, :]).then_inc(s(f"y_out{t % 2}"), 16)
            sp.wait_ge(s("stored"), 16 * 5)
            sp.wait_ge(s("y_out0"), 16 * ((NTL + 1) // 2))
            sp.wait_ge(s("y_out1"), 16 * (NTL // 2))

        @block.tensor
        def _(pe):
            def project(i, first, rope=None):
                for n in range(2):
                    pe.wait_ge(s("w_split"), 2 * i + (n + 1))
                    if not first:
                        pe.wait_ge(s("u_out"), 2 * (i - 1) + (n + 1))
                    for k in range(KD):
                        if first and n == 0:
                            pe.wait_ge(s("x_split"), k + 1)
                        for c in range(3):
                            a, b = TCUT[c], TCUT[c + 1]
                            o = ps[:, 3 * n + c, 0:b - a]
                            pe.matmul(o, whi[n][:, k, :], xh[:, k, a:b], start=k == 0, stop=False)
                            pe.matmul(o, whi[n][:, k, :], xl[:, k, a:b], start=False, stop=False)
                            last = pe.matmul(o, wlo[n][:, k, :], xh[:, k, a:b], start=False, stop=k == KD - 1)
                    last.then_inc(s("u_mm"), 1)
                    if n == 0 and rope is not None:
                        for j in range(3):
                            a, b = TCUT[j], TCUT[j + 1]
                            if j != 1:
                                pe.wait_ge(s("rope_sin"), 3 * rope + (j + 1 if j == 0 else 2))
                            pe.matmul(ps[:, 6 + j % 2, 0:b - a], rot, U[:, bass.ds(rope, 1), a:b].rearrange(
                                "p o c -> p (o c)"), start=True, stop=True).then_inc(s("rope_swap"), 1)

            project(0, True)
            with pe.Fori(1, NCH // 2 - NROPE) as i:
                project(i, False)
            pe.wait_ge(s("const_in"), 16 * 12)
            with pe.Fori(0, NROPE) as c:
                project(c + (NCH // 2 - NROPE), False, c)
            pe.wait_ge(s("u_out"), NCH)
            for t in range(NT):
                last = pe.transpose(ps[:, 2 + t // 4, P * (t % 4):P * (t % 4) + P], U[:, C_VA, P * t:P * t + P], ident)
                if t < 2:
                    last.then_inc(s("b_vtr2" if t else "b_pv"), 1)
            pe.transpose(ps[0:DEC, 4, 0:P], U[:, C_VA, SAM:MET], ident)
            pe.transpose(ps[0:META, 5, 0:P], U[:, C_VA, MET:TOK], ident).then_inc(s("va_tr"), 1)

            def a_scores(m, u, odd, peeled):
                if not (peeled and m < 2):
                    pe.wait_ge(s("a_masked"), u - 1)
                for g in range(2):
                    rows = slice(HD * g, HD * g + HD)
                    bank = ps[:, 2 * (m % 2) + g, :]
                    q = qas[odd][rows, m, :]
                    pe.matmul(bank[:, 0:META], q, U[rows, C_KA, MET:TOK], start=True, stop=True)
                    if peeled:
                        last = pe.matmul(bank[:, META + P:BAND], q, kas[odd][rows, P:2 * P], start=True, stop=True)
                    else:
                        last = pe.matmul(bank[:, META:BAND], q, kas[odd][rows, :], start=True, stop=True)
                last.then_inc(s("a_scored"), 1)

            def a_turn(m, u):
                pe.wait_ge(s("a_prob"), 2 * u + 2)
                for g in range(2):
                    e = prob[m % 2][:, g, :]
                    pe.transpose(ps[:, 4, 2 * P * g:2 * P * g + P], e[:, META:META + P], ident)
                    pe.transpose(ps[:, 4, 2 * P * g + P:2 * P * g + 2 * P], e[:, META + P:BAND], ident)
                    last = pe.transpose(ps[0:META, 5, P * g:P * g + P], e[:, 0:META], ident)
                last.then_inc(s("a_turned"), 1)

            def a_values(m, u, odd, peeled):
                pe.wait_ge(s("a_pt"), u + 1)
                pe.wait_ge(s("a_ptm"), u + 1)
                if not (peeled and m == 0):
                    pe.wait_ge(s("a_out"), u)
                for g in range(2):
                    rows = slice(HD * g, HD * g + HD)
                    o = ps[rows, 6, 0:P]
                    if not peeled:
                        pe.matmul(o, vas[odd][:, 0, rows], pts[:, 2 * P * g:2 * P * g + P], start=True, stop=False)
                    pe.matmul(o, vas[odd][:, 1, rows], pts[:, 2 * P * g + P:2 * P * g + 2 * P], start=peeled,
                              stop=False)
                    last = pe.matmul(o, van_m[:, rows], ptms[:, P * g:P * g + P], start=False, stop=True)
                last.then_inc(s("a_mixed"), 1)

            def a_tile(i, odd, peeled, last):
                for m in range(PAIRS):
                    u = PAIRS * i + m
                    a_turn(m, u)
                    if m < 2:
                        a_scores(m + 2, u + 2, odd, peeled)
                    elif not last:
                        if m == 2:
                            pe.wait_ge(s("a_staged"), i + 2)
                        a_scores(m - 2, u + 2, 1 - odd, False)
                    a_values(m, u, odd, peeled)

            pe.wait_ge(s("rope_done"), 3 * NROPE)
            pe.wait_ge(s("a_staged"), 1)
            pe.wait_ge(s("va_out"), 4)
            a_scores(0, 0, 0, True)
            a_scores(1, 1, 0, True)
            a_tile(0, 0, True, False)
            with pe.Fori(0, NT // 2 - 1) as i:
                a_tile(2 * i + 1, 1, False, False)
                a_tile(2 * i + 2, 0, False, False)
            a_tile(NT - 1, 1, False, True)
            NU = NT * PAIRS
            pe.wait_ge(s("cache_in"), 16 * 2)
            pe.wait_ge(s("as_staged"), 1)
            pe.wait_ge(s("a_masked"), NU)
            for g in range(2):
                rows = slice(HD * g, HD * g + HD)
                q = qas_s[rows].rearrange("p h q -> p (h q)")
                o = ps[:, g, :]
                pe.matmul(o[:, 0:DEC], q, U[rows, C_KA, SAM:MET], start=True, stop=True)
                pe.matmul(o[:, DEC:DEC + AWIN], q, ck_a[rows, :], start=True, stop=True)
                pe.matmul(o[:, DEC + AWIN:AKEYS], q, U[rows, C_KA, MET:TOK], start=True, stop=True
                          ).then_inc(s("as_scored"), 1)
            pe.wait_ge(s("a_out"), NU)
            for g in range(2):
                rows = slice(HD * g, HD * g + HD)
                pe.wait_ge(s("as_prob"), g + 1)
                if g:
                    pe.wait_ge(s("as_pt"), 3)
                e = prob[0][:, g, :]
                pe.transpose(ps[0:DEC, 4, 0:P], e[:, 0:DEC], ident)
                pe.transpose(ps[:, 4, P:2 * P], e[:, DEC:DEC + AWIN], ident)
                pe.transpose(ps[0:META, 4, 2 * P:3 * P], e[:, DEC + AWIN:AKEYS], ident).then_inc(s("as_turned"), 1)
                pe.wait_ge(s("as_pt"), 3 * g + 3)
                o = ps[rows, 6, 0:P]
                pe.matmul(o, van_s[:, rows], pts[0:DEC, 0:P], start=True, stop=False)
                pe.matmul(o, cv_a[:, rows], pts[:, P:2 * P], start=False, stop=False)
                pe.matmul(o, van_m[:, rows], pts[0:META, 2 * P:3 * P], start=False, stop=True
                          ).then_inc(s("as_mixed"), 1)

            pe.wait_ge(s("as_out"), 2)
            pe.wait_ge(s("b_vstaged"), 1)
            with pe.Fori(0, PAIRS) as p:
                def turn_values():
                    pe.wait_ge(s("b_vstaged"), p + 2)
                    for t in range(NT):
                        pe.transpose(ps[:, 6 + t // 4, P * (t % 4):P * (t % 4) + P], vts[:, P * t:P * t + P], ident
                                     ).then_inc(s("b_vtr"), 1)
                    pe.wait_ge(s("b_vn"), 5 * p + 2)
                    pe.transpose(ps[0:META, 6, 0:P], vts[:, MET:TOK], ident)
                    pe.transpose(ps[0:DEC, 7, 0:P], vts[:, SAM:MET], ident).then_inc(s("b_vtr2"), 1)

                def z_of(n):
                    a, c, t = STEPS[n]
                    rows = slice(HD * a, HD * a + HD)
                    M, q0, _ = step_shape(c, t)
                    o = ps[0:M, n % 4, q0:QCH]
                    keys = slice(P * t, P * t + P) if t >= 0 else slice(MET, TOK)
                    cols = slice(QCH * c + q0, QCH * c + QCH)
                    pe.matmul(o, kh[rows, keys], qh[rows, cols], start=True, stop=False, skip_group_check=True)
                    pe.matmul(o, kh[rows, keys], ql[rows, cols], start=False, stop=False, skip_group_check=True)
                    last = pe.matmul(o, kl[rows, keys], qh[rows, cols], start=False, stop=False,
                                     skip_group_check=True)
                    if t >= 4 * c:
                        last = pe.matmul(ps[:, n % 4, q0:q0 + P], ident_r[:], mask_r[:], start=False, stop=False,
                                         skip_group_check=True)
                    last.then_inc(s("b_z"), 1)

                def arg_of(n):
                    a, c, t = STEPS[n]
                    M, q0, first = step_shape(c, t)
                    o = ps[0:M, n % 4, q0:QCH]
                    def own():
                        for x in (soft_hi, soft_lo):
                            last = pe.matmul(o, ntri_r[0:M, 0:M], x[n % 3][0:M, q0:QCH], start=False,
                                             stop=(first or t < 0) and x is soft_lo, skip_group_check=True)
                        return last

                    pe.wait_ge(s("b_lo"), NSTEP * p + n + 1)
                    if t >= 0:
                        last = own()
                    if not first:
                        pe.wait_ge(s("b_later"), NLATER * p + LATER_BEFORE[n])
                        pe.wait_ge(s("b_zeroed"), 4 * p + (2 * a + c + 1))
                        last = pe.matmul(o, nones[:, 0:M], later[LATER_BEFORE[n] % 2][:, q0:QCH], start=False,
                                         stop=t >= 0, skip_group_check=True)
                    if t < 0:
                        last = own()
                    last.then_inc(s("b_arg"), 1)

                def values_of(n):
                    a, c, t = STEPS[n]
                    rows = slice(HD * a, HD * a + HD)
                    M, q0, first = step_shape(c, t)
                    group = 2 * a + c
                    if first:
                        pe.wait_ge(s("b_omain"), 4 * p + max(group, 1))
                    if n == 0:
                        pe.wait_ge(s("b_vn"), 5 * p + 5)
                    pe.wait_ge(s("b_w"), NSTEP * p + n + 1)
                    v = vn[:, t, rows] if t >= 0 else vn_m[:, rows]
                    last = pe.matmul(ps[rows, 4 + group % 2, q0:QCH], v, wgt[n % 2][0:M, q0:QCH],
                                     start=first, stop=t < 0, skip_group_check=True)
                    last.then_inc(s("b_pv"), 1)

                pe.wait_ge(s("b_lokq"), 2 * p + 2)
                for n in range(AHEAD):
                    z_of(n)
                turn_values()
                for n in range(NSTEP):
                    arg_of(n)
                    if n:
                        values_of(n - 1)
                    if n + AHEAD < NSTEP:
                        z_of(n + AHEAD)
                values_of(NSTEP - 1)

            pe.wait_ge(s("cache_in"), 16 * 4)
            pe.wait_ge(s("s_q"), 1)
            pe.wait_ge(s("b_omain"), 4 * PAIRS + 1)
            def s_z(n):
                M, kt, _ = SAMPLE_TILES[n]
                for h in range(NH):
                    m, a = divmod(h, 2)
                    rows = slice(HD * a, HD * a + HD)
                    k = U[rows, C_KB + m, kt] if n in (0, 3) else ck_b[rows, m, kt]
                    last = pe.matmul(ps[0:M, s_bank(n) + a, DEC * m:DEC * m + DEC], k, qs[rows, m, :],
                                     start=m == 0, stop=False, skip_group_check=True)
                if n == 0:
                    for a in range(2):
                        last = pe.matmul(ps[0:M, a, 0:P], ident[0:M, 0:M], smask[:, P * a:P * a + P], start=False,
                                         stop=False, skip_group_check=True)
                last.then_inc(s("s_z"), 1)

            s_z(0)
            s_z(1)
            for n, (M, kt, vt) in enumerate(SAMPLE_TILES):
                if n:
                    pe.wait_ge(s("s_later"), n)
                pe.wait_ge(s("s_soft"), n + 1)
                for a in range(2):
                    o = ps[0:M, s_bank(n) + a, 0:P]
                    if n:
                        pe.matmul(o, nones[:, 0:M], later_s[:, P * a:P * a + P], start=False, stop=False,
                                  skip_group_check=True)
                    last = pe.matmul(o, ntri[0:M, 0:M], soft_s[0:M, P * a:P * a + P], start=False, stop=True,
                                     skip_group_check=True)
                last.then_inc(s("s_arg"), 1)
                pe.wait_ge(s("s_w"), n + 1)
                for h in range(NH):
                    m, a = divmod(h, 2)
                    rows = slice(HD * a, HD * a + HD)
                    v = (vall_s[:, m, rows] if n == 0 else vall_m[:, m, rows] if n == 3
                         else cv_b[:, vt, HD * h:HD * h + HD])
                    last = pe.matmul(ps[rows, 4 + a, DEC * m:DEC * m + DEC], v,
                                     wgt_s[0:M, P * a + DEC * m:P * a + DEC * m + DEC], start=n == 0 and m == 0,
                                     stop=n == 3, skip_group_check=True)
                last.then_inc(s("s_pv"), 1)
                if n < 2:
                    s_z(n + 2)

            def mix_thirds(i, odd):
                for j in range(3):
                    bank = 4 * ((odd + j) % 2)
                    cols = slice(TW * j, TW * j + TW)
                    for n in range(3):
                        if j == 0:
                            pe.wait_ge(s("g_split"), 3 * i + (n + 1))
                        if j == 0 and n == 2:
                            pe.wait_ge(s("oa_split"), 2)
                        if n == 0:
                            pe.wait_ge(s("m_read"), 3 * i + (j + 1))
                        for k in range(KD):
                            if n < 2:
                                o, hi, lo, first, end = ps[:, bank + n, 0:TW], xh[:, k, cols], xl[:, k, cols], \
                                    k == 0, k == KD - 1
                            else:
                                src = (oa_hi, oa_lo) if k < 4 else (ob_hi, ob_lo)
                                o, hi, lo = ps[:, bank + 2 + k // 4, 0:TW], src[0][:, k % 4, cols], \
                                    src[1][:, k % 4, cols]
                                first, end = k % 4 == 0, k % 4 == 3
                            pe.matmul(o, ghi[n][:, k, :], hi, start=first, stop=False)
                            pe.matmul(o, ghi[n][:, k, :], lo, start=False, stop=False)
                            last = pe.matmul(o, glo[n][:, k, :], hi, start=False, stop=end)
                        if j == 2:
                            last.then_inc(s(f"w_used{n}"), 1)
                        elif n == 2:
                            last.then_inc(s("m_mm"), 1)

            pe.wait_ge(s("s_out"), 2)
            with pe.Fori(0, KD // 2) as i:
                mix_thirds(2 * i, 0)
                mix_thirds(2 * i + 1, 1)

            def turn_rows(t):
                M = rows_of(t)
                pe.wait_ge(s("h_done"), t + 1)
                if t:
                    pe.wait_ge(s("hT_out"), 2 * t)
                for k in range(KD):
                    last = pe.transpose(ps[:, 4 + k // 4, P * (k % 4):P * (k % 4) + M],
                                        hkeep[0:M, t, P * k:P * k + P], ident[0:M, 0:M])
                last.then_inc(s("hT_tr"), 1)

            def route_logits(t):
                M = rows_of(t)
                pe.wait_ge(s("hT_out"), 2 * t + 2)
                if t:
                    pe.wait_ge(s("r_read"), t)
                for k in range(KD):
                    last = pe.matmul(ps[0:M, 6, 0:NR], hT[:, k, 0:M], wr[:, k, :], start=k == 0, stop=k == KD - 1)
                last.then_inc(s("r_mm"), 1)

            def route_places(t):
                M = rows_of(t)
                pe.wait_ge(s("r_chosen"), t + 1)
                if t:
                    pe.wait_ge(s("r_seen"), t)
                pe.matmul(ps[0:M, 7, 0:NE], sup[0:M, 0:M], chosen[0:M, :], start=True, stop=False)
                pe.matmul(ps[0:M, 7, 0:NE], ones[:, 0:M], seen[:], start=False, stop=True).then_inc(s("r_pos"), 1)

            pe.wait_ge(s("ln_in"), 16 * 6)
            pe.wait_ge(s("m_read"), 3 * KD + 2)
            for t in range(NTL):
                M, n = rows_of(t), t % 2
                pe.wait_ge(s("ms_split"), t + 1)
                if t >= 2:
                    pe.wait_ge(s("r_added"), t - 1)
                for k in range(KD):
                    if t == 0:
                        pe.wait_ge(s("o_split"), k + 1)
                    elif k == 7:
                        turn_rows(t - 1)
                    for c in range(2):
                        o, cols = ps[0:M, 2 * n + c, :], slice(512 * c, 512 * c + 512)
                        pe.matmul(o, ms_hi[n][:, k, 0:M], ohi[:, k, cols], start=k == 0, stop=False)
                        pe.matmul(o, ms_hi[n][:, k, 0:M], olo[:, k, cols], start=False, stop=False)
                        last = pe.matmul(o, ms_lo[n][:, k, 0:M], ohi[:, k, cols], start=False, stop=k == KD - 1)
                last.then_inc(s("o_mm"), 1)
                if t:
                    route_logits(t - 1)
                if t >= 2:
                    route_places(t - 2)
            turn_rows(NTL - 1)
            route_logits(NTL - 1)
            route_places(NTL - 2)
            route_places(NTL - 1)
            pe.wait_ge(s("r_seen"), NTL)
            pe.matmul(ps[:, 0, 0:NE], ones, seen[:], start=True, stop=True).then_inc(s("r_count"), 1)
            pe.wait_ge(s("tokens"), 1)
            for g in range(3):
                last = pe.transpose(ps[:, 1, TABR * g:TABR * g + TABR], tab_f[:, g, :], ident[0:TABR, 0:TABR])
            last.then_inc(s("tab_tr"), 1)

            def turn_x(b):
                pe.wait_ge(s("x_got"), 16 * b + 16)
                for k in range(KD):
                    last = pe.transpose(ps[:, 2 + k // 4, P * (k % 4):P * (k % 4) + P], xg[:, P * k:P * k + P], ident)
                last.then_inc(s("xb_tr"), 1)

            def turn_h(b, half):
                pe.wait_ge(s("hid"), 2 * b + (half + 1))
                for k in (2 * half, 2 * half + 1):
                    last = pe.transpose(ps[:, 4, P * k:P * k + P], hid[:, P * k:P * k + P], ident)
                last.then_inc(s("hb_tr"), 1)

            def block_mm(b, e, first):
                for half in range(2):
                    if not first:
                        pe.wait_ge(s("hid"), 2 * (b - 1) + (half + 1))
                    for k in range(KD):
                        if half == 0 and k == 0:
                            pe.wait_ge(s("xb_split"), 2 * b + 2)
                        if half == 1 and k == 5:
                            turn_h(b, 0)
                        if k % 2 == 0:
                            q = k // 2
                            if q < 3:
                                pe.wait_ge(s("e_split"), 9 * e + (3 * half + q + 1))
                            else:
                                pe.wait_ge(s("e_last_split"), 3 * e + (half + 1))
                        o, c = ps[:, half, :], slice(2 * HH * k, 2 * HH * k + 2 * HH)
                        pe.matmul(o, xb_hi[:, k, :], e_hi[half][:, c], start=k == 0, stop=False)
                        pe.matmul(o, xb_hi[:, k, :], e_lo[half][:, c], start=False, stop=False)
                        last = pe.matmul(o, xb_lo[:, k, :], e_hi[half][:, c], start=False, stop=k == KD - 1)
                        if k in (3, 7):
                            last.then_inc(s(f"w_used{half}"), 1)
                turn_x(b + 1)
                if not first:
                    pe.wait_ge(s("y_read"), 2 * b)
                for k in range(4):
                    if k == 1:
                        turn_h(b, 1)
                    if k % 2 == 0:
                        pe.wait_ge(s("hb_split"), 2 * b + (k // 2 + 1))
                    if k < 3:
                        pe.wait_ge(s("e_split"), 9 * e + (6 + k + 1))
                    else:
                        pe.wait_ge(s("e_last_split"), 3 * e + 3)
                    for c in range(2):
                        o, cols = ps[:, 5 + c, :], slice(D * k + 512 * c, D * k + 512 * c + 512)
                        pe.matmul(o, hb_hi[:, k, :], e_hi[2][:, cols], start=k == 0, stop=False)
                        pe.matmul(o, hb_hi[:, k, :], e_lo[2][:, cols], start=False, stop=False)
                        last = pe.matmul(o, hb_lo[:, k, :], e_hi[2][:, cols], start=False, stop=k == 3)
                    if k in (1, 3):
                        last.then_inc(s("w_used2"), 1)

            turn_x(0)
            block_mm(0, 0, True)
            pe.wait_ge(s("plan"), 3)
            nb = pe.value_load(last_blk[0:1, NE - 1:NE], min_val=NE - 1, max_val=MAXBLK - 1) + 1
            with pe.Fori(1, nb) as b:
                e = pe.value_load(blk_i[0:1, 0, bass.ds(b, 1)], min_val=0, max_val=NE - 1)
                block_mm(b, e, False)

        @block.scalar
        def _(act):
            act.preload_act_table_set("natural_log_exp_and_others")
            for k in range(KD):
                act.wait_ge(s(f"k_in{k}"), 16)
                act.activation(xh[:, k, :], xraw[:, k, :], ACT.Copy).then_inc(s("x_hi"), 1)
                if k < 2:
                    act.wait_ge(s(f"w_in{k}"), 16)
                    act.activation(whi[k][:], wraw[k][:], ACT.Copy).then_inc(s("w_hi"), 1)
            with act.Fori(0, NCH // 2) as i:
                for n in range(2):
                    act.wait_ge(s("u_mm"), 2 * i + (n + 1))
                    for c in range(3):
                        a, b = TCUT[c], TCUT[c + 1]
                        last = act.activation(U[:, bass.ds(2 * i + n, 1), a:b], ps[:, 3 * n + c, 0:b - a], ACT.Copy)
                    last.then_inc(s("u_out"), 1)
            act.wait_ge(s("va_tr"), 1)
            for j in range(2):
                act.activation(van[:, 4 * j:4 * j + 4, :], ps[:, 2 + j, :].rearrange("p (t c) -> p t c", t=4),
                               ACT.Copy).then_inc(s("va_out"), 1)
            act.activation(van_s[:], ps[0:DEC, 4, 0:P], ACT.Copy).then_inc(s("va_out"), 1)
            act.activation(van_m[:], ps[0:META, 5, 0:P], ACT.Copy).then_inc(s("va_out"), 1)

            def a_exp(m, u):
                st = stat[m % 2]
                act.wait_ge(s("a_nmax"), 2 * u + 1)
                for g in range(2):
                    act.activation(prob[m % 2][:, g, :], msk[m % 2][:, g, :], ACT.Exp, bias=st[:, 1, g:g + 1],
                                   scale=SCALE, accum_out=st[:, 3, g:g + 1]).then_inc(s("a_exp"), 1)
                act.wait_ge(s("a_nmax"), 2 * u + 2)
                act.activation(st[:, 4, :], st[:, 2, :], ACT.Exp).then_inc(s("a_exp"), 1)

            def a_tile(i, cols, last):
                for m in range(PAIRS):
                    u = PAIRS * i + m
                    act.wait_ge(s("a_turned"), u + 1)
                    act.activation(pts[:], ps[:, 4, :], ACT.Copy).then_inc(s("a_pt"), 1)
                    if m < 2 or not last:
                        a_exp((m + 2) % PAIRS, u + 2)
                    act.wait_ge(s("a_mixed"), u + 1)
                    act.activation(U[:, m, cols], ps[:, 6, 0:P], ACT.Copy).then_inc(s("a_out"), 1)

            a_exp(0, 0)
            a_exp(1, 1)
            a_tile(0, slice(0, P), False)
            with act.Fori(0, NT // 2 - 1) as i:
                for n in (1, 2):
                    a_tile(2 * i + n, bass.ds(2 * P * i + n * P, P), False)
            a_tile(NT - 1, slice(P * (NT - 1), SEQ), True)
            for g in range(2):
                st = stat[0]
                act.wait_ge(s("as_nmax"), g + 1)
                act.activation(prob[0][:, g, 0:AKEYS], msk[0][:, g, 0:AKEYS], ACT.Exp, bias=st[:, 1, g:g + 1],
                               scale=SCALE, accum_out=st[:, 3, g:g + 1]).then_inc(s("as_exp"), 1)
                act.wait_ge(s("as_dsink"), g + 1)
                act.activation(st[:, 4, g:g + 1], st[:, 2, g:g + 1], ACT.Exp).then_inc(s("as_exp"), 1)
            for g in range(2):
                rows = slice(HD * g, HD * g + HD)
                act.wait_ge(s("as_turned"), g + 1)
                if g:
                    act.wait_ge(s("as_mixed"), 1)
                act.activation(pts[0:DEC, 0:P], ps[0:DEC, 4, 0:P], ACT.Copy).then_inc(s("as_pt"), 1)
                act.activation(pts[:, P:2 * P], ps[:, 4, P:2 * P], ACT.Copy).then_inc(s("as_pt"), 1)
                act.activation(pts[0:META, 2 * P:3 * P], ps[0:META, 4, 2 * P:3 * P], ACT.Copy
                               ).then_inc(s("as_pt"), 1)
                act.wait_ge(s("as_mixed"), g + 1)
                act.activation(U[rows, 0:4, SAM:MET], ps[rows, 6, 0:P].rearrange("p (h q) -> p h q", h=4),
                               ACT.Copy).then_inc(s("as_out"), 1)

            act.wait_ge(s("as_out"), 2)
            act.wait_ge(s("stored"), 16 * 4)

            def stage_kq(p):
                act.activation(kh[:], U[:, bass.ds(C_KB + p, 1), :], ACT.Copy).then_inc(s("b_hikq"), 1)
                act.activation(qh[:], U[:, bass.ds(C_QB + p, 1), 0:SEQ], ACT.Copy, scale=SCALE
                               ).then_inc(s("b_hikq"), 1)

            stage_kq(0)
            with act.Fori(0, PAIRS) as p:
                def drain_values():
                    act.wait_ge(s("b_vtr"), NT * p + NT)
                    for j in range(2):
                        act.activation(vn[:, 4 * j:4 * j + 4, :], ps[:, 6 + j, :].rearrange("p (t c) -> p t c", t=4),
                                       ACT.Copy).then_inc(s("b_vn"), 1)
                    act.wait_ge(s("b_vtr2"), p + 2)
                    act.activation(vn_m[:], ps[0:META, 6, 0:P], ACT.Copy).then_inc(s("b_vn"), 1)
                    act.activation(vall_m[:, bass.ds(p, 1), :], ps[0:META, 6, 0:P], ACT.Copy).then_inc(s("b_vn"), 1)
                    act.activation(vall_s[:, bass.ds(p, 1), :], ps[0:DEC, 7, 0:P], ACT.Copy).then_inc(s("b_vn"), 1)

                def soft_of(n):
                    a, c, t = STEPS[n]
                    M, q0, _ = step_shape(c, t)
                    e = capped[n % 2][0:M, q0:QCH]
                    act.wait_ge(s("b_cap"), NSTEP * p + n + 1)
                    act.activation(e, e, ACT.Exp).then_inc(s("b_exp"), 1)
                    act.wait_ge(s("b_exp"), NSTEP * p + n + 1)
                    act.activation(e, e, ACT.Ln, bias=1.0).then_inc(s("b_ln"), 1)

                def round_of(n):
                    a, c, t = STEPS[n]
                    M, q0, _ = step_shape(c, t)
                    act.wait_ge(s("b_soft"), NSTEP * p + n + 1)
                    if n >= 3:
                        act.wait_ge(s("b_arg"), NSTEP * p + n - 2)
                    act.activation(soft_hi[n % 3][0:M, q0:QCH], soft[n % 3][0:M, q0:QCH], ACT.Copy
                                   ).then_inc(s("b_hi"), 1)

                def weight_of(n):
                    a, c, t = STEPS[n]
                    M, q0, _ = step_shape(c, t)
                    act.wait_ge(s("b_arg"), NSTEP * p + n + 1)
                    if n >= 2:
                        act.wait_ge(s("b_pv"), NSTEP * p + n)
                    act.activation(wgt[n % 2][0:M, q0:QCH], ps[0:M, n % 4, q0:QCH], ACT.Exp).then_inc(s("b_w"), 1)

                for n in range(-AHEAD, NSTEP):
                    if n >= 0:
                        weight_of(n)
                    if 0 <= n + 2 < NSTEP:
                        round_of(n + 2)
                    if n + AHEAD < NSTEP:
                        soft_of(n + AHEAD)
                    if n == -2:
                        drain_values()
                    if n == NSTEP - AHEAD:
                        with act.If(p < PAIRS - 1):
                            act.wait_ge(s("b_z"), NSTEP * p + NSTEP)
                            stage_kq(p + 1)
            for n, (M, kt, vt) in enumerate(SAMPLE_TILES):
                e = capped_s[0:M, :]
                act.wait_ge(s("s_cap"), n + 1)
                act.activation(e, e, ACT.Exp).then_inc(s("s_exp"), 1)
                act.wait_ge(s("s_exp"), n + 1)
                act.activation(e, e, ACT.Ln, bias=1.0).then_inc(s("s_ln"), 1)
                act.wait_ge(s("s_arg"), n + 1)
                if n:
                    act.wait_ge(s("s_pv"), n)
                act.activation(halves(wgt_s[0:M, :]), ps[0:M, s_bank(n):s_bank(n) + 2, 0:P], ACT.Exp
                               ).then_inc(s("s_w"), 1)
            act.wait_ge(s("s_pv"), 4)
            for a in range(2):
                rows = slice(HD * a, HD * a + HD)
                act.activation(U[rows, C_QB:C_QB + PAIRS, SAM:MET],
                               ps[rows, 4 + a, 0:PAIRS * DEC].rearrange("p (m q) -> p m q", m=PAIRS), ACT.Copy
                               ).then_inc(s("s_out"), 1)

            act.wait_ge(s("s_out"), 2)
            act.wait_ge(s("b_omain"), 4 * PAIRS + 1)
            act.wait_ge(s("stored"), 16 * 4)
            act.activation(oa_hi[:, :, 0:LIVE], U[:, C_QA:C_QA + 4, 0:LIVE], ACT.Copy).then_inc(s("oa_hi"), 1)
            act.preload_act_table_set("sigmoid_and_others")
            def round_mix(i, n):
                act.wait_ge(s(f"g_in{n}"), 16 * i + 16)
                act.activation(ghi[n][:], graw[n][:], ACT.Copy).then_inc(s("g_hi"), 1)

            def gate_thirds(i, odd, last):
                for j in range(3):
                    if j < 2:
                        act.wait_ge(s("m_mm"), 2 * i + (j + 1))
                    else:
                        if not last:
                            round_mix(i + 1, 0)
                        act.wait_ge(s("w_used2"), i + 1)
                    act.wait_ge(s("m_read"), 3 * i + (j + 1))
                    for w in range(2):
                        act.activation(sig[(odd + j) % 2][w][:], ps[:, 4 * ((odd + j) % 2) + w, 0:TW], ACT.Sigmoid
                                       ).then_inc(s("sig"), 1)
                if not last:
                    round_mix(i + 1, 1)
                    round_mix(i + 1, 2)

            round_mix(0, 0)
            round_mix(0, 1)
            act.activation(ob_hi[:, :, 0:LIVE], U[:, C_QB:C_QB + 4, 0:LIVE], ACT.Copy).then_inc(s("oa_hi"), 1)
            round_mix(0, 2)
            with act.Fori(0, KD // 2 - 1) as i:
                gate_thirds(2 * i, 0, False)
                gate_thirds(2 * i + 1, 1, False)
            gate_thirds(KD - 2, 0, False)
            gate_thirds(KD - 1, 1, True)
            def ms_round(t):
                M, n = rows_of(t), t % 2
                if t >= 2:
                    act.wait_ge(s("o_mm"), t - 1)
                act.activation(ms_hi[n][:, :, 0:M], mT[:, :, P * t:P * t + M], ACT.Copy).then_inc(s("ms_hi"), 1)

            def hT_drain(t):
                M = rows_of(t)
                act.wait_ge(s("hT_tr"), t + 1)
                if t:
                    act.wait_ge(s("r_mm"), t)
                for c in range(2):
                    act.activation(hT[:, 4 * c:4 * c + 4, 0:M],
                                   ps[:, 4 + c, :].rearrange("p (k m) -> p k m", k=4)[:, :, 0:M], ACT.Copy
                                   ).then_inc(s("hT_out"), 1)

            def normalise(n, M, x):
                act.wait_ge(s("rstd"), 2 * n + 2)
                act.activation(x, x, ACT.Identity, bias=mv[n % 2][0:M, 5:6], scale=mv[n % 2][0:M, 4:5]
                               ).then_inc(s("normed"), 1)

            def route_exp(t):
                M = rows_of(t)
                act.wait_ge(s("r_nmax"), t + 1)
                act.activation(col(M, 4, 0, 4), col(M, 0, 0, 4), ACT.Exp, bias=col(M, 3, 0, 1),
                               accum_out=col(M, 5, 0, 1)).then_inc(s("r_exp"), 1)
                act.wait_ge(s("r_gap"), t + 1)
                act.activation(col(M, 7, 0, 1), col(M, 6, 0, 1), ACT.Exp).then_inc(s("r_exp"), 1)

            act.wait_ge(s("m_out"), 3 * KD + 1)
            act.preload_act_table_set("exp_and_others")
            ms_round(0)
            for k in range(KD):
                act.wait_ge(s(f"k_in{k}"), 32)
                act.activation(ohi[:, k, :], oraw[:, k, :], ACT.Copy).then_inc(s("o_hi"), 1)
            for t in range(NTL):
                if t + 1 < NTL:
                    ms_round(t + 1)
                if t:
                    hT_drain(t - 1)
                normalise(t, rows_of(t), hkeep[0:rows_of(t), t, :])
                if t:
                    route_exp(t - 1)
            hT_drain(NTL - 1)
            route_exp(NTL - 1)

            def drain_y(done):
                act.wait_ge(s("w_used2"), KD + 2 * done)
                act.wait_ge(s("rows_out"), 16 * (NTL - 1) + 16 * done)
                for c in range(2):
                    act.activation(yb[:, 512 * c:512 * c + 512], ps[:, 5 + c, :], ACT.Copy).then_inc(s("y_read"), 1)
                act.wait_ge(s("y_read"), 2 * done)
                act.dma_start(y_rows[bass.ds(P * (done - 1), P), :], yb[:]).then_inc(s("rows_out"), 16)

            def round_third(n, e, pieces=range(4)):
                for q in pieces:
                    if q % 2 == 0:
                        act.wait_ge(s(E_IN[n][q // 2]), E_IN_BEFORE[n][q // 2] + 16 * e + 16)
                    c = slice(PIECE * q, PIECE * q + PIECE)
                    act.activation(e_hi[n][:, c], e_raw[n][:, c], ACT.Copy).then_inc(s("e_hi"), 1)

            def silu(half, b):
                act.wait_ge(s(f"w_used{half}"), KD + 2 + 2 * b)
                act.activation(sg[:, HH * half:HH * half + HH], ps[:, half, 0:HH], ACT.Silu
                               ).then_inc(s("silu"), 1)

            def round_x(b):
                act.wait_ge(s("xb_tr"), b + 1)
                for c in range(2):
                    act.activation(xb_hi[:, 4 * c:4 * c + 4, :], ps[:, 2 + c, :].rearrange("p (k m) -> p k m", k=4),
                                   ACT.Copy).then_inc(s("xb_hi"), 1)

            def round_h(half, b):
                act.wait_ge(s("hb_tr"), 2 * b + (half + 1))
                act.activation(hb_hi[:, 2 * half:2 * half + 2, :],
                               ps[:, 4, HH * half:HH * half + HH].rearrange("p (k m) -> p k m", k=2), ACT.Copy
                               ).then_inc(s("hb_hi"), 1)

            def new_expert(b, e, first):
                if not first:
                    round_third(0, e)
                    drain_y(b)
                    round_third(1, e)
                silu(0, b)
                if not first:
                    round_third(2, e, range(2))
                round_h(0, b)
                if not first:
                    round_third(2, e, range(2, 4))
                silu(1, b)
                round_x(b + 1)
                round_h(1, b)

            def more_blocks(e, b):
                last = act.value_load(last_blk[0:1, bass.ds(e, 1)], min_val=0, max_val=MAXBLK - 1)
                with act.If(last > b):
                    with act.Fori(b + 1, last + 1) as more:
                        drain_y(more)
                        silu(0, more)
                        round_h(0, more)
                        silu(1, more)
                        round_x(more + 1)
                        round_h(1, more)

            for n in range(3):
                round_third(n, 0)
            act.preload_act_table_set(SILU_SET)
            round_x(0)
            new_expert(0, 0, True)
            act.wait_ge(s("plan"), 3)
            more_blocks(0, 0)
            with act.Fori(1, NE) as e:
                b = act.value_load(last_blk[0:1, bass.ds(e - 1, 1)], min_val=0, max_val=MAXBLK - 2) + 1
                new_expert(b, e, False)
                more_blocks(e, b)
            nb = act.value_load(last_blk[0:1, NE - 1:NE], min_val=NE - 1, max_val=MAXBLK - 1) + 1
            drain_y(nb)
            def scale_y(t):
                M, n = rows_of(t), t % YB
                act.wait_ge(s(f"y_got{n}"), 32 * (t // YB) + 32)
                act.activation(yg[n][0][0:M, :], yg[n][0][0:M, :], ACT.Copy, scale=prow[0:M, t, 0:1]
                               ).then_inc(s("c_scaled"), 1)

            scale_y(0)
            for t in range(NTL):
                if t + 1 < NTL:
                    scale_y(t + 1)
                normalise(NTL + t, rows_of(t), yg[t % YB][0][0:rows_of(t), :])

        @block.vector
        def _(dve):
            steps = [0]

            def link(ins):
                steps[0] += 1
                ins.then_inc(s("dve_step"), 1)
                dve.wait_ge(s("dve_step"), steps[0])

            dve.memset(ropet[0][:, 0:1], 0.0).then_inc(s("rope_sin"), 1)
            for k in range(KD):
                dve.wait_ge(s("x_hi"), k + 1)
                dve.tensor_tensor(xl[:, k, :], xraw[:, k, :], as_f32(xh[:, k, :]), ALU.subtract
                                  ).then_inc(s("x_split"), 1)
                if k < 2:
                    dve.wait_ge(s("w_hi"), k + 1)
                    dve.tensor_tensor(wlo[k][:], wraw[k][:], as_f32(whi[k][:]), ALU.subtract
                                      ).then_inc(s("w_split"), 1)

            def split_pair(i):
                for n in range(2):
                    dve.wait_ge(s(f"w_in{n}"), 16 * i + 16)
                    dve.tensor_copy(whi[n][:], wraw[n][:]).then_inc(s("w_hi"), 1)
                    dve.wait_ge(s("w_hi"), 2 * i + (n + 1))
                    dve.tensor_tensor(wlo[n][:], wraw[n][:], as_f32(whi[n][:]), ALU.subtract
                                      ).then_inc(s("w_split"), 1)

            def rotate(c):
                for j in range(3):
                    a, b = TCUT[j], TCUT[j + 1]
                    t, u = ropet[j][:, 0:b - a], U[:, bass.ds(c, 1), a:b].rearrange("p o c -> p (o c)")
                    dve.wait_ge(s("rope_swap"), 3 * c + (j + 1))
                    dve.tensor_tensor(t, ps[:, 6 + j % 2, 0:b - a], sin[:, a:b], ALU.mult).then_inc(s("rope_sin"), 1)
                    dve.tensor_tensor(u, u, cos[:, a:b], ALU.mult).then_inc(s("rope_cos"), 1)
                    dve.wait_ge(s("rope_sin"), 3 * c + (j + 2))
                    dve.wait_ge(s("rope_cos"), 3 * c + (j + 1))
                    dve.tensor_tensor(u, u, t, ALU.add).then_inc(s("rope_done"), 1)

            with dve.Fori(1, NCH // 2 - NROPE) as i:
                split_pair(i)
            dve.wait_ge(s("const_in"), 16 * 12)
            with dve.Fori(0, NROPE) as c:
                split_pair(c + (NCH // 2 - NROPE))
                rotate(c)
            dve.wait_ge(s("u_mm"), NCH)
            dve.wait_ge(s("rope_done"), 3 * NROPE)
            for n in range(2):
                dve.memset(msk[n][:, :, META:META + P], NEG).then_inc(s("b_omain" if n else "m_read"), 1)
            for n in range(2):
                dve.memset(stat[n][:, 6, :], 0.0).then_inc(s("m_out" if n else "m_read"), 1)

            def a_softmax_in(m, u, peeled):
                st, sm = stat[m % 2], msk[m % 2]
                banks = ps[:, 2 * (m % 2):2 * (m % 2) + 2, :]
                both = amask.rearrange("p (o k) -> p o k", o=1)
                dve.wait_ge(s("a_scored"), u + 1)
                if peeled:
                    dve.tensor_copy(sm[:, :, 0:META], banks[:, :, 0:META])
                    last = dve.tensor_tensor(sm[:, :, META + P:BAND], banks[:, :, META + P:BAND],
                                             both[:, :, META + P:BAND].to_broadcast([P, 2, P]), ALU.add)
                else:
                    last = dve.tensor_tensor(sm[:], banks[:, :, 0:BAND], both.to_broadcast([P, 2, BAND]), ALU.add)
                last.then_inc(s("a_masked"), 1)
                dve.wait_ge(s("a_masked"), u + 1)
                dve.tensor_reduce(st[:, 0, :], sm[:], AX.X, ALU.max).then_inc(s("a_max"), 1)
                dve.wait_ge(s("a_max"), u + 1)
                sink = sinks[:, m:m + 5:4]
                dve.scalar_tensor_tensor(out=st[:, 5, :], in0=st[:, 0, :], scalar=SCALE, in1=sink, op0=ALU.mult,
                                         op1=ALU.max).then_inc(s("a_top"), 1)
                dve.wait_ge(s("a_top"), u + 1)
                dve.tensor_scalar(st[:, 1, :], st[:, 5, :], -1.0, None, ALU.mult).then_inc(s("a_nmax"), 1)
                dve.tensor_tensor(st[:, 2, :], sink, st[:, 5, :], ALU.subtract).then_inc(s("a_nmax"), 1)

            def a_norm(m, u):
                st = stat[m % 2]
                dve.wait_ge(s("a_exp"), 3 * u + 3)
                dve.tensor_tensor(st[:, 6, :], st[:, 3, :], st[:, 4, :], ALU.add).then_inc(s("a_den"), 1)
                dve.wait_ge(s("a_den"), u + 1)
                dve.reciprocal(st[:, 7, :], st[:, 6, :]).then_inc(s("a_rden"), 1)
                dve.wait_ge(s("a_rden"), u + 1)
                for g in range(2):
                    e = prob[m % 2][:, g, :]
                    dve.tensor_scalar(e, e, st[:, 7, g:g + 1], None, ALU.mult).then_inc(s("a_prob"), 1)

            def a_meta(u):
                dve.wait_ge(s("a_turned"), u + 1)
                dve.tensor_copy(ptms[:], ps[0:META, 5, 0:2 * P]).then_inc(s("a_ptm"), 1)

            def a_tile(i, peeled, last):
                for m in range(PAIRS):
                    u = PAIRS * i + m
                    a_meta(u)
                    if m + 1 < PAIRS or not last:
                        a_norm(m + 1, u + 1)
                    if m < 2 or not last:
                        a_softmax_in((m + 2) % PAIRS, u + 2, peeled and m < 2)

            a_softmax_in(0, 0, True)
            a_softmax_in(1, 1, True)
            a_norm(0, 0)
            a_tile(0, True, False)
            with dve.Fori(0, NT // 2 - 1) as i:
                for n in (1, 2):
                    a_tile(2 * i + n, False, False)
            a_tile(NT - 1, False, True)
            st = stat[0]
            for g in range(2):
                sm = msk[0][:, g, 0:AKEYS]
                dve.wait_ge(s("as_scored"), g + 1)
                link(dve.tensor_copy(sm, ps[:, g, 0:AKEYS]))
                link(dve.tensor_reduce(st[:, 0, g:g + 1], sm, AX.X, ALU.max))
                sink = sinks_s[:, g:g + 1]
                link(dve.scalar_tensor_tensor(out=st[:, 5, g:g + 1], in0=st[:, 0, g:g + 1], scalar=SCALE, in1=sink,
                                              op0=ALU.mult, op1=ALU.max))
                dve.tensor_scalar(st[:, 1, g:g + 1], st[:, 5, g:g + 1], -1.0, None, ALU.mult
                                  ).then_inc(s("as_nmax"), 1)
                dve.tensor_tensor(st[:, 2, g:g + 1], sink, st[:, 5, g:g + 1], ALU.subtract
                                  ).then_inc(s("as_dsink"), 1)
            for g in range(2):
                e = prob[0][:, g, 0:AKEYS]
                dve.wait_ge(s("as_exp"), 2 * g + 2)
                link(dve.tensor_tensor(st[:, 6, g:g + 1], st[:, 3, g:g + 1], st[:, 4, g:g + 1], ALU.add))
                link(dve.reciprocal(st[:, 7, g:g + 1], st[:, 6, g:g + 1]))
                dve.tensor_scalar(e, e, st[:, 7, g:g + 1], None, ALU.mult).then_inc(s("as_prob"), 1)

            dve.wait_ge(s("as_out"), 2)
            dve.wait_ge(s("stored"), 16 * 4)

            def stage_rest(p):
                dve.wait_ge(s("b_hikq"), 2 * p + 1)
                dve.tensor_tensor(kl[:], U[:, bass.ds(C_KB + p, 1), :], as_f32(kh[:]), ALU.subtract
                                  ).then_inc(s("b_lokq"), 1)
                dve.wait_ge(s("b_hikq"), 2 * p + 2)
                dve.scalar_tensor_tensor(out=ql[:], in0=U[:, bass.ds(C_QB + p, 1), 0:SEQ], scalar=SCALE,
                                         in1=as_f32(qh[:]), op0=ALU.mult, op1=ALU.subtract
                                         ).then_inc(s("b_lokq"), 1)

            stage_rest(0)
            with dve.Fori(0, PAIRS) as p:
                def cap_of(n):
                    a, c, t = STEPS[n]
                    M, q0, _ = step_shape(c, t)
                    if n >= 2:
                        dve.wait_ge(s("b_soft"), NSTEP * p + n - 1)
                    dve.wait_ge(s("b_z"), NSTEP * p + n + 1)
                    dve.tensor_scalar(capped[n % 2][0:M, q0:QCH], ps[0:M, n % 4, q0:QCH], ZCAP, None, ALU.min
                                      ).then_inc(s("b_cap"), 1)

                def soft_of(n):
                    a, c, t = STEPS[n]
                    M, q0, _ = step_shape(c, t)
                    dve.wait_ge(s("b_ln"), NSTEP * p + n + 1)
                    if n >= 3:
                        dve.wait_ge(s("b_later"), NLATER * p + LATER_BEFORE[n - 2])
                        dve.wait_ge(s("b_lo"), NSTEP * p + n - 2)
                    dve.tensor_tensor(soft[n % 3][0:M, q0:QCH], capped[n % 2][0:M, q0:QCH],
                                      ps[0:M, n % 4, q0:QCH], ALU.max).then_inc(s("b_soft"), 1)

                def rest_of(n):
                    a, c, t = STEPS[n]
                    M, q0, _ = step_shape(c, t)
                    dve.wait_ge(s("b_hi"), NSTEP * p + n + 1)
                    dve.tensor_tensor(soft_lo[n % 3][0:M, q0:QCH], soft[n % 3][0:M, q0:QCH],
                                      as_f32(soft_hi[n % 3][0:M, q0:QCH]), ALU.subtract).then_inc(s("b_lo"), 1)

                def drain_of(n):
                    a, c, _ = STEPS[n]
                    rows = slice(HD * a, HD * a + HD)
                    dve.wait_ge(s("b_pv"), NSTEP * p + n + 2)
                    dve.tensor_scalar(U[rows, bass.ds(C_QB + p, 1), QCH * c:QCH * c + QCH], ps[rows, 4 + c, :],
                                      1.0, None, ALU.mult).then_inc(s("b_omain"), 1)

                for n in range(-AHEAD, NSTEP):
                    if 0 <= n + 2 < NSTEP:
                        soft_of(n + 2)
                    if n + AHEAD < NSTEP:
                        cap_of(n + AHEAD)
                    if 0 <= n + 2 < NSTEP:
                        rest_of(n + 2)
                    if n >= 2 and STEPS[n - 2][2] < 0:
                        drain_of(n - 2)
                with dve.If(p < PAIRS - 1):
                    stage_rest(p + 1)
                drain_of(NSTEP - 1)
            dve.tensor_scalar(qs[:], U[:, C_QB:C_QB + PAIRS, SAM:MET], SCALE, None, ALU.mult
                              ).then_inc(s("s_q"), 1)
            dve.memset(later_s[:], 0.0).then_inc(s("s_zeroed"), 1)
            dve.wait_ge(s("s_zeroed"), 1)
            for n, (M, kt, vt) in enumerate(SAMPLE_TILES):
                dve.wait_ge(s("s_z"), n + 1)
                dve.tensor_scalar(halves(capped_s[0:M, :]), ps[0:M, s_bank(n):s_bank(n) + 2, 0:P], ZCAP, None,
                                  ALU.min).then_inc(s("s_cap"), 1)
                dve.wait_ge(s("s_ln"), n + 1)
                dve.tensor_tensor(halves(soft_s[0:M, :]), halves(capped_s[0:M, :]),
                                  ps[0:M, s_bank(n):s_bank(n) + 2, 0:P], ALU.max).then_inc(s("s_soft"), 1)
                if n < 3:
                    dve.wait_ge(s("s_arg"), n + 1)
                    dve.wait_ge(s("s_soft"), n + 1)
                    dve.tensor_tensor(later_s[0:M, :], later_s[0:M, :], soft_s[0:M, :], ALU.add
                                      ).then_inc(s("s_later"), 1)
                    dve.wait_ge(s("s_later"), n + 1)


            def rest_mix(i, n):
                dve.wait_ge(s("g_hi"), 3 * i + (n + 1))
                dve.tensor_tensor(glo[n][:], graw[n][:], as_f32(ghi[n][:]), ALU.subtract).then_inc(s("g_split"), 1)

            def mix_of(i, odd, last):
                for j in range(3):
                    bank = (odd + j) % 2
                    if j == 2 and not last:
                        rest_mix(i + 1, 0)
                    dve.wait_ge(s("m_out"), 3 * i + (j + 1))
                    dve.wait_ge(s("sig"), 6 * i + (2 * j + 2))
                    dve.tensor_tensor(mixa[:], sig[bank][0][:], ps[:, 4 * bank + 2, 0:TW], ALU.mult
                                      ).then_inc(s("m_a"), 1)
                    dve.tensor_tensor(mixb[:], sig[bank][1][:], ps[:, 4 * bank + 3, 0:TW], ALU.mult
                                      ).then_inc(s("m_read"), 1)
                    dve.wait_ge(s("m_a"), 3 * i + (j + 1))
                    dve.wait_ge(s("m_read"), 3 * i + (j + 3))
                    dve.tensor_tensor(mT[:, bass.ds(i, 1), TW * j:TW * j + TW], mixa[:], mixb[:], ALU.add
                                      ).then_inc(s("m_out"), 1)
                if not last:
                    rest_mix(i + 1, 1)
                    rest_mix(i + 1, 2)

            rest_mix(0, 0)
            rest_mix(0, 1)
            for n, (hi, lo, c) in enumerate(((oa_hi, oa_lo, C_QA), (ob_hi, ob_lo, C_QB))):
                dve.wait_ge(s("oa_hi"), n + 1)
                dve.tensor_tensor(lo[:, :, 0:LIVE], U[:, c:c + 4, 0:LIVE], as_f32(hi[:, :, 0:LIVE]), ALU.subtract
                                  ).then_inc(s("oa_split"), 1)
            rest_mix(0, 2)
            with dve.Fori(0, KD // 2 - 1) as i:
                mix_of(2 * i, 0, False)
                mix_of(2 * i + 1, 1, False)
            mix_of(KD - 2, 0, False)
            mix_of(KD - 1, 1, True)

            dve.wait_ge(s("m_out"), 3 * KD + 1)
            link(dve.memset(rt[:], -3e38))
            link(dve.memset(seen[:], 0.0))
            link(dve.memset(onehot[:], 0.0))

            def ms_rest(t):
                M, n = rows_of(t), t % 2
                dve.wait_ge(s("ms_hi"), t + 1)
                dve.tensor_tensor(ms_lo[n][:, :, 0:M], mT[:, :, P * t:P * t + M], as_f32(ms_hi[n][:, :, 0:M]),
                                  ALU.subtract).then_inc(s("ms_split"), 1)

            def stats(n, M, x):
                v = mv[n % 2][0:M]
                for c in range(2):
                    link(dve.bn_stats(bn[0:M, c, :], x[:, 512 * c:512 * c + 512]))
                if n >= 2:
                    dve.wait_ge(s("normed"), n - 1)
                link(dve.bn_aggr(v[:, 0:2], bn[0:M].rearrange("p c k -> p (c k)")))
                dve.tensor_scalar(v[:, 2:3], v[:, 1:2], EPS, None, ALU.add).then_inc(s("var_out"), 1)
                dve.tensor_scalar(v[:, 3:4], v[:, 0:1], -1.0, None, ALU.mult).then_inc(s("var_out"), 1)

            def norm1(t):
                M, n = rows_of(t), t % 2
                h = hkeep[0:M, t, :]
                dve.wait_ge(s("o_mm"), t + 1)
                dve.wait_ge(s(f"xn_in{n}"), 16 * (t // 2) + 16)
                dve.scalar_tensor_tensor(out=halves(h), in0=halves(xn[n][0:M, :]), scalar=ALPHA,
                                         in1=ps[0:M, 2 * n:2 * n + 2, :], op0=ALU.mult, op1=ALU.add
                                         ).then_inc(s("r_added"), 1)
                dve.wait_ge(s("r_added"), t + 1)
                stats(t, M, h)

            def route(t):
                M = rows_of(t)
                dve.wait_ge(s("r_mm"), t + 1)
                link(dve.tensor_tensor(col(M, 0, 0, NG), ps[0:M, 6, 0:NG], rbias[0:M, 0:NG], ALU.add))
                dve.tensor_tensor(el[0:M].rearrange("p g e -> p (g e)"), ps[0:M, 6, NG:NR], rbias[0:M, NG:NR],
                                  ALU.add).then_inc(s("r_read"), 1)
                link(dve.max(col(M, 1, 0, 8), col(M, 0, 0, 8)))
                link(dve.max_index(gi[0:M, :], col(M, 1, 0, 8), col(M, 0, 0, 8)))
                dve.tensor_scalar(col(M, 3, 0, 1), col(M, 1, 0, 1), -1.0, None, ALU.mult).then_inc(s("r_nmax"), 1)
                link(dve.tensor_copy(col(M, 2, 0, 1), gi[0:M, 0:1]))
                link(dve.tensor_scalar(col(M, 8, 0, NG), iota[0:M, 0:NG], col(M, 2, 0, 1), None, ALU.is_equal))
                dve.wait_ge(s("r_read"), t + 1)
                link(dve.tensor_tensor(elm[0:M], el[0:M],
                                       col(M, 8, 0, NG).rearrange("p (g o) -> p g o", o=1).to_broadcast([M, NG, EPG]),
                                       ALU.mult))
                link(dve.tensor_reduce(col(M, 9, 0, EPG), elm[0:M].rearrange("p g e -> p e g"), AX.X, ALU.add))
                link(dve.max(col(M, 10, 0, 8), col(M, 9, 0, 8)))
                link(dve.max_index(ei[0:M, :], col(M, 10, 0, 8), col(M, 9, 0, 8)))
                dve.tensor_tensor(col(M, 6, 0, 1), col(M, 10, 1, 2), col(M, 10, 0, 1), ALU.subtract
                                  ).then_inc(s("r_gap"), 1)
                link(dve.tensor_copy(col(M, 11, 0, 2), ei[0:M, 0:2]))
                link(dve.tensor_scalar(col(M, 12, 0, 1), col(M, 2, 0, 1), float(EPG), None, ALU.mult))
                link(dve.tensor_scalar(exk[0:M, t, :], col(M, 11, 0, 2), col(M, 12, 0, 1), None, ALU.add))
                for k in range(2):
                    link(dve.tensor_scalar(onehot[0:M, t, k, :], iota[0:M, 0:NE], exk[0:M, t, k:k + 1], None,
                                           ALU.is_equal))
                if t:
                    place(t - 1)
                dve.tensor_tensor(chosen[0:M, :], onehot[0:M, t, 0, :], onehot[0:M, t, 1, :], ALU.add
                                  ).then_inc(s("r_chosen"), 1)
                dve.wait_ge(s("r_exp"), 2 * t + 2)
                link(dve.tensor_scalar(col(M, 13, 0, 1), col(M, 7, 0, 1), 1.0, None, ALU.add))
                link(dve.tensor_tensor(col(M, 13, 1, 2), col(M, 13, 0, 1), col(M, 5, 0, 1), ALU.mult))
                link(dve.reciprocal(prow[0:M, t, 0:1], col(M, 13, 1, 2)))
                link(dve.tensor_tensor(prow[0:M, t, 1:2], prow[0:M, t, 0:1], col(M, 7, 0, 1), ALU.mult))

            def place(t):
                M = rows_of(t)
                dve.wait_ge(s("r_chosen"), t + 1)
                dve.wait_ge(s("r_pos"), t + 1)
                link(dve.tensor_tensor(posx[0:M], onehot[0:M, t],
                                       ps[0:M, 7, 0:NE].rearrange("p (o e) -> p o e", o=1).to_broadcast([M, 2, NE]),
                                       ALU.mult))
                link(dve.tensor_reduce(loc[0:M, t, :], posx[0:M], AX.X, ALU.add))
                dve.scalar_tensor_tensor(out=vdest[0:M, t, :], in0=exk[0:M, t, :], scalar=float(VROWS),
                                         in1=loc[0:M, t, :], op0=ALU.mult, op1=ALU.add).then_inc(s("r_dest"), 1)
                dve.tensor_tensor(seen[0:M, :], seen[0:M, :], chosen[0:M, :], ALU.add).then_inc(s("r_seen"), 1)
                dve.wait_ge(s("r_seen"), t + 1)

            ms_rest(0)
            for k in range(KD):
                dve.wait_ge(s("o_hi"), k + 1)
                dve.tensor_tensor(olo[:, k, :], oraw[:, k, :], as_f32(ohi[:, k, :]), ALU.subtract
                                  ).then_inc(s("o_split"), 1)
            for t in range(NTL):
                if t + 1 < NTL:
                    ms_rest(t + 1)
                if t == 0:
                    dve.wait_ge(s("ln_in"), 16 * 6)
                norm1(t)
                if t:
                    route(t - 1)
            route(NTL - 1)
            place(NTL - 1)

            dve.wait_ge(s("r_count"), 1)
            link(dve.tensor_scalar(cnt_i[:], ps[:, 0, 0:NE], float(P - 1), None, ALU.add))
            link(dve.tensor_scalar(cnt_i[:], cnt_i[:], 7, None, ALU.arith_shift_right))
            link(dve.tensor_copy(nblk[:], cnt_i[:]))
            link(dve.tensor_scalar(nblk[:], nblk[:], 1.0, None, ALU.max))
            link(dve.tensor_copy(cum[0][:], nblk[:]))
            a, d = 0, 1
            while d < NE:
                link(dve.tensor_tensor(cum[1 - a][:, d:], cum[a][:, d:], cum[a][:, :NE - d], ALU.add))
                link(dve.tensor_copy(cum[1 - a][:, :d], cum[a][:, :d]))
                a, d = 1 - a, 2 * d
            total = cum[a]
            dve.tensor_scalar(last_blk[:], total[0:1, :], -1.0, None, ALU.add).then_inc(s("plan"), 1)
            NB1 = MAXBLK + 1
            cells = cmp[0:1, 0:NB1 * NE].rearrange("p (b e) -> p b e", e=NE)
            link(dve.tensor_tensor(cells, total[0:1, :].rearrange("p (o e) -> p o e", o=1).to_broadcast([1, NB1, NE]),
                                   iota[0:1, :].rearrange("p (b o) -> p b o", o=1).to_broadcast([1, NB1, NE]),
                                   ALU.is_le))
            link(dve.tensor_reduce(blk[:, 0, :], cells, AX.X, ALU.add))
            link(dve.tensor_tensor(cells, cells,
                                   nblk[0:1, :].rearrange("p (o e) -> p o e", o=1).to_broadcast([1, NB1, NE]),
                                   ALU.mult))
            link(dve.tensor_reduce(blk[:, 1, :], cells, AX.X, ALU.add))
            link(dve.tensor_scalar(blk[:, 0, :], blk[:, 0, :], float(NE - 1), None, ALU.min))
            link(dve.tensor_tensor(blk[:, 2, :], iota[0:1, :], blk[:, 1, :], ALU.subtract))
            link(dve.scalar_tensor_tensor(out=blk[:, 3, :], in0=blk[:, 0, :], scalar=float(NTL),
                                          in1=blk[:, 2, :], op0=ALU.mult, op1=ALU.add))
            dve.tensor_copy(blk_i[:, 0, :], blk[:, 0, :]).then_inc(s("plan"), 1)
            dve.tensor_scalar(blk_i[:, 1, :], blk[:, 3, :], float(NE * NTL - 1), None, ALU.min
                              ).then_inc(s("plan"), 1)
            dve.wait_ge(s("tab_in"), 16)
            dve.tensor_copy(tab_f[:], tab_i[:]).then_inc(s("tokens"), 1)
            dve.wait_ge(s("tab_tr"), 1)
            dve.tensor_copy(tokens[:], ps[:, 1, 0:NE * NTL]).then_inc(s("tokens"), 1)

            def rest_third(n, e, pieces=range(3)):
                for q in pieces:
                    dve.wait_ge(s("e_hi"), 12 * e + (4 * n + q + 1))
                    c = slice(PIECE * q, PIECE * q + PIECE)
                    dve.tensor_tensor(e_lo[n][:, c], e_raw[n][:, c], as_f32(e_hi[n][:, c]), ALU.subtract
                                      ).then_inc(s("e_split"), 1)

            def hidden(half, b, first):
                dve.wait_ge(s("silu"), 2 * b + (half + 1))
                if not first:
                    dve.wait_ge(s("hb_tr"), 2 * (b - 1) + (half + 1))
                c = slice(HH * half, HH * half + HH)
                dve.tensor_tensor(hid[:, c], sg[:, c], ps[:, half, HH:2 * HH], ALU.mult
                                  ).then_inc(s("hid"), 1)

            def rest_x(b):
                for c in range(2):
                    dve.wait_ge(s("xb_hi"), 2 * b + (c + 1))
                    dve.tensor_tensor(xb_lo[:, 4 * c:4 * c + 4, :], ps[:, 2 + c, :].rearrange("p (k m) -> p k m", k=4),
                                      as_f32(xb_hi[:, 4 * c:4 * c + 4, :]), ALU.subtract
                                      ).then_inc(s("xb_split"), 1)

            def rest_h(half, b):
                dve.wait_ge(s("hb_hi"), 2 * b + (half + 1))
                dve.tensor_tensor(hb_lo[:, 2 * half:2 * half + 2, :],
                                  ps[:, 4, HH * half:HH * half + HH].rearrange("p (k m) -> p k m", k=2),
                                  as_f32(hb_hi[:, 2 * half:2 * half + 2, :]), ALU.subtract
                                  ).then_inc(s("hb_split"), 1)

            def new_expert(b, e):
                rest_third(0, e)
                rest_third(1, e)
                hidden(0, b, False)
                rest_third(2, e, range(1))
                rest_h(0, b)
                rest_third(2, e, range(1, 3))
                hidden(1, b, False)
                rest_x(b + 1)
                rest_h(1, b)

            def more_blocks(e, b):
                last = dve.value_load(last_blk[0:1, bass.ds(e, 1)], min_val=0, max_val=MAXBLK - 1)
                with dve.If(last > b):
                    with dve.Fori(b + 1, last + 1) as more:
                        hidden(0, more, False)
                        rest_h(0, more)
                        hidden(1, more, False)
                        rest_x(more + 1)
                        rest_h(1, more)

            rest_third(0, 0)
            rest_third(1, 0)
            rest_x(0)
            rest_third(2, 0)
            hidden(0, 0, True)
            rest_h(0, 0)
            hidden(1, 0, True)
            rest_x(1)
            rest_h(1, 0)
            link(dve.tensor_tensor(first_row[:], total[:], nblk[:], ALU.subtract))
            link(dve.tensor_scalar(first_row[:], first_row[:], float(P), None, ALU.mult))
            own = cmp[:, 0:NTL * 2 * NE].rearrange("p (a e) -> p a e", e=NE)
            link(dve.tensor_tensor(own, onehot[:].rearrange("p t k e -> p (t k) e"),
                                   first_row[:].rearrange("p (o e) -> p o e", o=1).to_broadcast([P, 2 * NTL, NE]),
                                   ALU.mult))
            link(dve.tensor_reduce(yfirst[:], own, AX.X, ALU.add))
            for t in range(NTL):
                M = rows_of(t)
                link(dve.tensor_tensor(ydest[0:M, t, :], yfirst[0:M, 2 * t:2 * t + 2], loc[0:M, t, :], ALU.add))
            dve.tensor_copy(ydest_done[:], total[:, 0:1]).then_inc(s("ydest"), 1)
            more_blocks(0, 0)
            with dve.Fori(1, NE) as e:
                b = dve.value_load(last_blk[0:1, bass.ds(e - 1, 1)], min_val=0, max_val=MAXBLK - 2) + 1
                new_expert(b, e)
                more_blocks(e, b)
            def shift2(t):
                M, n = rows_of(t), t % 2
                dve.wait_ge(s("gained"), NTL + t + 1)
                if t >= 2:
                    dve.wait_ge(s(f"y_out{n}"), 16 * (t // 2))
                dve.tensor_tensor(on[n][0:M, :], yg[t % YB][0][0:M, :], b2[0:M, :], ALU.add).then_inc(s("out_done"), 1)

            for t in range(NTL):
                M, n = rows_of(t), t % YB
                f = yg[n][0][0:M, :]
                dve.wait_ge(s("c_scaled"), t + 1)
                link(dve.scalar_tensor_tensor(out=f, in0=yg[n][1][0:M, :], scalar=prow[0:M, t, 1:2], in1=f,
                                              op0=ALU.mult, op1=ALU.add))
                link(dve.scalar_tensor_tensor(out=f, in0=hkeep[0:M, t, :], scalar=ALPHA, in1=f, op0=ALU.mult,
                                              op1=ALU.add))
                stats(NTL + t, M, f)
                if t:
                    shift2(t - 1)
            shift2(NTL - 1)

        @block.gpsimd
        def _(pool):
            pool.wait_ge(s("rope_done"), 3 * NROPE)
            pool.wait_ge(s("va_out"), 4)
            pool.tensor_copy(qas_s[:], U[:, C_QA:C_QA + 4, SAM:MET]).then_inc(s("as_staged"), 1)
            pool.tensor_copy(vas[0][:, 1, :], van[:, 0, :])
            pool.tensor_copy(kas[0][:, P:2 * P], U[:, C_KA, 0:P])
            pool.tensor_copy(qas[0][:], U[:, C_QA:C_QA + 4, 0:P]).then_inc(s("a_staged"), 1)

            def stage(i, odd):
                pool.tensor_copy(vas[odd][:], van[:, bass.ds(i - 1, 2), :])
                pool.tensor_copy(kas[odd][:], U[:, C_KA, bass.ds(P * (i - 1), 2 * P)])
                pool.tensor_copy(qas[odd][:], U[:, C_QA:C_QA + 4, bass.ds(P * i, P)]).then_inc(s("a_staged"), 1)

            stage(1, 1)
            with pool.Fori(1, NT // 2) as i:
                for odd in range(2):
                    pool.wait_ge(s("a_mixed"), PAIRS * (2 * i + odd - 1))
                    stage(2 * i + odd, odd)
            pool.wait_ge(s("as_out"), 2)
            for dst, src in ((ident_r, ident), (mask_r, blkmask), (ntri_r, ntri)):
                last = pool.tensor_copy(dst[:], src)
            last.then_inc(s("b_vstaged"), 1)
            with pool.Fori(0, PAIRS) as p:
                pool.wait_ge(s("b_vtr2"), p + 1)
                pool.tensor_copy(vts[:], U[:, bass.ds(C_VB + p, 1), :]).then_inc(s("b_vstaged"), 1)
                for n in range(NSTEP):
                    a, c, t = STEPS[n]
                    M, q0, first = step_shape(c, t)
                    if t < 0:
                        continue
                    if n:
                        pool.wait_ge(s("b_arg"), NSTEP * p + n)
                    pool.wait_ge(s("b_soft"), NSTEP * p + n + 1)
                    x = soft[n % 3]
                    cols = slice(q0, QCH)
                    old, new = (later[(LATER_BEFORE[n] + k) % 2] for k in range(2))
                    if first:
                        pool.tensor_tensor(new[:, cols], x[:, cols], zero.to_broadcast([P, QCH - q0]), ALU.add
                                           ).then_inc(s("b_later"), 1)
                        pool.memset(new[:, 0:q0], 0.0)
                        pool.memset(old[:, 0:q0], 0.0).then_inc(s("b_zeroed"), 1)
                    else:
                        pool.wait_ge(s("b_later"), NLATER * p + LATER_BEFORE[n])
                        pool.wait_ge(s("b_zeroed"), 4 * p + (2 * a + c + 1))
                        pool.tensor_tensor(new[:, cols], old[:, cols], x[:, cols], ALU.add
                                           ).then_inc(s("b_later"), 1)

            pool.wait_ge(s("w_used2"), KD)
            pool.memset(zeros_i[:], 0).then_inc(s("zeros"), 1)
            pool.tensor_copy(tokid[:], const[:, K_TOK:K_TOK + NTL]).then_inc(s("pool_step"), 1)
            pool.wait_ge(s("pool_step"), 1)
            pool.wait_ge(s("stored"), 16 * 5)

            def rstd(n, M):
                v = mv[n % 2][0:M]
                pool.wait_ge(s("var_out"), 2 * n + 2)
                pool.tensor_tensor(v[:, 4:5], v[:, 2:3], const[0:M, K_HALF:K_HALF + 1], ALU.pow
                                   ).then_inc(s("rstd"), 1)
                pool.wait_ge(s("rstd"), 2 * n + 1)
                pool.tensor_tensor(v[:, 5:6], v[:, 3:4], v[:, 4:5], ALU.mult).then_inc(s("rstd"), 1)

            def gain(n, x, g):
                pool.wait_ge(s("normed"), n + 1)
                pool.tensor_tensor(x, x, g, ALU.mult).then_inc(s("gained"), 1)

            def enter(t):
                M = rows_of(t)
                pool.wait_ge(s("r_dest"), t + 1)
                for k in range(2):
                    pool.indirect_dma_start(
                        out=tok_table, out_offset=bass.IndirectOffsetOnAxis(ap=vdest[0:M, t, k:k + 1], axis=0),
                        in_=tokid[0:M, t:t + 1], in_offset=None).then_inc(s("table_in"), 16)

            for t in range(NTL):
                M = rows_of(t)
                h = hkeep[0:M, t, :]
                rstd(t, M)
                gain(t, h, g1[0:M, :])
                pool.wait_ge(s("gained"), t + 1)
                pool.tensor_tensor(h, h, b1[0:M, :], ALU.add).then_inc(s("h_done"), 1)
                if t >= 2:
                    enter(t - 2)
            enter(NTL - 2)
            enter(NTL - 1)
            pool.wait_ge(s("table_in"), 16 * 2 * NTL)
            pool.dma_start(tab_i[:], tok_table.rearrange("(g r p) o -> r g (p o)", g=3, p=P)).then_inc(s("tab_in"), 16)
            pool.wait_ge(s("rows_out"), 16 * NTL)

            def step(count):
                pool.wait_ge(s("pool_step"), count)
                pool.tensor_tensor(tick[:], zero[0:1, :], zero[0:1, :], ALU.add).then_inc(s("pool_step"), 1)

            def fetch(b, first):
                if not first:
                    column = pool.value_load(blk_i[0:1, 1, bass.ds(b, 1)], min_val=0, max_val=NE * NTL - 1)
                    pool.wait_ge(s("x_got"), 16 * b)
                    pool.wait_ge(s("xb_tr"), b)
                    step(2 * b)
                pool.tensor_copy(idx[:], tokens[:, 0:1] if first else tokens[:, bass.ds(column, 1)]
                                 ).then_inc(s("idx_set"), 1)
                pool.wait_ge(s("idx_set"), b + 1)
                step(2 * b + 1)
                pool.indirect_dma_start(out=xg[:], out_offset=None, in_=h_rows,
                                        in_offset=bass.IndirectOffsetOnAxis(ap=idx[:, 0:1], axis=0)
                                        ).then_inc(s("x_got"), 16)

            def rest_last(n, e):
                pool.wait_ge(s("e_hi"), 12 * e + (4 * n + 4))
                c = slice(3 * PIECE, 4 * PIECE)
                pool.tensor_tensor(e_lo[n][:, c], e_raw[n][:, c], as_f32(e_hi[n][:, c]), ALU.subtract
                                   ).then_inc(s("e_last_split"), 1)

            def more_blocks(e, b):
                last = pool.value_load(last_blk[0:1, bass.ds(e, 1)], min_val=0, max_val=MAXBLK - 1)
                with pool.If(last > b):
                    with pool.Fori(b + 1, last + 1) as more:
                        fetch(more + 1, False)

            pool.wait_ge(s("tokens"), 2)
            fetch(0, True)
            for n in range(3):
                rest_last(n, 0)
            pool.wait_ge(s("plan"), 3)
            fetch(1, False)
            more_blocks(0, 0)
            with pool.Fori(1, NE) as e:
                b = pool.value_load(last_blk[0:1, bass.ds(e - 1, 1)], min_val=0, max_val=MAXBLK - 2) + 1
                fetch(b + 1, False)
                rest_last(0, e)
                rest_last(1, e)
                rest_last(2, e)
                more_blocks(e, b)
            nb = pool.value_load(last_blk[0:1, NE - 1:NE], min_val=NE - 1, max_val=MAXBLK - 1) + 1
            pool.wait_ge(s("rows_out"), 16 * NTL + 16 * nb)
            step(2 * nb + 2)

            def collect(t):
                M, n = rows_of(t), t % YB
                if t >= YB:
                    pool.wait_ge(s("out_done"), t - YB + 1)
                for k in range(2):
                    pool.indirect_dma_start(
                        out=yg[n][k][0:M, :], out_offset=None, in_=y_rows,
                        in_offset=bass.IndirectOffsetOnAxis(ap=ydest[0:M, t, k:k + 1], axis=0)
                    ).then_inc(s(f"y_got{n}"), 16)

            pool.wait_ge(s("ydest"), 1)
            for t in range(YB - 1):
                collect(t)
            for t in range(NTL):
                M = rows_of(t)
                rstd(NTL + t, M)
                gain(NTL + t, yg[t % YB][0][0:M, :], g2[0:M, :])
                if t + YB - 1 < NTL:
                    collect(t + YB - 1)


def constants(np):
    i = np.arange(P)
    rot = np.zeros((P, P), np.float32)
    for h in range(0, P, HD):
        for d in range(HD // 2):
            rot[h + d + HD // 2, h + d] = -1.0
            rot[h + d, h + d + HD // 2] = 1.0
    band = np.zeros((P, BAND), np.float32)
    band[P // 2:, META:META + P // 2] = NEG
    band[:P // 2, META + P + P // 2:] = NEG
    smask = np.zeros((P, NH, DEC), np.float32)
    smask[:DEC] = np.where(i[:DEC, None] >= i[None, :DEC], np.float32(NEG), np.float32(0))[:, None, :]
    cols = [np.eye(P), -1.0 * (i[:, None] >= i), -np.ones((P, P)), i[:, None] < i, np.ones((P, P)),
            np.where(i[:, None] >= i, NEG, 0.0), rot, band, smask.reshape(P, -1),
            np.broadcast_to(np.arange(MAXBLK + 1), (P, MAXBLK + 1)), P * np.arange(NTL)[None] + i[:, None],
            np.full((P, 1), -0.5)]
    const = np.concatenate([np.asarray(c, np.float32) for c in cols], axis=1)
    pos = np.concatenate([np.arange(SEQ) + META, np.arange(DEC) + META + PAST, np.arange(META)]).astype(np.float32)
    inv = np.float32(10000.0) ** (-np.arange(HD // 2, dtype=np.float32) * np.float32(2.0) / np.float32(HD))
    ang = (pos[None, :] * inv.astype(np.float32)[:, None]).astype(np.float32)
    ang = np.tile(ang, (P // (HD // 2), 1))
    return const, np.cos(ang), np.sin(ang)


def lay_out(np, x):
    a = {k: np.asarray(v) for k, v in x.items()}
    const, cos, sin = constants(np)
    d = {"const": const, "cos": cos, "sin": sin}
    tok = np.concatenate([a["x_prompt"][0], a["x_sample"][0], a["meta_tokens"]])
    d["xT"] = tok.T.reshape(KD, P, TOK).transpose(1, 0, 2)
    w = a["w_in"][0]
    q = w[:, :NH * HD].reshape(D, 2, 4, HD).transpose(0, 2, 1, 3).reshape(D, NH * HD)
    gates = NH * HD + 2 * P + 3 * NH * HD
    u = np.concatenate([q, w[:, NH * HD:gates]], axis=1)
    d["w_u"] = u.reshape(KD, P, NCH, P).transpose(2, 1, 0, 3)
    d["sinks"] = a["attn_sinks"][0]
    d["ck_a"] = a["cache_a_k"][0, 0].reshape(AWIN, P).T
    d["cv_a"] = a["cache_a_v"][0, 0].reshape(AWIN, P)
    d["ck_b"] = a["cache_b_k"][0, 0].reshape(PAST, PAIRS, P).transpose(2, 1, 0)
    d["cv_b"] = a["cache_b_v"][0, 0].reshape(2, P, PAIRS * P).transpose(1, 0, 2)
    def tiles(m):
        return m.reshape(-1, P, KD, P).transpose(2, 1, 0, 3)

    ga, gb = w[:, gates:gates + D], w[:, gates + D:]
    woa = a["w_oa"][0].reshape(2, 4, HD, D).transpose(1, 0, 2, 3).reshape(NH * HD, D)
    d["w_mix"] = np.stack([tiles(ga), tiles(gb), np.concatenate([tiles(woa), tiles(a["w_ob"][0])], axis=2)], axis=1)
    d["w_out"] = a["w_out"][0].reshape(KD, P, D)
    d["x_nat"] = np.concatenate([a["x_prompt"][0], a["x_sample"][0]])
    for k in ("ln1_g", "ln1_b", "ln2_g", "ln2_b"):
        d[k] = a[k][0]
    d["w_r"] = np.concatenate([a["w_router_group"][0], a["w_router_expert"][0]], axis=1
                              ).reshape(KD, P, NR).transpose(1, 0, 2)
    d["b_r"] = np.concatenate([a["b_router_group"][0], a["b_router_expert"][0]])
    gu = np.stack([a["w_gate"][0], a["w_up"][0]]).reshape(2, NE, KD, P, 2, HH)
    moe = np.empty((NE, 3, P, GC), np.float32)
    moe[:, 0:2] = gu.transpose(1, 4, 3, 2, 0, 5).reshape(NE, 2, P, GC)
    moe[:, 2] = a["w_down"][0].reshape(NE, 4, P, D).transpose(0, 2, 1, 3).reshape(NE, P, GC)
    d["w_moe"] = moe
    return {k: np.ascontiguousarray(v) for k, v in d.items()}


_OUTS = {"kat": (P, AWIN + DEC), "vat": (P, AWIN + DEC), "kvb": (P, 2 * PAIRS, LIVE), "y": (LIVE, D)}


def kernel(**inputs):
    import numpy as np
    import concourse.bacc as bacc
    from concourse.bass_utils import run_bass_kernel_spmd as run

    nc = bacc.Bacc("TRN2", target_bir_lowering=False, num_devices=1)
    arrays = lay_out(np, inputs)
    io = {k: nc.dram_tensor(k, v.shape, mybir.dt.from_np(v.dtype), kind="ExternalInput").ap()
          for k, v in arrays.items()}
    for k, shape in _OUTS.items():
        io[k] = nc.dram_tensor(k, shape, F32, kind="ExternalOutput").ap()
    build(nc, io)
    r = run(nc, [arrays], core_ids=[0]).results[0]
    kv_a = [r[k].T.reshape(1, 1, AWIN + DEC, 2, HD) for k in ("kat", "vat")]
    kv_b = r["kvb"].transpose(2, 1, 0).reshape(1, 1, LIVE, 2, NH, HD)
    kv_b = [kv_b[:, :, :, n] for n in range(2)]
    out = [r["y"][None, :SEQ], r["y"][None, SEQ:]]
    out += [x[:, :, :AWIN] for x in kv_a] + [x[:, :, :SEQ] for x in kv_b]
    out += [x[:, :, AWIN:] for x in kv_a] + [x[:, :, SEQ:] for x in kv_b]
    return tuple(np.ascontiguousarray(x) for x in out)
```
